# Optimizing a Trainium2 kernel written in Bass

```python
import jax, jax.numpy as jnp
from jax import lax
import numpy as np

D_MODEL = 2048
BATCH = 1
SEQ = 128
DEPTH = 2
DEC_BATCH = 1
DEC_SEQ = 128
PAST_LEN = 128

GRID_W = 64
N_MIXERS = 2
NA_HEADS = 16
NA_HEAD_DIM = D_MODEL // NA_HEADS
NA_WIN_ROWS = 8
NA_WIN_COLS = 16
GLA_HEADS = 4
GLA_KEY_DIM = D_MODEL // 2
GLA_VAL_DIM = D_MODEL
GLA_DK = GLA_KEY_DIM // GLA_HEADS
GLA_DV = GLA_VAL_DIM // GLA_HEADS
GLA_GATE_RANK = 16
GLA_GATE_NORM = 16.0
GLA_CHUNK = 64
D_FF = 4 * D_MODEL
ROPE_THETA = 10000.0
EPS = 1e-6
ATTN_Q_BLOCK = 128
N_NA_LAYERS = (DEPTH + 1) // 2
N_GLA_LAYERS = DEPTH // 2
NEG_INF = -1e30

kernel_name = 'hybrid_natten_gla_diffusion_step'

def rmsnorm(x, g):
    xf = x.astype(jnp.float32)
    y = xf * lax.rsqrt(jnp.mean(xf * xf, axis=-1, keepdims=True) + EPS)
    return (y * g.astype(jnp.float32)).astype(x.dtype)

def adaln(cond, w, b):
    m = jax.nn.silu(cond) @ w + b
    m = m.reshape(cond.shape[0], 6, 1, D_MODEL)
    return [m[:, j] for j in range(6)]

def modulate(x, g, shift, scale):
    return rmsnorm(x, g) * (1 + scale) + shift

def split_heads(x, h):
    b, l, _ = x.shape
    return x.reshape(b, l, h, -1).transpose(0, 2, 1, 3)

def merge_heads(x):
    b, h, l, d = x.shape
    return x.transpose(0, 2, 1, 3).reshape(b, l, h * d)

def na_qkv(h, w_qkv):
    b, l, _ = h.shape
    p = (h @ w_qkv).reshape(b, l, 3, NA_HEADS, NA_HEAD_DIM).transpose(2, 0, 3, 1, 4)
    return p[0], p[1], p[2]

def context_attention(q, k, v):
    b, h, l, dh = q.shape
    nb = l // ATTN_Q_BLOCK
    qb = q.reshape(b, h, nb, ATTN_Q_BLOCK, dh).transpose(2, 0, 1, 3, 4)

    def one(qblk):
        s = jnp.einsum('bhqd,bhkd->bhqk', qblk, k).astype(jnp.float32) * (dh ** -0.5)
        p = jax.nn.softmax(s, axis=-1).astype(v.dtype)
        return jnp.einsum('bhqk,bhkd->bhqd', p, v)

    o = lax.map(one, qb)
    return o.transpose(1, 2, 0, 3, 4).reshape(b, h, l, dh)

def neighborhood_attention(q, k, v, k_ctx, v_ctx, rpb):
    b, h, t, dh = q.shape
    rows = t // GRID_W
    kr = min(NA_WIN_ROWS, rows)
    kw = NA_WIN_COLS
    scale = dh ** -0.5
    qg = q.reshape(b, h, rows, GRID_W, dh)
    kg = k.reshape(b, h, rows, GRID_W, dh)
    vg = v.reshape(b, h, rows, GRID_W, dh)
    r = jnp.arange(rows)
    c = jnp.arange(GRID_W)
    row_start = jnp.clip(r - kr // 2, 0, rows - kr)
    row_idx = row_start[:, None] + jnp.arange(kr)[None, :]
    col_start = jnp.clip(c - kw // 2, 0, GRID_W - kw)
    col_in = (c[None, :] >= col_start[:, None]) & (c[None, :] < col_start[:, None] + kw)
    k_band = kg[:, :, row_idx]
    v_band = vg[:, :, row_idx]
    s_lat = jnp.einsum('bhrqd,bhrkwd->bhrqkw', qg, k_band).astype(jnp.float32) * scale
    dr = row_idx - r[:, None] + NA_WIN_ROWS - 1
    dc = jnp.clip(c[None, :] - c[:, None] + kw - 1, 0, 2 * kw - 2)
    bias = rpb[:, dr[:, None, :, None], dc[None, :, None, :]]
    s_lat = jnp.where(col_in[None, None, None, :, None, :],
                      s_lat + bias.astype(jnp.float32)[None], NEG_INF)
    s_ctx = jnp.einsum('bhrqd,bhld->bhrql', qg, k_ctx).astype(jnp.float32) * scale
    n_lat = kr * GRID_W
    s = jnp.concatenate([s_lat.reshape(b, h, rows, GRID_W, n_lat), s_ctx], axis=-1)
    p = jax.nn.softmax(s, axis=-1).astype(v.dtype)
    p_lat = p[..., :n_lat].reshape(b, h, rows, GRID_W, kr, GRID_W)
    p_ctx = p[..., n_lat:]
    o = (jnp.einsum('bhrqkw,bhrkwd->bhrqd', p_lat, v_band)
         + jnp.einsum('bhrql,bhld->bhrqd', p_ctx, v_ctx))
    return o.reshape(b, h, t, dh)

def rope_axial(x):
    t_len, d = x.shape[2], x.shape[3]
    t = jnp.arange(t_len)
    half = d // 2
    n = half // 2
    freqs = ROPE_THETA ** (-jnp.arange(n, dtype=jnp.float32) / n)

    def rot(xa, pos):
        ang = pos.astype(jnp.float32)[:, None] * freqs[None, :]
        cos, sin = jnp.cos(ang), jnp.sin(ang)
        x1, x2 = xa[..., :n], xa[..., n:]
        return jnp.concatenate([x1 * cos - x2 * sin, x1 * sin + x2 * cos], axis=-1)

    return jnp.concatenate([rot(x[..., :half], t // GRID_W), rot(x[..., half:], t % GRID_W)], axis=-1)

def gla_chunked(q, k, v, log_a, s0):
    b, h, l, dk = q.shape
    dv = v.shape[-1]
    n = l // GLA_CHUNK
    rs = lambda z: z.reshape(b, h, n, GLA_CHUNK, z.shape[-1])
    q, k, v, log_a = rs(q), rs(k), rs(v), rs(log_a)
    cum = jnp.cumsum(log_a, axis=3)
    cum_last = cum[:, :, :, -1:]
    q_dec = q * jnp.exp(cum)
    k_dec = k * jnp.exp(-cum)
    mask = jnp.tril(jnp.ones((GLA_CHUNK, GLA_CHUNK), dtype=bool))
    attn = jnp.where(mask, jnp.einsum('bhncd,bhnsd->bhncs', q_dec, k_dec), 0.0)
    o_intra = jnp.einsum('bhncs,bhnsv->bhncv', attn, v)
    kv = jnp.einsum('bhncd,bhncv->bhndv', k * jnp.exp(cum_last - cum), v)
    decay = jnp.exp(cum_last[:, :, :, 0])

    def step(s, inp):
        dec, kvn = inp
        return dec[..., None] * s + kvn, s

    s_final, s_prev = lax.scan(step, s0, (jnp.moveaxis(decay, 2, 0), jnp.moveaxis(kv, 2, 0)))
    s_prev = jnp.moveaxis(s_prev, 0, 2)
    o = o_intra + jnp.einsum('bhncd,bhndv->bhncv', q_dec, s_prev)
    return o.reshape(b, h, l, dv), s_final

def gla_mix(h, w_qkvg, w_a1, w_a2, b_a, g_head, w_o, s_init, latent):
    f32 = jnp.float32
    proj = h @ w_qkvg
    q, k, v, g = jnp.split(proj, [GLA_KEY_DIM, 2 * GLA_KEY_DIM, 2 * GLA_KEY_DIM + GLA_VAL_DIM], axis=-1)
    q = split_heads(q, GLA_HEADS).astype(f32)
    k = split_heads(k, GLA_HEADS).astype(f32)
    v = split_heads(v, GLA_HEADS).astype(f32)
    if latent:
        q = rope_axial(q)
        k = rope_axial(k)
    q = q * (GLA_DK ** -0.5)
    flip = lambda z: jnp.flip(z, axis=2)
    outs, finals = [], []
    for d in range(2):
        z = (h @ w_a1[d]) @ w_a2[d] + b_a[d]
        log_a = split_heads(jax.nn.log_sigmoid(z.astype(f32)) / GLA_GATE_NORM, GLA_HEADS)
        s0 = s_init[:, d].astype(f32)
        if d == 0:
            o, sf = gla_chunked(q, k, v, log_a, s0)
        else:
            o, sf = gla_chunked(flip(q), flip(k), flip(v), flip(log_a), s0)
            o = flip(o)
        outs.append(o)
        finals.append(sf)
    o = outs[0] + outs[1]
    o = o * lax.rsqrt(jnp.mean(o * o, axis=-1, keepdims=True) + EPS) * g_head.astype(f32)
    o = o * jax.nn.silu(split_heads(g, GLA_HEADS).astype(f32))
    out = merge_heads(o).astype(h.dtype) @ w_o
    return out, jnp.stack(finals, axis=1).astype(h.dtype)

def sq_relu_mlp(h, w1, w2):
    return jnp.square(jax.nn.relu(h @ w1)) @ w2

def setup_inputs(seed: int = 0) -> dict:
    key = jax.random.key(seed)
    ks = jax.random.split(key, 24)
    nrm = lambda k, shape, s: jax.random.normal(k, shape, jnp.float32) * s
    d = D_MODEL
    return {
        'x_prompt': nrm(ks[0], (BATCH, SEQ, d), 1.0),
        'x_sample': nrm(ks[1], (DEC_BATCH, DEC_SEQ, d), 1.0),
        'cache_na_k': nrm(ks[2], (DEC_BATCH, N_NA_LAYERS, NA_HEADS, PAST_LEN, NA_HEAD_DIM), 1.0),
        'cache_na_v': nrm(ks[3], (DEC_BATCH, N_NA_LAYERS, NA_HEADS, PAST_LEN, NA_HEAD_DIM), 1.0),
        'state_gla': nrm(ks[4], (DEC_BATCH, N_GLA_LAYERS, 2, GLA_HEADS, GLA_DK, GLA_DV), 1.0),
        'c': nrm(ks[5], (DEC_BATCH, d), 1.0),
        'c_ctx': nrm(ks[6], (d,), 1.0),
        'w_ada': nrm(ks[7], (DEPTH, d, 6 * d), 0.5 * d ** -0.5),
        'b_ada': nrm(ks[8], (DEPTH, 6 * d), 0.01),
        'norm_g': 1.0 + nrm(ks[9], (DEPTH, 4, d), 0.01),
        'w_qkv_na': nrm(ks[10], (N_NA_LAYERS, d, 3 * d), d ** -0.5),
        'w_o_na': nrm(ks[11], (N_NA_LAYERS, d, d), d ** -0.5),
        'rpb_na': nrm(ks[12], (N_NA_LAYERS, NA_HEADS, 2 * NA_WIN_ROWS - 1, 2 * NA_WIN_COLS - 1), 0.1),
        'w_qkvg_gla': nrm(ks[13], (N_GLA_LAYERS, d, 2 * GLA_KEY_DIM + 2 * GLA_VAL_DIM), d ** -0.5),
        'w_a1_gla': nrm(ks[14], (N_GLA_LAYERS, 2, d, GLA_GATE_RANK), d ** -0.5),
        'w_a2_gla': nrm(ks[15], (N_GLA_LAYERS, 2, GLA_GATE_RANK, GLA_KEY_DIM), GLA_GATE_RANK ** -0.5),
        'b_a_gla': nrm(ks[16], (N_GLA_LAYERS, 2, GLA_KEY_DIM), 0.1),
        'g_head_gla': 1.0 + nrm(ks[17], (N_GLA_LAYERS, GLA_DV), 0.01),
        'w_o_gla': nrm(ks[18], (N_GLA_LAYERS, GLA_VAL_DIM, d), GLA_VAL_DIM ** -0.5),
        'w1_mlp': nrm(ks[19], (DEPTH, d, D_FF), d ** -0.5),
        'w2_mlp': nrm(ks[20], (DEPTH, D_FF, d), D_FF ** -0.5),
    }

def reference(x_prompt, x_sample, cache_na_k, cache_na_v, state_gla, c, c_ctx,
              w_ada, b_ada, norm_g, w_qkv_na, w_o_na, rpb_na,
              w_qkvg_gla, w_a1_gla, w_a2_gla, b_a_gla, g_head_gla, w_o_gla,
              w1_mlp, w2_mlp):
    xp, xs = x_prompt, x_sample
    new_k, new_v, new_s = [], [], []
    for l in range(DEPTH):
        i = l // N_MIXERS
        sh1p, sc1p, g1p, sh2p, sc2p, g2p = adaln(c_ctx[None], w_ada[l], b_ada[l])
        sh1s, sc1s, g1s, sh2s, sc2s, g2s = adaln(c, w_ada[l], b_ada[l])
        hp = modulate(xp, norm_g[l, 0], sh1p, sc1p)
        hs = modulate(xs, norm_g[l, 0], sh1s, sc1s)
        if l % N_MIXERS == 0:
            qp, kp, vp = na_qkv(hp, w_qkv_na[i])
            yp = merge_heads(context_attention(qp, kp, vp)) @ w_o_na[i]
            new_k.append(kp)
            new_v.append(vp)
            qs, ks_, vs = na_qkv(hs, w_qkv_na[i])
            os_ = neighborhood_attention(qs, ks_, vs, cache_na_k[:, i], cache_na_v[:, i], rpb_na[i])
            ys = merge_heads(os_) @ w_o_na[i]
        else:
            zero_state = jnp.zeros((xp.shape[0], 2, GLA_HEADS, GLA_DK, GLA_DV), jnp.float32)
            yp, sp = gla_mix(hp, w_qkvg_gla[i], w_a1_gla[i], w_a2_gla[i], b_a_gla[i],
                             g_head_gla[i], w_o_gla[i], zero_state, False)
            new_s.append(sp)
            ys, _ = gla_mix(hs, w_qkvg_gla[i], w_a1_gla[i], w_a2_gla[i], b_a_gla[i],
                            g_head_gla[i], w_o_gla[i], state_gla[:, i], True)
        xp = xp + g1p * rmsnorm(yp, norm_g[l, 1])
        xs = xs + g1s * rmsnorm(ys, norm_g[l, 1])
        mp = sq_relu_mlp(modulate(xp, norm_g[l, 2], sh2p, sc2p), w1_mlp[l], w2_mlp[l])
        ms = sq_relu_mlp(modulate(xs, norm_g[l, 2], sh2s, sc2s), w1_mlp[l], w2_mlp[l])
        xp = xp + g2p * rmsnorm(mp, norm_g[l, 3])
        xs = xs + g2s * rmsnorm(ms, norm_g[l, 3])
    new_na_k = jnp.stack(new_k, axis=1)
    new_na_v = jnp.stack(new_v, axis=1)
    new_gla = jnp.stack(new_s, axis=1)
    return (xp, xs, new_na_k, new_na_v, new_gla)


_drawn_inputs = setup_inputs


def setup_inputs(seed=0):
    import zlib

    import numpy as np

    out = dict(_drawn_inputs(seed))
    spreads = {}
    factors = {'state_gla': 15.741,
     'norm_g': 3.66,
     'rpb_na': 4.019,
     'g_head_gla': 64.0,
     'cache_na_k': 8.0,
     'cache_na_v': 8.0}
    for name, (base, spread) in spreads.items():
        noise = np.random.default_rng([zlib.crc32(name.encode()), seed]).standard_normal(out[name].shape)
        drawn = base * np.exp(spread * noise) if base else spread * noise
        out[name] = __import__('jax').numpy.asarray(drawn.astype(out[name].dtype))
    for name, factor in factors.items():
        out[name] = (out[name] * factor).astype(out[name].dtype)
    return out
```

```python
import concourse.bass as bass
from concourse import mybir
from contextlib import ExitStack
import numpy as np

P = 128
D = 2048
KC = D // P
TOK = 128
T2 = 2 * TOK
FF = 4 * D
HID_GROUPS = FF // D
ADA = 6 * D
UNIT_ROWS = 1024
UKC = UNIT_ROWS // P
UC = 256
UNIT = UKC * UC
NA_H = 16
DH = 128
GRID_W = 64
WIN_COLS = 16
LINE = 2 * GRID_W - 1
N_DR = 3
GLA_H = 4
DK = 256
DV = 512
KEY = GLA_H * DK
CHUNK = 64
RANK = 16
EPS = 1e-6
NA_SCALE = DH ** -0.5
GLA_SCALE = DK ** -0.5
GATE_NORM = 16.0
NEG = -1e30
ADA_BLOCKS = ADA // P


def shape_tables():
    ident = np.eye(P, dtype=np.float32)
    sel = np.zeros((P, 2), np.float32)
    for j in range(4):
        sel[32 * j, 0] = 1.0
        sel[32 * j + 1, 1] = 1.0
    c = np.arange(P) % GRID_W
    start = np.clip(c - WIN_COLS // 2, 0, GRID_W - WIN_COLS)
    inside = (c[None, :] >= start[:, None]) & (c[None, :] < start[:, None] + WIN_COLS)
    window = np.where(inside, 0.0, NEG).astype(np.float32)
    s, t = np.arange(P)[:, None], np.arange(P)[None, :]
    same = (s // CHUNK) == (t // CHUNK)
    upto = [same & (s <= t), same & (s >= t)]
    after = [same & (s > t), same & (s < t)]
    gates = [m.astype(np.float32) / np.float32(GATE_NORM) for m in upto + after]
    n = DK // 4
    freqs = np.float32(10000.0) ** (-np.arange(n, dtype=np.float32) / np.float32(n))
    pos = np.arange(TOK)
    ang = np.concatenate([(pos // GRID_W).astype(np.float32)[:, None] * freqs[None],
                          (pos % GRID_W).astype(np.float32)[:, None] * freqs[None]], axis=1)
    base = np.concatenate([ident, sel], axis=1)
    gla = np.concatenate(gates + [np.cos(ang).astype(np.float32), np.sin(ang).astype(np.float32)], axis=1)
    return base, window, gla


def build_program(nc, x_prompt, x_sample, cache_na_k, cache_na_v, state_gla, c, c_ctx, w_ada, b_ada, norm_g,
                  w_qkv_na, w_o_na, rpb_na, w_qkvg_gla, w_a1_gla, w_a2_gla, b_a_gla, g_head_gla, w_o_gla,
                  w1_mlp, w2_mlp, t_base, t_window, t_gla,
                  y_prompt, y_sample, new_na_k, new_na_v, new_gla):
    f32 = mybir.dt.float32
    f32r = mybir.dt.float32r
    u32 = mybir.dt.uint32
    ALU = mybir.AluOpType
    ACT = mybir.ActivationFunctionType
    AX = mybir.AxisListType
    ds = bass.ds

    ctx = ExitStack()
    with ctx:
        def sb(name, shape, dt=f32):
            return ctx.enter_context(nc.sbuf_tensor(name, shape, dt))

        sems = {}

        def sem(name):
            if name not in sems:
                sems[name] = ctx.enter_context(nc.semaphore(name))
            return sems[name]

        with nc.sbuf_tensor("HID", [P, KC, 2 * T2], f32r) as HID:
            pass
        SCR = sb("SCR", [P, 3 * KC * T2])
        with nc.sbuf_tensor("HM", [P, KC, 2 * T2], f32r) as HM:
            pass
        TMP = sb("TMP", [P, 2 * KC * T2])
        X = sb("X", [P, KC, T2])
        RAW = sb("RAW", [P, 2, UNIT])
        WHI = sb("WHI", [P, 4, UNIT], f32r)
        WLO = sb("WLO", [P, 4, UNIT], f32r)
        ADW = sb("ADW", [P, 2, UNIT])
        CB = sb("CB", [P, 2048])
        BASE = sb("BASE", [P, P + 2])
        ONES = sb("ONES", [P, P])
        MODT = sb("MODT", [P, 2 * ADA_BLOCKS, 2])
        BT = sb("BT", [P, 2 * ADA_BLOCKS])
        NGT = sb("NGT", [P, P])
        CS = sb("CS", [P, KC, 32])
        MROW = sb("MROW", [P, UC])
        GAIN = sb("GAIN", [P, KC, 2])
        EPSC = sb("EPSC", [P, 1])
        ONEC = sb("ONEC", [P, 1])

        IDENT = BASE[:, 0:P]
        SEL = BASE[:, P:P + 2]
        S4 = KC * T2
        SQ = SCR[:, 0:S4].rearrange("p (c t) -> p c t", c=KC)
        PART = SCR[:, S4:S4 + 4 * T2].rearrange("p (g t) -> p g t", g=4)
        STD = SCR[:, S4 + 4 * T2:S4 + 5 * T2]
        RSTD = SCR[:, S4 + 5 * T2:S4 + 6 * T2]
        Y = SCR[:, 2 * S4:3 * S4].rearrange("p (c t) -> p c t", c=KC)
        XLD = SCR[:, 0:S4].rearrange("p (s n) -> p s n", s=2)
        OUTS = XLD
        SMALL = SCR[:, S4:S4 + 4 * P].rearrange("p (a n) -> p a n", a=4)
        CE = SCR[:, S4 + 4 * P:S4 + 4 * P + 32]
        CC = SCR[:, S4 + 5 * P:S4 + 5 * P + 32]
        WINM = SCR[:, 2 * S4:2 * S4 + P]
        RPT = SCR[:, 2 * S4 + P:2 * S4 + 2 * P]
        BIAS = CB[:, :].rearrange("p (h k) -> p h k", h=NA_H)
        RELU = CB[:, 0:2 * T2].rearrange("p (b t) -> p b t", b=2)
        QK = SCR[:, 0:2 * S4].rearrange("p (h t) -> p h t", h=2 * NA_H)
        VN = SCR[:, 2 * S4:3 * S4].rearrange("p (s n) -> p s n", s=2)

        psum = [ctx.enter_context(nc.psum_tensor(f"PS{i}", [P, 512], f32)) for i in range(8)]
        rpb_pad = nc.dram_tensor("rpb_pad", [N_DR, NA_H, GRID_W, LINE], f32, kind="Internal").ap()

        M_QKV0 = 0
        M_WO0 = M_QKV0 + 3 * D // UC
        M_MLP0 = M_WO0 + D // UC
        MLP_SLABS = 2 * HID_GROUPS * D // UC
        M_QKV1 = M_MLP0 + MLP_SLABS
        M_WO1 = M_QKV1 + 3 * D // UC
        M_MLP1 = M_WO1 + D // UC
        M_END = M_MLP1 + MLP_SLABS
        NB = D // UC // 2
        A_QKV0 = 2 * D // UC
        A_WO0 = A_QKV0 + 2 * 3 * NB
        A_MLP0 = A_WO0 + 2 * NB
        A_QKV1 = A_MLP0 + 2 * HID_GROUPS * NB
        A_WO1 = A_QKV1 + 3 * NB
        A_END = A_WO1 + NB
        assert A_END == 2 * ADA // UC

        raw_in = [sem("raw_in0"), sem("raw_in1")]
        hi_done = sem("hi_done")
        lo_done = sem("lo_done")
        unit0_used = sem("unit0_used")
        block_done = sem("block_done")
        bank_free = sem("bank_free")
        ada_in = [sem("ada_in0"), sem("ada_in1")]
        ada0_used = sem("ada0_used")
        ada_done = sem("ada_done")
        row_ready = sem("row_ready")
        sel_done = sem("sel_done")
        mod_done = sem("mod_done")
        relu_done = sem("relu_done")
        square_done = sem("square_done")
        hid_hi = sem("hid_hi")
        hid_done = sem("hid_done")
        h_ready = sem("h_ready")
        squares = sem("squares")
        parts = sem("parts")
        sumsq = sem("sumsq")
        std_ready = sem("std_ready")
        x_ready = sem("x_ready")
        xn_ready = sem("xn_ready")
        mod_x = sem("mod_x")
        hm_hi = sem("hm_hi")
        y_zero = sem("y_zero")

        MAIN = psum[0:4]
        ROWB = psum[4]
        SELB = psum[5]
        NORMB = psum[6]

        SLOT = 2056

        def slot(p, at, n):
            return TMP[:, SLOT * p + at:SLOT * p + at + n]

        QS = [slot(p, 0, T2) for p in range(2)]
        KS = [slot(p, 256, T2) for p in range(2)]
        VS = [slot(p, 512, T2).rearrange("p (s d) -> p s d", s=2) for p in range(2)]
        KCACHE = [slot(p, 768, DH) for p in range(2)]
        VCACHE = [slot(p, 896, DH) for p in range(2)]
        KCT = [slot(p, 1024, P) for p in range(2)]
        NEWK = TMP[:, 2 * SLOT:2 * SLOT + D]
        PROB = [slot(p, 1280, 3 * P) for p in range(2)]
        PROBT = [slot(p, 1664, 3 * P) for p in range(2)]
        MAXES = [slot(p, 2048, 2) for p in range(2)]
        NEGMAX = [slot(p, 2050, 2) for p in range(2)]
        ROWSUM = [slot(p, 2052, 2) for p in range(2)]
        RECIP = [slot(p, 2054, 2) for p in range(2)]
        SCORE_B, TURN_B, OUT_B, PROBT_B = psum[0:2], psum[2:4], psum[4:6], psum[6:8]
        cache_in = [sem("cache_in0"), sem("cache_in1")]
        head_done = sem("head_done")
        o_copied = sem("o_copied")
        PAIRS = NA_H // 2

        def attention_tensor(pe):
            mm, turn = nc.tensor.matmul, nc.tensor.transpose
            pe.sem_inc(head_done, 2)
            pe.wait_ge(bank_free, 4 + 2 * M_WO0)
            with pe.Fori(0, PAIRS) as i:
                for p in range(2):
                    pe.wait_ge(sem("qk_staged"), i * 2 + (p + 1))
                    pe.wait_ge(cache_in[p], i * 32 + 32)
                    turn(TURN_B[p][:, 0:P], KCACHE[p], IDENT)
                    turn(TURN_B[p][:, P:2 * P], KS[p][:, 0:TOK], IDENT).then_inc(sem("k_turned"), 1)
                    for s in range(2):
                        t = slice(TOK * s, TOK * s + TOK)
                        mm(SCORE_B[p][:, t], QS[p][:, t], KS[p][:, t], start=True, stop=True)
                    pe.wait_ge(sem("kct_ready"), i * 2 + (p + 1))
                    mm(SCORE_B[p][:, 2 * P:3 * P], QS[p][:, TOK:T2], KCT[p], start=True,
                       stop=True).then_inc(sem("scores_done"), 1)
                for p in range(2):
                    pe.wait_ge(sem("probs_ready"), i * 2 + (p + 1))
                    for b in range(3):
                        end = turn(PROBT_B[p][:, P * b:P * b + P], PROB[p][:, P * b:P * b + P], IDENT)
                    end.then_inc(sem("probs_turned"), 1)
                for p in range(2):
                    pe.wait_ge(sem("probt_ready"), i * 2 + (p + 1))
                    pe.wait_ge(sem("v_staged"), i * 2 + (p + 1))
                    pe.wait_ge(o_copied, i * 2 + (p + 1))
                    mm(OUT_B[p][:, 0:TOK], VS[p][:, 0, :], PROBT[p][:, 0:P], start=True, stop=True)
                    mm(OUT_B[p][:, TOK:T2], VS[p][:, 1, :], PROBT[p][:, P:2 * P], start=True, stop=False)
                    mm(OUT_B[p][:, TOK:T2], VCACHE[p], PROBT[p][:, 2 * P:3 * P], start=False,
                       stop=True).then_inc(head_done, 1)

        def attention_scalar(act):
            actv = nc.scalar.activation
            with act.Fori(0, PAIRS) as i:
                for p in range(2):
                    act.wait_ge(sem("k_turned"), i * 2 + (p + 1))
                    actv(KCT[p], TURN_B[p][:, 0:P], ACT.Copy).then_inc(sem("kct_ready"), 1)
                    actv(NEWK[:, ds(i * (2 * DH) + p * DH, DH)], TURN_B[p][:, P:2 * P], ACT.Copy).then_inc(
                        sem("newk_staged"), 1)
                for p in range(2):
                    act.wait_ge(sem("negmax_ready"), i * 2 + (p + 1))
                    actv(PROB[p][:, 0:P], SCORE_B[p][:, 0:P], ACT.Exp, bias=NEGMAX[p][:, 0:1],
                         accum_out=ROWSUM[p][:, 0:1])
                    actv(PROB[p][:, P:3 * P], SCORE_B[p][:, P:3 * P], ACT.Exp, bias=NEGMAX[p][:, 1:2],
                         accum_out=ROWSUM[p][:, 1:2]).then_inc(sem("exp_done"), 1)
                for p in range(2):
                    act.wait_ge(sem("probs_turned"), i * 2 + (p + 1))
                    actv(PROBT[p], PROBT_B[p][:, 0:3 * P], ACT.Copy).then_inc(sem("probt_ready"), 1)
            act.wait_ge(o_copied, 2 + NA_H)
            act.wait_ge(sem("newk_out"), 16)
            for g in range(4):
                actv(HM[:, 4 * g:4 * g + 4, 0:T2], QK[:, 4 * g:4 * g + 4, :], ACT.Copy).then_inc(sem("o_hi"), 1)

        def attention_vector(dve, link):
            ts, tt = nc.vector.tensor_scalar, nc.vector.tensor_tensor
            dve.sem_inc(o_copied, 2)
            dve.wait_ge(bank_free, 4 + 2 * M_WO0)

            def head(ap, h):
                return ap[:, ds(h, 1), :].rearrange("p o t -> p (o t)")

            with dve.Fori(0, PAIRS) as i:
                for p in range(2):
                    dve.wait_ge(head_done, i * 2 + (p + 1))
                    ts(QS[p], head(QK, i * 2 + p), NA_SCALE, None, ALU.mult)
                    ts(KS[p], head(QK, i * 2 + (NA_H + p)), 1.0, None, ALU.mult).then_inc(sem("qk_staged"), 1)
                for p in range(2):
                    dve.wait_ge(sem("scores_done"), i * 2 + (p + 1))
                    lat = SCORE_B[p][:, P:2 * P]
                    tt(lat, lat, head(BIAS, i * 2 + p), ALU.add).then_inc(sem("biased"), 1)
                    nc.vector.reduce_max(MAXES[p][:, 0:1], SCORE_B[p][:, 0:P], AX.X)
                    dve.wait_ge(sem("biased"), i * 2 + (p + 1))
                    nc.vector.reduce_max(MAXES[p][:, 1:2], SCORE_B[p][:, P:3 * P], AX.X).then_inc(sem("maxed"), 1)
                    dve.wait_ge(sem("maxed"), i * 2 + (p + 1))
                    ts(NEGMAX[p], MAXES[p], -1.0, None, ALU.mult).then_inc(sem("negmax_ready"), 1)
                for p in range(2):
                    dve.wait_ge(sem("exp_done"), i * 2 + (p + 1))
                    nc.vector.reciprocal(RECIP[p], ROWSUM[p]).then_inc(sem("recip_done"), 1)
                    dve.wait_ge(sem("recip_done"), i * 2 + (p + 1))
                    ts(PROB[p][:, 0:P], PROB[p][:, 0:P], RECIP[p][:, 0:1], None, ALU.mult)
                    ts(PROB[p][:, P:3 * P], PROB[p][:, P:3 * P], RECIP[p][:, 1:2], None,
                       ALU.mult).then_inc(sem("probs_ready"), 1)
                for p in range(2):
                    dve.wait_ge(head_done, i * 2 + (p + 3))
                    ts(head(QK, i * 2 + p), OUT_B[p][:, 0:T2], 1.0, None, ALU.mult).then_inc(o_copied, 1)
            for g in range(4):
                q = slice(4 * g, 4 * g + 4)
                dve.wait_ge(sem("o_hi"), g + 1)
                tt(HM[:, q, T2:2 * T2], QK[:, q, :], HM[:, q, 0:T2].bitcast(f32), ALU.subtract).then_inc(h_ready, 1)

        def attention_pool(pool):
            pool.wait_ge(bank_free, 4 + 2 * M_WO0)
            pool.dma_start(new_na_v[0, 0].rearrange("h t d -> t h d"),
                           VN[:, 0, :].rearrange("p (h d) -> p h d", h=NA_H)).then_inc(sem("newv_out"), 16)
            with pool.Fori(0, PAIRS) as i:
                for p in range(2):
                    pool.wait_ge(head_done, i * 2 + (p + 1))
                    pool.wait_ge(sem("bias_ready"), 1)
                    for dst, src in ((KCACHE[p], cache_na_k), (VCACHE[p], cache_na_v)):
                        pool.dma_start(dst, src[0, 0, ds(i * 2 + p, 1)].rearrange("o t d -> (o t) d")) \
                            .then_inc(cache_in[p], 16)
                    nc.gpsimd.tensor_copy(VS[p], VN[:, :, ds(i * (2 * DH) + p * DH, DH)]).then_inc(
                        sem("v_staged"), 1)
            pool.wait_ge(sem("newk_staged"), NA_H)
            pool.dma_start(new_na_k[0, 0].rearrange("h t d -> t h d"),
                           NEWK.rearrange("p (h d) -> p h d", h=NA_H)).then_inc(sem("newk_out"), 16)
            pool.wait_ge(head_done, 2 + NA_H)
            pool.wait_ge(sem("newv_out"), 16)
            nc.gpsimd.memset(SCR[:, 2 * S4:3 * S4], 0.0).then_inc(y_zero, 1)

        QG = SCR[:, 0:S4 // 2].rearrange("p (s n) -> p s n", s=2)
        KG = SCR[:, S4 // 2:S4].rearrange("p (s n) -> p s n", s=2)
        VG = SCR[:, S4:2 * S4].rearrange("p (s n) -> p s n", s=2)
        GG = SCR[:, 2 * S4:3 * S4].rearrange("p (s n) -> p s n", s=2)
        A1 = SCR[:, 2 * S4:2 * S4 + KC * 64].rearrange("p (c n) -> p c n", c=KC)
        CUM_TAB = [CB[:, 0:P], CB[:, P:2 * P]]
        AFTER_TAB = [CB[:, 2 * P:3 * P], CB[:, 3 * P:4 * P]]
        COS = CB[:, 4 * P:5 * P].rearrange("p (h n) -> p h n", h=2)
        SIN = CB[:, 5 * P:6 * P].rearrange("p (h n) -> p h n", h=2)
        W2A = CB[0:64, 768:768 + KEY]
        LOWR = CB[0:64, 1792:2048]
        ST0 = TMP[:, 0:2048].rearrange("p (d j v) -> p d j v", d=2, j=2)
        ST1 = TMP[:, 2048:4096].rearrange("p (d j v) -> p d j v", d=2, j=2)
        QKST = TMP[:, 4096:4608].rearrange("p (x n) -> p x n", x=2)
        QKTT = TMP[:, 4608:5120].rearrange("p (x n) -> p x n", x=2)
        LOGA = TMP[:, 5120:5632].rearrange("p (d n) -> p d n", d=2)
        QDEC = TMP[:, 5632:6144].rearrange("p (d n) -> p d n", d=2)
        KDEC = TMP[:, 6144:6656].rearrange("p (d n) -> p d n", d=2)
        KEND = TMP[:, 6656:7168].rearrange("p (d n) -> p d n", d=2)
        ROT = TMP[:, 5632:6656].rearrange("p (r h n) -> p r h n", r=8, h=2)
        ATT = TMP[:, 7168:7424].rearrange("p (d n) -> p d n", d=2)
        ATTSUM = TMP[:, 7424:7552]
        W2H = TMP[0:64, 7576:7576 + DK]
        WAITED = TMP[:, 7832:7833]
        VHEAD = TMP[:, 5120:5632]
        DECAY = TMP[:, 7552:7560].rearrange("p (d n j) -> p d n j", d=2, n=2)
        OSQ = TMP[:, 7560:7568]
        ORS = TMP[:, 7568:7576]
        SILU_E = TMP[:, 0:4096].rearrange("p (s n) -> p s n", s=2)
        GHEAD = TMP[:, 4096:4096 + DV]
        ATT_B, QK_B, CUM_B, AFTER_B = psum[0], psum[1], psum[2], psum[3]
        Z_B = [ATT_B[:, 0:DK], AFTER_B[:, 0:DK]]
        KV_B = psum[4:8]
        gla_saved = sem("gla_saved")

        def gla_low_rank_tensor(pe):
            pe.wait_ge(sem("a1_in"), 32)
            for g in range(4):
                pe.wait_ge(mod_x, 4 * 2 + g + 1)
                for k in range(4 * g, 4 * g + 4):
                    end = nc.tensor.matmul(psum[7][0:64, 0:T2], A1[:, k, :], SQ[:, k, :], start=(k == 0),
                                           stop=(k == KC - 1))
            end.then_inc(sem("low_rank_done"), 1)

        def gla_low_rank_vector(dve):
            dve.wait_ge(sem("low_rank_done"), 1)
            dve.wait_ge(sem("low_rank_ones"), 1)
            for d in range(2):
                rows = slice(32 * d, 32 * d + RANK)
                end = nc.vector.tensor_copy(LOWR[rows, :], psum[7][rows, 0:T2])
            end.then_inc(sem("low_rank_ready"), 1)

        def gla_tensor(pe):
            mm, turn = nc.tensor.matmul, nc.tensor.transpose
            pe.wait_ge(bank_free, 4 + 2 * M_WO1)
            pe.wait_ge(sem("low_rank_ready"), 1)
            pe.wait_ge(sem("gla_in"), 5 * 16)
            with pe.Fori(0, GLA_H) as i:
                for t in range(2):
                    n = i * 2 + (t + 1)
                    tok = slice(TOK * t, TOK * t + TOK)
                    pe.wait_ge(gla_saved, n)
                    if t == 0:
                        pe.wait_ge(sem("gla_w2_staged"), i + 1)
                    for d in range(2):
                        rows = slice(32 * d, 32 * d + RANK + 1)
                        end = mm(Z_B[d], LOWR[rows, tok], W2H[rows, :],
                                 start=True, stop=True)
                    end.then_inc(sem("gla_z"), 1)
                    pe.wait_ge(sem("gla_staged"), n)
                    for x in range(2):
                        for j in range(2):
                            b = 2 * x + j
                            end = turn(QK_B[:, P * b:P * b + P], QKST[:, x, P * j:P * j + P], IDENT)
                    end.then_inc(sem("gla_qk_turned"), 1)
                    pe.wait_ge(sem("gla_loga"), n)
                    for d in range(2):
                        for j in range(2):
                            b = 2 * d + j
                            mm(CUM_B[:, P * b:P * b + P], LOGA[:, d, P * j:P * j + P], CUM_TAB[d], start=True,
                               stop=True)
                        end = mm(AFTER_B[:, DK * d:DK * d + DK], AFTER_TAB[d], LOGA[:, d, :], start=True, stop=True)
                    end.then_inc(sem("gla_cum"), 1)
                    pe.wait_ge(sem("gla_gated"), n)
                    for d in range(2):
                        for j in range(2):
                            end = mm(ATT_B[:, P * d:P * d + P], KDEC[:, d, P * j:P * j + P],
                                     QDEC[:, d, P * j:P * j + P], start=(j == 0), stop=(j == 1))
                    end.then_inc(sem("gla_att"), 1)

                    def states(second, name):
                        for j in range(2):
                            for d in range(2):
                                c = d if not second else 1 - d
                                rows = slice(CHUNK * c, CHUNK * c + CHUNK)
                                e = mm(KV_B[2 * d + j][:, :], KEND[rows, d, P * j:P * j + P],
                                       VHEAD[rows, :], start=True, stop=True)
                        e.then_inc(sem(name), 1)

                    states(False, "gla_kv")
                    pe.wait_ge(sem("gla_state"), n)
                    if t == 0:
                        states(True, "gla_kv2")
                    pe.wait_ge(sem("gla_att_ready"), n)
                    O = QK_B
                    mm(O[:, :], ATTSUM, VHEAD, start=True, stop=False)
                    terms = []
                    for j in range(2):
                        if t == 1:
                            terms += [(d, d, j, ST0) for d in range(2)]
                        terms += [(1 - d, d, j, ST1) for d in range(2)]
                    for x, (c, d, j, st) in enumerate(terms):
                        rows = slice(CHUNK * c, CHUNK * c + CHUNK)
                        end = mm(O[rows, :], QDEC[:, d, P * j + CHUNK * c:P * j + CHUNK * c + CHUNK], st[:, d, j, :],
                                 start=False, stop=(x >= len(terms) - 2))
                    end.then_inc(sem("gla_o"), 1)
            pe.wait_ge(sem("gla_out_ready"), 1)
            for g in range(4):
                if g >= 2:
                    pe.wait_ge(h_ready, 4 * 4 + g - 1)
                for k in range(4 * g, 4 * g + 4):
                    bank = MAIN[2 * (g % 2) + (k % 4) // 2]
                    for s in range(2):
                        at = T2 * (k % 2) + TOK * s
                        end = turn(bank[:, at:at + TOK], VG[:, s, P * k:P * k + P], IDENT)
                end.then_inc(sem("gla_out_turned"), 1)
            pe.wait_ge(h_ready, 4 * 5)

        def gla_scalar(act):
            actv = nc.scalar.activation
            with act.Fori(0, GLA_H) as i:
                for t in range(2):
                    n = i * 2 + (t + 1)
                    e = TMP[:, 6656:7168]
                    act.wait_ge(sem("gla_z"), n)
                    actv(e[:, 0:DK], Z_B[0], ACT.Abs)
                    actv(e[:, DK:2 * DK], Z_B[1], ACT.Abs).then_inc(sem("gla_abs"), 1)
                    act.wait_ge(sem("gla_abs"), n)
                    actv(e, e, ACT.Exp, scale=-1.0).then_inc(sem("gla_absexp"), 1)
                    act.wait_ge(sem("gla_absexp"), n)
                    actv(e, e, ACT.Ln, bias=ONEC[:, :]).then_inc(sem("gla_ln"), 1)
                    act.wait_ge(sem("gla_qk_turned"), n)
                    actv(QKTT[:, 0, :], QK_B[:, 0:DK], ACT.Copy, scale=GLA_SCALE)
                    actv(QKTT[:, 1, :], QK_B[:, DK:2 * DK], ACT.Copy).then_inc(sem("gla_qkt"), 1)
                    act.wait_ge(sem("gla_cum"), n)
                    actv(TMP[:, 5632:6144], CUM_B[:, :], ACT.Exp)
                    actv(TMP[:, 6144:6656], CUM_B[:, :], ACT.Exp, scale=-1.0)
                    actv(e, AFTER_B[:, :], ACT.Exp).then_inc(sem("gla_exps"), 1)
                    act.wait_ge(sem("gla_o"), n)
                    actv(TMP[:, 5120:5632], QK_B[:, :], ACT.Square,
                         accum_out=OSQ[:, ds(i * 2 + t, 1)]).then_inc(sem("gla_osq"), 1)
            act.wait_ge(gla_saved, 1 + 2 * GLA_H)
            actv(SILU_E, GG, ACT.Exp, scale=-1.0).then_inc(sem("gla_silu_e"), 1)
            actv(ORS, OSQ, ACT.Sqrt, bias=EPSC[:, :], scale=1.0 / DV).then_inc(sem("gla_ostd"), 1)
            for g in range(4):
                act.wait_ge(sem("gla_out_turned"), g + 1)
                for b in range(2):
                    k = 4 * g + 2 * b
                    end = actv(HM[:, k:k + 2, 0:T2],
                               MAIN[2 * (g % 2) + b][:, :].rearrange("p (c t) -> p c t", c=2), ACT.Copy)
                end.then_inc(sem("gla_hi"), 1)

        def gla_vector(dve, link):
            ts, tt, stt = nc.vector.tensor_scalar, nc.vector.tensor_tensor, nc.vector.scalar_tensor_tensor
            dve.sem_inc(gla_saved, 1)
            dve.wait_ge(bank_free, 4 + 2 * M_WO1)
            dve.wait_ge(sem("gla_in"), 5 * 16)
            with dve.Fori(0, GLA_H) as i:
                for t in range(2):
                    n = i * 2 + (t + 1)
                    cols = ds(i * DK, DK)
                    if t == 0:
                        ts(W2H, W2A[:, cols], 1.0, None, ALU.mult).then_inc(sem("gla_w2_staged"), 1)
                        ts(QKST[:, 0, :], QG[:, 0, cols], 1.0, None, ALU.mult)
                        ts(QKST[:, 1, :], KG[:, 0, cols], 1.0, None, ALU.mult).then_inc(sem("gla_staged"), 1)
                    else:
                        for x, src in enumerate((QG, KG)):
                            v = src[:, 1, cols].rearrange("p (h x n) -> p h x n", h=2, x=2)
                            for r, (a, tab) in enumerate(((0, COS), (1, SIN), (0, SIN), (1, COS))):
                                end = tt(ROT[:, 4 * x + r], v[:, :, a, :], tab, ALU.mult)
                        end.then_inc(sem("gla_rot"), 1)
                        dve.wait_ge(sem("gla_rot"), i + 1)
                        for x in range(2):
                            v = QKST[:, x, :].rearrange("p (h x n) -> p h x n", h=2, x=2)
                            tt(v[:, :, 0, :], ROT[:, 4 * x], ROT[:, 4 * x + 1], ALU.subtract)
                            end = tt(v[:, :, 1, :], ROT[:, 4 * x + 2], ROT[:, 4 * x + 3], ALU.add)
                        end.then_inc(sem("gla_staged"), 1)
                    dve.wait_ge(sem("gla_ln"), n)
                    for d in range(2):
                        end = stt(LOGA[:, d, :], Z_B[d], 0.0, KEND[:, d, :], ALU.min, ALU.subtract)
                    end.then_inc(sem("gla_loga"), 1)
                    dve.wait_ge(sem("gla_exps"), n)
                    nc.vector.memset(TMP[:, 7168:7424], 0.0)
                    for d in range(2):
                        for k in range(2):
                            c = k if d == 0 else 1 - k
                            at = CHUNK * c + (CHUNK - 1 if d == 0 else 0)
                            end = nc.vector.tensor_copy(
                                DECAY[:, d, k, :],
                                QDEC[:, d, :].rearrange("p (j t) -> p j t", j=2)[:, :, at])
                    end.then_inc(sem("gla_decay"), 1)
                    dve.wait_ge(sem("gla_decay"), n)
                    tt(QDEC, QDEC, QKTT[:, 0:1, :].broadcast_to([P, 2, DK]), ALU.mult)
                    tt(KDEC, KDEC, QKTT[:, 1:2, :].broadcast_to([P, 2, DK]), ALU.mult)
                    ts(VHEAD, VG[:, t, ds(i * DV, DV)], 1.0, None, ALU.mult)
                    tt(KEND, KEND, QKST[:, 1:2, :].broadcast_to([P, 2, DK]), ALU.mult).then_inc(
                        sem("gla_gated"), 1)
                    dve.wait_ge(sem("gla_att"), n)
                    nc.vector.memset(WAITED, 0.0)
                    for d in range(2):
                        end = nc.vector.copy_predicated(ATT[:, d, :], CUM_TAB[d].bitcast(u32),
                                                        ATT_B[:, P * d:P * d + P])
                    end.then_inc(sem("gla_masked"), 1)
                    dve.wait_ge(sem("gla_masked"), n)
                    tt(ATTSUM, ATT[:, 0, :], ATT[:, 1, :], ALU.add).then_inc(sem("gla_att_ready"), 1)
                    dve.wait_ge(sem("gla_kv"), n)
                    if t == 1:
                        dve.wait_ge(sem("gla_st0_in"), i * 32 + 32)
                    for d in range(2):
                        for j in range(2):
                            if t == 0:
                                end = ts(ST1[:, d, j, :], KV_B[2 * d + j][:, :], 1.0, None, ALU.mult)
                            else:
                                end = stt(ST1[:, d, j, :], ST0[:, d, j, :], DECAY[:, d, 0, j:j + 1],
                                          KV_B[2 * d + j][:, :], ALU.mult, ALU.add)
                    end.then_inc(sem("gla_state"), 1)
                    if t == 0:
                        dve.wait_ge(sem("gla_state"), n)
                        dve.wait_ge(sem("gla_kv2"), i + 1)
                        for d in range(2):
                            for j in range(2):
                                end = stt(ST0[:, d, j, :], ST1[:, d, j, :], DECAY[:, d, 1, j:j + 1],
                                          KV_B[2 * d + j][:, :], ALU.mult, ALU.add)
                        end.then_inc(sem("gla_final"), 1)
                    dve.wait_ge(sem("gla_osq"), n)
                    ts(VG[:, t, ds(i * DV, DV)], QK_B[:, :], 1.0, None, ALU.mult).then_inc(gla_saved, 1)
            dve.wait_ge(sem("gla_silu_e"), 1)
            e = TMP[:, 0:4096]
            link(ts(e, e, 1.0, None, ALU.add))
            link(nc.vector.reciprocal(e, e))
            gg = SCR[:, 2 * S4:3 * S4]
            link(tt(gg, gg, e, ALU.mult))
            dve.wait_ge(sem("ghead_in"), 16)
            g8 = gg.rearrange("p (x v) -> p x v", v=DV)
            link(tt(g8, g8, GHEAD.unsqueeze(1).broadcast_to([P, 2 * GLA_H, DV]), ALU.mult))
            dve.wait_ge(sem("gla_ostd"), 1)
            link(nc.vector.reciprocal(ORS, ORS))
            for h in range(GLA_H):
                for t in range(2):
                    cols = slice(DV * h, DV * h + DV)
                    end = stt(VG[:, t, cols], VG[:, t, cols], ORS[:, 2 * h + t:2 * h + t + 1], GG[:, t, cols],
                              ALU.mult, ALU.mult)
            end.then_inc(sem("gla_out_ready"), 1)
            for g in range(4):
                dve.wait_ge(sem("gla_hi"), g + 1)
                for b in range(2):
                    k = 4 * g + 2 * b
                    end = tt(HM[:, k:k + 2, T2:2 * T2],
                             MAIN[2 * (g % 2) + b][:, :].rearrange("p (c t) -> p c t", c=2),
                             HM[:, k:k + 2, 0:T2].bitcast(f32), ALU.subtract)
                end.then_inc(h_ready, 1)

        def gla_pool(pool):
            pool.wait_ge(hid_done, HID_GROUPS * KC + 2)
            pool.dma_start(CB[:, 0:768], t_gla).then_inc(sem("gla_in"), 16)
            nc.gpsimd.memset(CB[0:64, 768:2048], 1.0).then_inc(sem("low_rank_ones"), 1)
            pool.wait_ge(sem("low_rank_ones"), 1)
            for d in range(2):
                pool.dma_start(W2A[32 * d:32 * d + RANK, :], w_a2_gla[0, d]).then_inc(sem("gla_in"), 16)
                pool.dma_start(W2A[32 * d + RANK:32 * d + RANK + 1, :], b_a_gla[0, d:d + 1]).then_inc(
                    sem("gla_in"), 16)
            pool.wait_ge(x_ready, 8)
            nc.gpsimd.memset(A1, 0.0).then_inc(sem("a1_zero"), 1)
            pool.wait_ge(sem("a1_zero"), 1)
            for d in range(2):
                pool.dma_start(A1[:, :, 32 * d:32 * d + RANK],
                               w_a1_gla[0, d].rearrange("(c p) r -> p c r", p=P)).then_inc(sem("a1_in"), 16)
            for i in range(GLA_H):
                pool.wait_ge(sem("gla_final"), i + 1)
                for d in range(2):
                    pool.dma_start(
                        new_gla[0, 0, d, i].rearrange("(j p) v -> p j v", p=P),
                        ST0[:, d, :, :]).then_inc(sem("gla_final_out"), 16)
                pool.wait_ge(sem("gla_final_out"), i * 32 + 32)
                for d in range(2):
                    pool.dma_start(
                        ST0[:, d, :, :],
                        state_gla[0, 0, d, i].rearrange("(j p) v -> p j v", p=P)
                    ).then_inc(sem("gla_st0_in"), 16)
            pool.wait_ge(gla_saved, 1 + 2 * GLA_H)
            pool.dma_start(GHEAD, g_head_gla[0:1, :].partition_broadcast(P)).then_inc(sem("ghead_in"), 16)
            pool.wait_ge(sem("gla_out_turned"), 4)
            nc.gpsimd.memset(SCR[:, 2 * S4:3 * S4], 0.0).then_inc(y_zero, 1)

        block = ctx.enter_context(nc.Block())

        @block.sync
        def _(sp):
            def load_slab(m, w, row, col):
                for u in range(2):
                    sp.wait_ge(lo_done, m * 2 + u + 1)
                    src = w[ds(row + u * UNIT_ROWS, UNIT_ROWS), ds(col, UC)].rearrange("(c p) n -> p c n", p=P)
                    sp.dma_start(RAW[:, u, :].rearrange("p (c n) -> p c n", c=UKC), src).then_inc(raw_in[u], 16)

            def load_ada(a, layer, col):
                for u in range(2):
                    sp.wait_ge(ada0_used if u == 0 else ada_done, a + 1)
                    src = w_ada[layer, u * UNIT_ROWS:(u + 1) * UNIT_ROWS, ds(col, UC)] \
                        .rearrange("(c p) n -> p c n", p=P)
                    sp.dma_start(ADW[:, u, :].rearrange("p (c n) -> p c n", c=UKC), src).then_inc(ada_in[u], 16)

            def stream(m, bodies, w, row, ada, a=0, layer=0, a_first=0):
                with sp.Fori(0, bodies) as i:
                    for s in range(2):
                        load_slab(i * 2 + (m + s), w, row, i * (2 * UC) + s * UC)
                        if s < ada:
                            load_ada(i * ada + (a + s), layer, i * (ada * UC) + (a + s - a_first) * UC)

            wq0 = w_qkv_na[0]
            load_slab(0, wq0, 0, 0)
            with sp.Fori(0, A_QKV0) as i:
                load_ada(i, 0, i * UC)
            load_slab(1, wq0, 0, UC)
            load_ada(A_QKV0, 0, A_QKV0 * UC)
            load_ada(A_QKV0 + 1, 0, (A_QKV0 + 1) * UC)
            with sp.Fori(1, 3 * NB) as i:
                for s in range(2):
                    load_slab(i * 2 + s, wq0, 0, i * (2 * UC) + s * UC)
                    load_ada(i * 2 + (A_QKV0 + s), 0, i * (2 * UC) + (A_QKV0 + s) * UC)
            stream(M_WO0, NB, w_o_na[0], 0, 2, A_WO0, 0, 0)

            def mlp(layer, m, a):
                with sp.Fori(0, HID_GROUPS) as g:
                    for half, w in ((0, w1_mlp[layer]), (1, w2_mlp[layer])):
                        with sp.Fori(0, NB) as i:
                            for s in range(2):
                                mm = g * (4 * NB) + i * 2 + (m + 2 * NB * half + s)
                                if half == 0:
                                    load_slab(mm, w, 0, g * D + i * (2 * UC) + s * UC)
                                else:
                                    load_slab(mm, w, g * D, i * (2 * UC) + s * UC)
                                if s == 0 and a is not None:
                                    aa = g * (2 * NB) + i + NB * half
                                    load_ada(aa + a, 1, aa * UC)

            mlp(0, M_MLP0, A_MLP0)
            stream(M_QKV1, 3 * NB, w_qkvg_gla[0], 0, 1, A_QKV1, 1, A_MLP0)
            stream(M_WO1, NB, w_o_gla[0], 0, 1, A_WO1, 1, A_MLP0)
            mlp(1, M_MLP1, None)
            for q in range(8):
                s, cols = q // 4, slice(512 * (q % 4), 512 * (q % 4) + 512)
                sp.wait_ge(sem("out_staged"), q + 1)
                sp.dma_start((y_prompt, y_sample)[s][0, :, cols], OUTS[:, s, cols]).then_inc(sem("y_out"), 16)
            sp.wait_ge(sem("y_out"), 8 * 16)

        @block.tensor
        def _(pe):
            mm = nc.tensor.matmul
            pe.sem_inc(unit0_used, 2)
            pe.sem_inc(block_done, 4)
            pe.sem_inc(ada0_used, 1)
            pe.sem_inc(ada_done, 1)

            def unit(m, s, u, body):
                pe.wait_ge(lo_done, m * 2 + u + 3)
                slot = 2 * s + u
                hi = WHI[:, slot, :].rearrange("p (c n) -> p c n", c=UKC)
                lo = WLO[:, slot, :].rearrange("p (c n) -> p c n", c=UKC)
                for b in range(2):
                    if u == 0:
                        pe.wait_ge(bank_free, m * 2 + b + 1)
                    bank = MAIN[2 * s + b]
                    for k in range(UKC):
                        first, last = u == 0 and k == 0, u == 1 and k == UKC - 1
                        end = body(bank, hi, lo, b, UKC * u + k, k, first, last)
                    if u == 1:
                        end.then_inc(block_done, 1)
                if u == 0:
                    end.then_inc(unit0_used, 1)

            def features_out(act):
                def body(bank, hi, lo, b, kc, k, first, last):
                    cols = slice(P * b, P * b + P)
                    mm(bank[:, 0:T2], hi[:, k, cols], act[:, kc, 0:T2], start=first, stop=False)
                    mm(bank[:, 0:T2], hi[:, k, cols], act[:, kc, T2:2 * T2], start=False, stop=False)
                    return mm(bank[:, 0:T2], lo[:, k, cols], act[:, kc, 0:T2], start=False, stop=last)
                return body

            def tokens_out(act):
                def body(bank, hi, lo, b, kc, k, first, last):
                    xh = act[:, kc, TOK * b:TOK * b + TOK]
                    xl = act[:, kc, T2 + TOK * b:T2 + TOK * b + TOK]
                    mm(bank[:, 0:UC], xh, hi[:, k, :], start=first, stop=False)
                    mm(bank[:, 0:UC], xh, lo[:, k, :], start=False, stop=False)
                    return mm(bank[:, 0:UC], xl, hi[:, k, :], start=False, stop=last)
                return body

            def ada_rows(a):
                for u in range(2):
                    pe.wait_ge(ada_in[u], a * 16 + 16)
                    w = ADW[:, u, :].rearrange("p (c n) -> p c n", c=UKC)
                    for r in range(2):
                        for j in range(4):
                            k = 4 * r + j
                            end = mm(ROWB[32 * j:32 * j + 32, 0:UC], CS[:, UKC * u + k, :], w[:, k, :],
                                     start=(u == 0 and r == 0), stop=(u == 1 and r == 1))
                    end.then_inc(ada0_used if u == 0 else ada_done, 1)

            def ada_select(a):
                pe.wait_ge(row_ready, a + 1)
                pe.wait_ge(mod_done, a + 1)
                for b in range(2):
                    end = mm(SELB[:, 2 * b:2 * b + 2], MROW[:, P * b:P * b + P], SEL, start=True, stop=True)
                end.then_inc(sel_done, 1)

            def step(m, s, body, ada=None, act_waits=None):
                for u in range(2):
                    if act_waits:
                        act_waits(u)
                    unit(m, s, u, body)
                    if ada is not None:
                        (ada_rows if u == 0 else ada_select)(ada)

            def stream(m, bodies, body, ada, a=0, act_waits=None, start=0):
                with pe.Fori(start, bodies) as i:
                    for s in range(2):
                        step(i * 2 + (m + s), s, body, i * ada + (a + s) if s < ada else None, act_waits)

            def filled(f):
                return lambda u: pe.wait_ge(h_ready, 4 * f + 2 + 2 * u)

            def norm_sum(r):
                for g in range(4):
                    pe.wait_ge(parts, 4 * r + g + 1)
                    end = mm(NORMB[:, 0:T2], ONES[:, :], PART[:, g, :], start=(g == 0), stop=(g == 3))
                end.then_inc(sumsq, 1)

            pe.wait_ge(sem("small_in"), 6 * 16)
            rows = (P, ADA_BLOCKS, ADA_BLOCKS, 2 * KC)
            off = 0
            for a, n in enumerate(rows):
                end = nc.tensor.transpose(psum[7][:, off:off + n], SMALL[0:n, a, :], IDENT[0:n, 0:n])
                off += n
            end.then_inc(sem("small_turned"), 1)
            pe.wait_ge(sem("x_in"), 2 * 16)
            for q in range(8):
                s, c0 = q // 4, 4 * (q % 4)
                if q >= 4:
                    pe.wait_ge(sem("x_copied"), q - 3)
                for j in range(4):
                    end = nc.tensor.transpose(MAIN[q % 4][:, P * j:P * j + P],
                                              XLD[:, s, P * (c0 + j):P * (c0 + j + 1)], IDENT)
                end.then_inc(sem("x_turned"), 1)
            pe.wait_ge(sem("ones_set"), 3)
            pe.wait_ge(sem("cond_ready"), 1)
            with pe.Fori(0, A_QKV0) as i:
                ada_rows(i)
                ada_select(i)

            norm_sum(0)
            with pe.Fori(0, 2 * NB) as i:
                for s in range(2):
                    step(i * 2 + s, s, features_out(HM), i * 2 + (A_QKV0 + s), filled(0))
            stream(M_QKV0 + 4 * NB, NB, tokens_out(HM), 2, A_QKV0 + 4 * NB)
            attention_tensor(pe)
            stream(M_WO0, NB, features_out(HM), 2, A_WO0, filled(1))
            norm_sum(1)
            norm_sum(2)

            def mlp(layer, m, a, f):
                with pe.Fori(0, HID_GROUPS) as g:
                    for half in range(2):
                        with pe.Fori(0, NB) as i:
                            for s in range(2):
                                slab = g * (4 * NB) + i * 2 + (m + 2 * NB * half + s)
                                ada = None
                                if s == 0 and a is not None:
                                    ada = g * (2 * NB) + i + (NB * half + a)
                                if half == 0:
                                    step(slab, s, features_out(HM), ada, filled(f))
                                else:
                                    step(slab, s, features_out(HID), ada,
                                         lambda u, g=g: pe.wait_ge(
                                             hid_done, g * KC + (layer * HID_GROUPS * KC + UKC * (u + 1) + 2)))

            mlp(0, M_MLP0, A_MLP0, 2)
            norm_sum(3)
            norm_sum(4)
            gla_low_rank_tensor(pe)
            stream(M_QKV1, 3 * NB, tokens_out(HM), 1, A_QKV1, filled(3))
            gla_tensor(pe)
            stream(M_WO1, NB, features_out(HM), 1, A_WO1, filled(4))
            norm_sum(5)
            norm_sum(6)
            mlp(1, M_MLP1, None, 5)
            norm_sum(7)
            for q in range(8):
                s, c0 = q // 4, 4 * (q % 4)
                pe.wait_ge(x_ready, 4 * 3 + (q % 4) + 1)
                if q >= 4:
                    pe.wait_ge(sem("out_staged"), q - 3)
                for j in range(4):
                    end = nc.tensor.transpose(MAIN[q % 4][:, P * j:P * j + P],
                                              X[:, c0 + j, TOK * s:TOK * s + TOK], IDENT)
                end.then_inc(sem("out_turned"), 1)

        @block.scalar
        def _(act):
            actv = nc.scalar.activation

            def split_hi(m, s):
                for u in range(2):
                    act.wait_ge(raw_in[u], m * 16 + 16)
                    if u == 0:
                        act.wait_ge(unit0_used, m + 1)
                    else:
                        act.wait_ge(block_done, m * 2 + 2)
                    actv(WHI[:, 2 * s + u, :], RAW[:, u, :], ACT.Copy).then_inc(hi_done, 1)

            def ada_row(a):
                act.wait_ge(ada_done, a + 2)
                actv(MROW[:, :], ROWB[:, 0:UC], ACT.Copy).then_inc(row_ready, 1)

            def square_hidden(k):
                for b in range(2):
                    act.wait_ge(relu_done, k + b + 1)
                    actv(RELU[:, b, :], RELU[:, b, :], ACT.Square).then_inc(square_done, 1)

            def step(m, s, ada=None, hidden=None, prefetch=True):
                if prefetch:
                    split_hi(m + 1, 1 - s)
                if ada is not None:
                    ada_row(ada)
                if hidden is not None:
                    square_hidden(hidden)

            def stream(m, bodies, ada, a=0):
                with act.Fori(0, bodies) as i:
                    for s in range(2):
                        step(i * 2 + (m + s), s, i * ada + (a + s) if s < ada else None)

            def norm_squares(r, src):
                for g in range(4):
                    if r in (2, 4, 6):
                        act.wait_ge(x_ready, 4 * (r // 2 - 1) + g + 1)
                    actv(SQ[:, 4 * g:4 * g + 4, :], src[:, 4 * g:4 * g + 4, :], ACT.Square).then_inc(squares, 1)
                act.wait_ge(sumsq, r + 1)
                actv(STD, NORMB[:, 0:T2], ACT.Sqrt, bias=EPSC[:, :], scale=1.0 / D).then_inc(std_ready, 1)

            def modulate(f, layer, j):
                shift = ADA_BLOCKS * layer + KC * j
                for g in range(4):
                    act.wait_ge(xn_ready, 4 * f + g + 1)
                    for k in range(4 * g, 4 * g + 4):
                        for s in range(2):
                            t = slice(TOK * s, TOK * s + TOK)
                            end = actv(SQ[:, k, t], SQ[:, k, t], ACT.Identity,
                                       bias=MODT[:, shift + k, s:s + 1], scale=GAIN[:, k, s:s + 1])
                    end.then_inc(mod_x, 1)
                    act.wait_ge(mod_x, 4 * f + g + 1)
                    actv(HM[:, 4 * g:4 * g + 4, 0:T2], SQ[:, 4 * g:4 * g + 4, :], ACT.Copy).then_inc(hm_hi, 1)

            act.dma_start(BASE[:, :], t_base).then_inc(sem("small_in"), 16)
            act.dma_start(SMALL[:, 0, :], norm_g.rearrange("l j (c p) -> (l j c) p", p=P)).then_inc(
                sem("small_in"), 16)
            for layer in range(2):
                act.dma_start(SMALL[0:ADA_BLOCKS, 1 + layer, :],
                              b_ada[layer].rearrange("(c p) -> c p", p=P)).then_inc(sem("small_in"), 16)
            act.dma_start(SMALL[0:KC, 3, :], c_ctx.rearrange("(c p) -> c p", p=P)).then_inc(sem("small_in"), 16)
            act.dma_start(SMALL[KC:2 * KC, 3, :], c[0].rearrange("(c p) -> c p", p=P)).then_inc(
                sem("small_in"), 16)
            act.wait_ge(sem("ones_set"), 3)
            split_hi(0, 0)
            act.wait_ge(sem("small_turned"), 1)
            actv(NGT[:, :], psum[7][:, 0:P], ACT.Copy).then_inc(sem("gains_ready"), 1)
            actv(BT[:, :], psum[7][:, P:P + 2 * ADA_BLOCKS], ACT.Copy).then_inc(sem("biases_ready"), 1)
            actv(CC, psum[7][:, P + 2 * ADA_BLOCKS:P + 2 * ADA_BLOCKS + 2 * KC], ACT.Copy).then_inc(
                sem("cond_copied"), 1)
            act.wait_ge(sem("cond_copied"), 1)
            actv(CE, CC, ACT.Exp, scale=-1.0).then_inc(sem("cond_exp"), 1)
            for q in range(8):
                s, c0 = q // 4, 4 * (q % 4)
                act.wait_ge(sem("x_turned"), q + 1)
                actv(X[:, c0:c0 + 4, TOK * s:TOK * s + TOK],
                     MAIN[q % 4][:, :].rearrange("p (c t) -> p c t", c=4), ACT.Copy).then_inc(sem("x_copied"), 1)
            act.wait_ge(sem("x_copied"), 8)
            with act.Fori(0, A_QKV0) as i:
                ada_row(i)

            norm_squares(0, X)
            modulate(0, 0, 0)
            stream(M_QKV0, 3 * NB, 2, A_QKV0)
            attention_scalar(act)
            stream(M_WO0, NB, 2, A_WO0)
            act.wait_ge(bank_free, 4 + 2 * M_MLP0)
            norm_squares(1, Y)
            norm_squares(2, X)
            modulate(1, 0, 3)

            def mlp(layer, m, a, last):
                with act.Fori(0, HID_GROUPS - (1 if last else 0)) as g:
                    mlp_group(g, layer, m, a)
                if last:
                    mlp_group(HID_GROUPS - 1, layer, m, a, last)

            def mlp_group(g, layer, m, a, last=False):
                for half in range(2):
                    peel = last and half == 1
                    with act.Fori(0, NB - (1 if peel else 0)) as i:
                        mlp_body(g, i, half, layer, m, a)
                    if peel:
                        mlp_body(g, NB - 1, half, layer, m, a, True)

            def mlp_body(g, i, half, layer, m, a, end=False):
                for s in range(2):
                    slab = g * (4 * NB) + i * 2 + (m + 2 * NB * half + s)
                    ada = None
                    if s == 0 and a is not None:
                        ada = g * (2 * NB) + i + (NB * half + a)
                    hidden = None
                    if half == 0:
                        hidden = g * KC + i * 4 + (layer * HID_GROUPS * KC + 2 * s)
                    step(slab, s, ada, hidden, prefetch=not (end and s == 1))

            mlp(0, M_MLP0, A_MLP0, False)
            act.wait_ge(bank_free, 4 + 2 * M_QKV1)
            norm_squares(3, Y)
            norm_squares(4, X)
            modulate(2, 1, 0)
            stream(M_QKV1, 3 * NB, 1, A_QKV1)
            gla_scalar(act)
            stream(M_WO1, NB, 1, A_WO1)
            act.wait_ge(bank_free, 4 + 2 * M_MLP1)
            norm_squares(5, Y)
            norm_squares(6, X)
            modulate(3, 1, 3)
            mlp(1, M_MLP1, None, True)
            act.wait_ge(bank_free, 4 + 2 * M_END)
            norm_squares(7, Y)
            for q in range(8):
                act.wait_ge(sem("out_turned"), q + 1)
                actv(OUTS[:, q // 4, 512 * (q % 4):512 * (q % 4) + 512], MAIN[q % 4][:, :], ACT.Copy).then_inc(
                    sem("out_staged"), 1)

        @block.vector
        def _(dve):
            tt = nc.vector.tensor_tensor
            ts = nc.vector.tensor_scalar
            own = sem("dve_own")
            count = [0]

            def link(ins):
                count[0] += 1
                ins.then_inc(own, 1)
                dve.wait_ge(own, count[0])

            dve.sem_inc(lo_done, 2)
            dve.sem_inc(bank_free, 4)
            dve.sem_inc(mod_done, 1)
            dve.sem_inc(hid_done, 2)

            def split_lo(m, s):
                for u in range(2):
                    dve.wait_ge(hi_done, m * 2 + u + 1)
                    tt(WLO[:, 2 * s + u, :], RAW[:, u, :], WHI[:, 2 * s + u, :].bitcast(f32),
                       ALU.subtract).then_inc(lo_done, 1)

            def ada_mod(a):
                dve.wait_ge(sel_done, a + 1)
                tt(MODT[:, ds(a * 2, 2), :], SELB[:, 0:4].rearrange("p (b s) -> p b s", b=2),
                   BT[:, ds(a * 2, 2)].unsqueeze(2).broadcast_to([P, 2, 2]),
                   ALU.add).then_inc(mod_done, 1)

            def evacuate(m, s, how):
                for b in range(2):
                    dve.wait_ge(block_done, m * 2 + b + 5)
                    how(MAIN[2 * s + b][:, 0:T2], b).then_inc(bank_free, 1)

            def step(m, s, how, ada=None, after=None, prefetch=True):
                if prefetch:
                    split_lo(m + 1, 1 - s)
                evacuate(m, s, how)
                if ada is not None:
                    ada_mod(ada)
                if after:
                    after()

            def stream(m, bodies, how, ada, a=0):
                with dve.Fori(0, bodies) as i:
                    for s in range(2):
                        step(i * 2 + (m + s), s, how(i, s), i * ada + (a + s) if s < ada else None)

            def to_blocks(dst, first):
                return lambda i, s: lambda src, b: ts(
                    dst[:, ds(i * 4 + (first + 2 * s + b), 1), :].rearrange("p o t -> p (o t)"), src, 1.0, None,
                    ALU.mult)

            def to_tokens(dst, col):
                return lambda i, s: lambda src, b: ts(
                    dst[:, b, ds(i * (2 * UC) + (col + s * UC), UC)], src, 1.0, None, ALU.mult)

            def add_to_y(i, s):
                def how(src, b):
                    y = Y[:, ds(i * 4 + (2 * s + b), 1), :].rearrange("p o t -> p (o t)")
                    return tt(y, src, y, ALU.add)
                return how

            def norm_rstd(r):
                for g in range(4):
                    dve.wait_ge(squares, 4 * r + g + 1)
                    nc.vector.tensor_reduce(PART[:, g, :], SQ[:, 4 * g:4 * g + 4, :].rearrange("p c t -> p t c"),
                                            AX.X, ALU.add).then_inc(parts, 1)
                dve.wait_ge(std_ready, r + 1)
                link(nc.vector.reciprocal(RSTD, STD))

            def gain(layer, norm, mod, plus):
                first = ADA_BLOCKS * layer + KC * mod
                ng = NGT[:, (4 * layer + norm) * KC:(4 * layer + norm + 1) * KC]
                link(ts(GAIN[:, :, :], MODT[:, first:first + KC, :], plus, None, ALU.add))
                link(tt(GAIN[:, :, :], GAIN[:, :, :],
                        ng.unsqueeze(2).broadcast_to([P, KC, 2]), ALU.mult))

            def residual(r, layer, norm, mod):
                gain(layer, norm, mod, 0.0)
                norm_rstd(r)
                for g in range(4):
                    q = slice(4 * g, 4 * g + 4)
                    link(tt(SQ[:, q, :], Y[:, q, :], RSTD.unsqueeze(1).broadcast_to([P, 4, T2]), ALU.mult))
                    for k in range(4 * g, 4 * g + 4):
                        for s in range(2):
                            t = slice(TOK * s, TOK * s + TOK)
                            end = nc.vector.scalar_tensor_tensor(X[:, k, t], SQ[:, k, t], GAIN[:, k, s:s + 1],
                                                                 X[:, k, t], ALU.mult, ALU.add)
                    end.then_inc(x_ready, 1)

            def pre_norm(r, f, layer, norm, mod, residual_no=None):
                if residual_no is not None:
                    dve.wait_ge(x_ready, 4 * residual_no + 4)
                gain(layer, norm, mod, 1.0)
                norm_rstd(r)
                for g in range(4):
                    q = slice(4 * g, 4 * g + 4)
                    tt(SQ[:, q, :], X[:, q, :], RSTD.unsqueeze(1).broadcast_to([P, 4, T2]), ALU.mult).then_inc(xn_ready, 1)
                for g in range(4):
                    q = slice(4 * g, 4 * g + 4)
                    dve.wait_ge(hm_hi, 4 * f + g + 1)
                    tt(HM[:, q, T2:2 * T2], SQ[:, q, :], HM[:, q, 0:T2].bitcast(f32), ALU.subtract).then_inc(
                        h_ready, 1)

            split_lo(0, 0)
            dve.wait_ge(sem("cond_exp"), 1)
            link(nc.vector.memset(CS[:, :, :], 0.0))
            link(ts(CE, CE, 1.0, None, ALU.add))
            link(nc.vector.reciprocal(CE, CE))
            tt(CS[:, :, 0:2], CC.rearrange("p (s c) -> p c s", s=2), CE.rearrange("p (s c) -> p c s", s=2),
               ALU.mult).then_inc(sem("cond_ready"), 1)
            dve.wait_ge(sem("biases_ready"), 1)
            with dve.Fori(0, A_QKV0) as i:
                ada_mod(i)
            dve.wait_ge(mod_done, A_QKV0 + 1)

            pre_norm(0, 0, 0, 0, 1)
            dve.wait_ge(sem("bias_ready"), 1)
            stream(M_QKV0, 2 * NB, to_blocks(QK, 0), 2, A_QKV0)
            stream(M_QKV0 + 4 * NB, NB, to_tokens(VN, 0), 2, A_QKV0 + 4 * NB)
            attention_vector(dve, link)
            dve.wait_ge(y_zero, 1)
            stream(M_WO0, NB, add_to_y, 2, A_WO0)
            dve.wait_ge(bank_free, 4 + 2 * M_MLP0)
            dve.wait_ge(mod_done, A_MLP0 + 1)
            residual(1, 0, 1, 2)
            pre_norm(2, 1 + 0, 0, 2, 4, 0)

            def mlp(layer, m, a, last):
                with dve.Fori(0, HID_GROUPS - (1 if last else 0)) as g:
                    mlp_group(g, layer, m, a)
                if last:
                    mlp_group(HID_GROUPS - 1, layer, m, a, last)

            def mlp_group(g, layer, m, a, last=False):
                for half in range(2):
                    peel = last and half == 1
                    with dve.Fori(0, NB - (1 if peel else 0)) as i:
                        mlp_body(g, i, half, layer, m, a)
                    if peel:
                        mlp_body(g, NB - 1, half, layer, m, a, True)

            def mlp_body(g, i, half, layer, m, a, end=False):
                for s in range(2):
                    slab = g * (4 * NB) + i * 2 + (m + 2 * NB * half + s)
                    ada = None
                    if s == 0 and a is not None:
                        ada = g * (2 * NB) + i + (NB * half + a)
                    if half == 1:
                        step(slab, s, add_to_y(i, s), ada, prefetch=not (end and s == 1))
                        continue
                    k = g * KC + i * 4 + (layer * HID_GROUPS * KC + 2 * s)
                    hid = [HID[:, ds(i * 4 + (2 * s + b), 1), :].rearrange("p o t -> p (o t)") for b in range(2)]
                    split_lo(slab + 1, 1 - s)
                    for b in range(2):
                        dve.wait_ge(hid_done, k + b + 1)
                        dve.wait_ge(block_done, slab * 2 + b + 5)
                        ts(RELU[:, b, :], MAIN[2 * s + b][:, 0:T2], 0.0, None, ALU.max).then_inc(relu_done, 1)
                    if ada is not None:
                        ada_mod(ada)
                    for b in range(2):
                        dve.wait_ge(square_done, k + b + 1)
                        ts(hid[b][:, 0:T2], RELU[:, b, :], 1.0, None, ALU.mult).then_inc(bank_free, 1)
                    for b in range(2):
                        dve.wait_ge(bank_free, slab * 2 + b + 5)
                        tt(hid[b][:, T2:2 * T2], RELU[:, b, :], hid[b][:, 0:T2].bitcast(f32),
                           ALU.subtract).then_inc(hid_done, 1)

            dve.wait_ge(y_zero, 2)
            mlp(0, M_MLP0, A_MLP0, False)
            dve.wait_ge(bank_free, 4 + 2 * M_QKV1)
            dve.wait_ge(mod_done, A_QKV1 + 1)
            residual(3, 0, 3, 5)
            pre_norm(4, 2, 1, 0, 1, 1)
            gla_low_rank_vector(dve)
            m, a = M_QKV1, A_QKV1
            for dst, n in ((QG, KEY), (KG, KEY), (VG, D), (GG, D)):
                bodies = n // (2 * UC)
                stream(m, bodies, to_tokens(dst, 0), 1, a)
                m, a = m + 2 * bodies, a + bodies
            gla_vector(dve, link)
            dve.wait_ge(y_zero, 3)
            stream(M_WO1, NB, add_to_y, 1, A_WO1)
            dve.wait_ge(bank_free, 4 + 2 * M_MLP1)
            dve.wait_ge(mod_done, A_END + 1)
            residual(5, 1, 1, 2)
            pre_norm(6, 3, 1, 2, 4, 2)
            dve.wait_ge(y_zero, 4)
            mlp(1, M_MLP1, None, True)
            dve.wait_ge(bank_free, 4 + 2 * M_END)
            residual(7, 1, 3, 5)

        @block.gpsimd
        def _(pool):
            for s, x in enumerate((x_prompt, x_sample)):
                pool.dma_start(XLD[:, s, :], x[0]).then_inc(sem("x_in"), 16)
            nc.gpsimd.memset(ONES[:, :], 1.0).then_inc(sem("ones_set"), 1)
            nc.gpsimd.memset(EPSC[:, :], EPS).then_inc(sem("ones_set"), 1)
            nc.gpsimd.memset(ONEC[:, :], 1.0).then_inc(sem("ones_set"), 1)
            nc.gpsimd.memset(RPT[0:N_DR * NA_H, :], 0.0).then_inc(sem("pad_zero"), 1)
            pool.wait_ge(sem("pad_zero"), 1)
            pool.dma_start(WINM, t_window).then_inc(sem("window_in"), 16)
            mid = GRID_W - 1
            for r in range(N_DR):
                pool.dma_start(RPT[NA_H * r:NA_H * r + NA_H, mid - WIN_COLS + 1:mid + WIN_COLS],
                               rpb_na[0, :, 6 + r, :]).then_inc(sem("rpb_in"), 16)
            pool.wait_ge(sem("rpb_in"), 16 * N_DR)
            pool.dma_start(rpb_pad.rearrange("r h q w -> (r h) q w"),
                           RPT[0:N_DR * NA_H, 0:LINE].unsqueeze(1).broadcast_to([N_DR * NA_H, GRID_W, LINE])).then_inc(
                sem("rpb_padded"), 16)
            pool.wait_ge(sem("rpb_padded"), 16)
            for qr in range(2):
                for kr in range(2):
                    src = bass.AP(rpb_pad.tensor, (1 - qr + kr) * NA_H * GRID_W * LINE + mid,
                                  [[LINE - 1, GRID_W], [GRID_W * LINE, NA_H], [1, GRID_W]])
                    pool.dma_start(BIAS[GRID_W * qr:GRID_W * qr + GRID_W, :, GRID_W * kr:GRID_W * kr + GRID_W],
                                   src).then_inc(sem("bias_in"), 16)
            pool.wait_ge(sem("bias_in"), 64)
            pool.wait_ge(sem("window_in"), 16)
            nc.gpsimd.tensor_tensor(BIAS, BIAS, WINM.unsqueeze(1).broadcast_to([P, NA_H, P]), ALU.add).then_inc(
                sem("bias_ready"), 1)
            attention_pool(pool)
            pool.wait_ge(x_ready, 4)
            nc.gpsimd.memset(SCR[:, 2 * S4:3 * S4], 0.0).then_inc(y_zero, 1)
            gla_pool(pool)
            pool.wait_ge(x_ready, 12)
            nc.gpsimd.memset(SCR[:, 2 * S4:3 * S4], 0.0).then_inc(y_zero, 1)
            pool.wait_ge(sem("newk_out"), 16)
            pool.wait_ge(sem("newv_out"), 16)
            pool.wait_ge(sem("gla_final_out"), 32 * GLA_H)


_INS = ['x_prompt', 'x_sample', 'cache_na_k', 'cache_na_v', 'state_gla', 'c', 'c_ctx', 'w_ada', 'b_ada', 'norm_g',
        'w_qkv_na', 'w_o_na', 'rpb_na', 'w_qkvg_gla', 'w_a1_gla', 'w_a2_gla', 'b_a_gla', 'g_head_gla', 'w_o_gla',
        'w1_mlp', 'w2_mlp']
_OUTS = [(1, TOK, D), (1, TOK, D), (1, 1, NA_H, TOK, DH), (1, 1, NA_H, TOK, DH), (1, 1, 2, GLA_H, DK, DV)]


def kernel(**inputs):
    import numpy as _np
    import concourse.bacc as _bacc
    from concourse import mybir as _mybir
    from concourse.bass_utils import run_bass_kernel_spmd as _run

    nc = _bacc.Bacc("TRN2", target_bir_lowering=False, num_devices=1)
    arrays, args = {}, []
    named = [(n, _np.ascontiguousarray(inputs[n])) for n in _INS]
    named += list(zip(("t_base", "t_window", "t_gla"), shape_tables()))
    for name, a in named:
        arrays[f"in_{name}"] = a
        args.append(nc.dram_tensor(f"in_{name}", a.shape, _mybir.dt.from_np(a.dtype), kind="ExternalInput").ap())
    for i, shape in enumerate(_OUTS):
        args.append(nc.dram_tensor(f"out_{i}", shape, _mybir.dt.float32, kind="ExternalOutput").ap())
    build_program(nc, *args)
    r = _run(nc, [arrays], core_ids=[0])
    return tuple(r.results[0][f"out_{i}"] for i in range(len(_OUTS)))
```

```python
import concourse.bass as bass
from concourse import mybir
from contextlib import ExitStack
import numpy as np

P = 128
D = 2048
KC = D // P
TOK = 128
T2 = 2 * TOK
FF = 4 * D
HID_GROUPS = FF // D
ADA = 6 * D
UNIT_ROWS = 1024
UKC = UNIT_ROWS // P
UC = 256
UNIT = UKC * UC
NA_H = 16
DH = 128
GRID_W = 64
WIN_COLS = 16
LINE = 2 * GRID_W - 1
N_DR = 3
GLA_H = 4
DK = 256
DV = 512
KEY = GLA_H * DK
CHUNK = 64
RANK = 16
EPS = 1e-6
NA_SCALE = DH ** -0.5
GLA_SCALE = DK ** -0.5
GATE_NORM = 16.0
NEG = -1e30
ADA_BLOCKS = ADA // P


def shape_tables():
    ident = np.eye(P, dtype=np.float32)
    sel = np.zeros((P, 2), np.float32)
    for j in range(4):
        sel[32 * j, 0] = 1.0
        sel[32 * j + 1, 1] = 1.0
    c = np.arange(P) % GRID_W
    start = np.clip(c - WIN_COLS // 2, 0, GRID_W - WIN_COLS)
    inside = (c[None, :] >= start[:, None]) & (c[None, :] < start[:, None] + WIN_COLS)
    window = np.where(inside, 0.0, NEG).astype(np.float32)
    s, t = np.arange(P)[:, None], np.arange(P)[None, :]
    same = (s // CHUNK) == (t // CHUNK)
    upto = [same & (s <= t), same & (s >= t)]
    after = [same & (s > t), same & (s < t)]
    gates = [m.astype(np.float32) / np.float32(GATE_NORM) for m in upto + after]
    n = DK // 4
    freqs = np.float32(10000.0) ** (-np.arange(n, dtype=np.float32) / np.float32(n))
    pos = np.arange(TOK)
    ang = np.concatenate([(pos // GRID_W).astype(np.float32)[:, None] * freqs[None],
                          (pos % GRID_W).astype(np.float32)[:, None] * freqs[None]], axis=1)
    base = np.concatenate([ident, sel], axis=1)
    gla = np.concatenate(gates + [np.cos(ang).astype(np.float32), np.sin(ang).astype(np.float32)], axis=1)
    return base, window, gla


def build_program(nc, x_prompt, x_sample, cache_na_k, cache_na_v, state_gla, c, c_ctx, w_ada, b_ada, norm_g,
                  w_qkv_na, w_o_na, rpb_na, w_qkvg_gla, w_a1_gla, w_a2_gla, b_a_gla, g_head_gla, w_o_gla,
                  w1_mlp, w2_mlp, t_base, t_window, t_gla,
                  y_prompt, y_sample, new_na_k, new_na_v, new_gla):
    f32 = mybir.dt.float32
    f32r = mybir.dt.float32r
    u32 = mybir.dt.uint32
    ALU = mybir.AluOpType
    ACT = mybir.ActivationFunctionType
    AX = mybir.AxisListType
    ds = bass.ds

    ctx = ExitStack()
    with ctx:
        def sb(name, shape, dt=f32):
            return ctx.enter_context(nc.sbuf_tensor(name, shape, dt))

        sems = {}

        def sem(name):
            if name not in sems:
                sems[name] = ctx.enter_context(nc.semaphore(name))
            return sems[name]

        with nc.sbuf_tensor("HID", [P, KC, 2 * T2], f32r) as HID:
            pass
        SCR = sb("SCR", [P, 3 * KC * T2])
        with nc.sbuf_tensor("HM", [P, KC, 2 * T2], f32r) as HM:
            pass
        TMP = sb("TMP", [P, 2 * KC * T2])
        X = sb("X", [P, KC, T2])
        RAW = sb("RAW", [P, 2, UNIT])
        with nc.sbuf_tensor("GLA_A", [P, 4, UNIT], f32) as GLA_A:
            pass
        WHI = sb("WHI", [P, 4, UNIT], f32r)
        with nc.sbuf_tensor("GLA_B", [P, 4, UNIT], f32) as GLA_B:
            pass
        WLO = sb("WLO", [P, 4, UNIT], f32r)
        ADW = sb("ADW", [P, 2, UNIT])
        CB = sb("CB", [P, 2048])
        BASE = sb("BASE", [P, P + 2])
        ONES = sb("ONES", [P, P])
        MODT = sb("MODT", [P, 2 * ADA_BLOCKS, 2])
        BT = sb("BT", [P, 2 * ADA_BLOCKS])
        NGT = sb("NGT", [P, P])
        CS = sb("CS", [P, KC, 32])
        MROW = sb("MROW", [P, UC])
        GAIN = sb("GAIN", [P, KC, 2])
        EPSC = sb("EPSC", [P, 1])
        ONEC = sb("ONEC", [P, 1])

        IDENT = BASE[:, 0:P]
        SEL = BASE[:, P:P + 2]
        S4 = KC * T2
        SQ = SCR[:, 0:S4].rearrange("p (c t) -> p c t", c=KC)
        PART = SCR[:, S4:S4 + 4 * T2].rearrange("p (g t) -> p g t", g=4)
        STD = SCR[:, S4 + 4 * T2:S4 + 5 * T2]
        RSTD = SCR[:, S4 + 5 * T2:S4 + 6 * T2]
        Y = SCR[:, 2 * S4:3 * S4].rearrange("p (c t) -> p c t", c=KC)
        XLD = SCR[:, 0:S4].rearrange("p (s n) -> p s n", s=2)
        OUTS = XLD
        SMALL = SCR[:, S4:S4 + 4 * P].rearrange("p (a n) -> p a n", a=4)
        CE = SCR[:, S4 + 4 * P:S4 + 4 * P + 32]
        CC = SCR[:, S4 + 5 * P:S4 + 5 * P + 32]
        WINM = SCR[:, 2 * S4:2 * S4 + P]
        RPT = SCR[:, 2 * S4 + P:2 * S4 + 2 * P]
        BIAS = CB[:, :].rearrange("p (h k) -> p h k", h=NA_H)
        RELU = CB[:, 0:2 * T2].rearrange("p (b t) -> p b t", b=2)
        QK = SCR[:, 0:2 * S4].rearrange("p (h t) -> p h t", h=2 * NA_H)
        VN = SCR[:, 2 * S4:3 * S4].rearrange("p (s n) -> p s n", s=2)

        psum = [ctx.enter_context(nc.psum_tensor(f"PS{i}", [P, 512], f32)) for i in range(8)]
        rpb_pad = nc.dram_tensor("rpb_pad", [N_DR, NA_H, GRID_W, LINE], f32, kind="Internal").ap()

        M_QKV0 = 0
        M_WO0 = M_QKV0 + 3 * D // UC
        M_MLP0 = M_WO0 + D // UC
        MLP_SLABS = 2 * HID_GROUPS * D // UC
        M_QKV1 = M_MLP0 + MLP_SLABS
        M_WO1 = M_QKV1 + 3 * D // UC
        M_MLP1 = M_WO1 + D // UC
        M_END = M_MLP1 + MLP_SLABS
        NB = D // UC // 2
        A_QKV0 = 2 * D // UC
        A_WO0 = A_QKV0 + 2 * 3 * NB
        A_MLP0 = A_WO0 + 2 * NB
        A_QKV1 = A_MLP0 + 2 * HID_GROUPS * NB
        A_WO1 = A_QKV1 + 3 * NB
        A_END = A_WO1 + NB
        assert A_END == 2 * ADA // UC

        raw_in = [sem("raw_in0"), sem("raw_in1")]
        hi_done = sem("hi_done")
        lo_done = sem("lo_done")
        unit0_used = sem("unit0_used")
        block_done = sem("block_done")
        bank_free = sem("bank_free")
        ada_in = [sem("ada_in0"), sem("ada_in1")]
        ada0_used = sem("ada0_used")
        ada_done = sem("ada_done")
        row_ready = sem("row_ready")
        sel_done = sem("sel_done")
        mod_done = sem("mod_done")
        relu_done = sem("relu_done")
        square_done = sem("square_done")
        hid_hi = sem("hid_hi")
        hid_done = sem("hid_done")
        h_ready = sem("h_ready")
        squares = sem("squares")
        parts = sem("parts")
        sumsq = sem("sumsq")
        std_ready = sem("std_ready")
        x_ready = sem("x_ready")
        xn_ready = sem("xn_ready")
        mod_x = sem("mod_x")
        hm_hi = sem("hm_hi")
        y_zero = sem("y_zero")

        MAIN = psum[0:4]
        ROWB = psum[4]
        SELB = psum[5]
        NORMB = psum[6]

        SLOT = 2056

        def slot(p, at, n):
            return TMP[:, SLOT * p + at:SLOT * p + at + n]

        QS = [slot(p, 0, T2) for p in range(2)]
        KS = [slot(p, 256, T2) for p in range(2)]
        VS = [slot(p, 512, T2).rearrange("p (s d) -> p s d", s=2) for p in range(2)]
        KCACHE = [slot(p, 768, DH) for p in range(2)]
        VCACHE = [slot(p, 896, DH) for p in range(2)]
        KCT = [slot(p, 1024, P) for p in range(2)]
        NEWK = TMP[:, 2 * SLOT:2 * SLOT + D]
        PROB = [slot(p, 1280, 3 * P) for p in range(2)]
        PROBT = [slot(p, 1664, 3 * P) for p in range(2)]
        MAXES = [slot(p, 2048, 2) for p in range(2)]
        NEGMAX = [slot(p, 2050, 2) for p in range(2)]
        ROWSUM = [slot(p, 2052, 2) for p in range(2)]
        RECIP = [slot(p, 2054, 2) for p in range(2)]
        SCORE_B, TURN_B, OUT_B, PROBT_B = psum[0:2], psum[2:4], psum[4:6], psum[6:8]
        cache_in = [sem("cache_in0"), sem("cache_in1")]
        head_done = sem("head_done")
        o_copied = sem("o_copied")
        PAIRS = NA_H // 2

        def attention_tensor(pe):
            mm, turn = nc.tensor.matmul, nc.tensor.transpose
            pe.sem_inc(head_done, 2)
            pe.wait_ge(bank_free, 4 + 2 * M_WO0)
            with pe.Fori(0, PAIRS) as i:
                for p in range(2):
                    pe.wait_ge(sem("qk_staged"), i * 2 + (p + 1))
                    pe.wait_ge(cache_in[p], i * 32 + 32)
                    turn(TURN_B[p][:, 0:P], KCACHE[p], IDENT)
                    turn(TURN_B[p][:, P:2 * P], KS[p][:, 0:TOK], IDENT).then_inc(sem("k_turned"), 1)
                    for s in range(2):
                        t = slice(TOK * s, TOK * s + TOK)
                        mm(SCORE_B[p][:, t], QS[p][:, t], KS[p][:, t], start=True, stop=True)
                    pe.wait_ge(sem("kct_ready"), i * 2 + (p + 1))
                    mm(SCORE_B[p][:, 2 * P:3 * P], QS[p][:, TOK:T2], KCT[p], start=True,
                       stop=True).then_inc(sem("scores_done"), 1)
                for p in range(2):
                    pe.wait_ge(sem("probs_ready"), i * 2 + (p + 1))
                    for b in range(3):
                        end = turn(PROBT_B[p][:, P * b:P * b + P], PROB[p][:, P * b:P * b + P], IDENT)
                    end.then_inc(sem("probs_turned"), 1)
                for p in range(2):
                    pe.wait_ge(sem("probt_ready"), i * 2 + (p + 1))
                    pe.wait_ge(sem("v_staged"), i * 2 + (p + 1))
                    pe.wait_ge(o_copied, i * 2 + (p + 1))
                    mm(OUT_B[p][:, 0:TOK], VS[p][:, 0, :], PROBT[p][:, 0:P], start=True, stop=True)
                    mm(OUT_B[p][:, TOK:T2], VS[p][:, 1, :], PROBT[p][:, P:2 * P], start=True, stop=False)
                    mm(OUT_B[p][:, TOK:T2], VCACHE[p], PROBT[p][:, 2 * P:3 * P], start=False,
                       stop=True).then_inc(head_done, 1)

        def attention_scalar(act):
            actv = nc.scalar.activation
            with act.Fori(0, PAIRS) as i:
                for p in range(2):
                    act.wait_ge(sem("k_turned"), i * 2 + (p + 1))
                    actv(KCT[p], TURN_B[p][:, 0:P], ACT.Copy).then_inc(sem("kct_ready"), 1)
                    actv(NEWK[:, ds(i * (2 * DH) + p * DH, DH)], TURN_B[p][:, P:2 * P], ACT.Copy).then_inc(
                        sem("newk_staged"), 1)
                for p in range(2):
                    act.wait_ge(sem("negmax_ready"), i * 2 + (p + 1))
                    actv(PROB[p][:, 0:P], SCORE_B[p][:, 0:P], ACT.Exp, bias=NEGMAX[p][:, 0:1],
                         accum_out=ROWSUM[p][:, 0:1])
                    actv(PROB[p][:, P:3 * P], SCORE_B[p][:, P:3 * P], ACT.Exp, bias=NEGMAX[p][:, 1:2],
                         accum_out=ROWSUM[p][:, 1:2]).then_inc(sem("exp_done"), 1)
                for p in range(2):
                    act.wait_ge(sem("probs_turned"), i * 2 + (p + 1))
                    actv(PROBT[p], PROBT_B[p][:, 0:3 * P], ACT.Copy).then_inc(sem("probt_ready"), 1)
            act.wait_ge(o_copied, 2 + NA_H)
            act.wait_ge(sem("newk_out"), 16)
            for g in range(4):
                actv(HM[:, 4 * g:4 * g + 4, 0:T2], QK[:, 4 * g:4 * g + 4, :], ACT.Copy).then_inc(sem("o_hi"), 1)

        def attention_vector(dve, link):
            ts, tt = nc.vector.tensor_scalar, nc.vector.tensor_tensor
            dve.sem_inc(o_copied, 2)
            dve.wait_ge(bank_free, 4 + 2 * M_WO0)

            def head(ap, h):
                return ap[:, ds(h, 1), :].rearrange("p o t -> p (o t)")

            with dve.Fori(0, PAIRS) as i:
                for p in range(2):
                    dve.wait_ge(head_done, i * 2 + (p + 1))
                    ts(QS[p], head(QK, i * 2 + p), NA_SCALE, None, ALU.mult)
                    ts(KS[p], head(QK, i * 2 + (NA_H + p)), 1.0, None, ALU.mult).then_inc(sem("qk_staged"), 1)
                for p in range(2):
                    dve.wait_ge(sem("scores_done"), i * 2 + (p + 1))
                    lat = SCORE_B[p][:, P:2 * P]
                    tt(lat, lat, head(BIAS, i * 2 + p), ALU.add).then_inc(sem("biased"), 1)
                    nc.vector.reduce_max(MAXES[p][:, 0:1], SCORE_B[p][:, 0:P], AX.X)
                    dve.wait_ge(sem("biased"), i * 2 + (p + 1))
                    nc.vector.reduce_max(MAXES[p][:, 1:2], SCORE_B[p][:, P:3 * P], AX.X).then_inc(sem("maxed"), 1)
                    dve.wait_ge(sem("maxed"), i * 2 + (p + 1))
                    ts(NEGMAX[p], MAXES[p], -1.0, None, ALU.mult).then_inc(sem("negmax_ready"), 1)
                for p in range(2):
                    dve.wait_ge(sem("exp_done"), i * 2 + (p + 1))
                    nc.vector.reciprocal(RECIP[p], ROWSUM[p]).then_inc(sem("recip_done"), 1)
                    dve.wait_ge(sem("recip_done"), i * 2 + (p + 1))
                    ts(PROB[p][:, 0:P], PROB[p][:, 0:P], RECIP[p][:, 0:1], None, ALU.mult)
                    ts(PROB[p][:, P:3 * P], PROB[p][:, P:3 * P], RECIP[p][:, 1:2], None,
                       ALU.mult).then_inc(sem("probs_ready"), 1)
                for p in range(2):
                    dve.wait_ge(head_done, i * 2 + (p + 3))
                    ts(head(QK, i * 2 + p), OUT_B[p][:, 0:T2], 1.0, None, ALU.mult).then_inc(o_copied, 1)
            for g in range(4):
                q = slice(4 * g, 4 * g + 4)
                dve.wait_ge(sem("o_hi"), g + 1)
                tt(HM[:, q, T2:2 * T2], QK[:, q, :], HM[:, q, 0:T2].bitcast(f32), ALU.subtract).then_inc(h_ready, 1)

        def attention_pool(pool):
            pool.wait_ge(bank_free, 4 + 2 * M_WO0)
            pool.dma_start(new_na_v[0, 0].rearrange("h t d -> t h d"),
                           VN[:, 0, :].rearrange("p (h d) -> p h d", h=NA_H)).then_inc(sem("newv_out"), 16)
            with pool.Fori(0, PAIRS) as i:
                for p in range(2):
                    pool.wait_ge(head_done, i * 2 + (p + 1))
                    pool.wait_ge(sem("bias_ready"), 1)
                    for dst, src in ((KCACHE[p], cache_na_k), (VCACHE[p], cache_na_v)):
                        pool.dma_start(dst, src[0, 0, ds(i * 2 + p, 1)].rearrange("o t d -> (o t) d")) \
                            .then_inc(cache_in[p], 16)
                    nc.gpsimd.tensor_copy(VS[p], VN[:, :, ds(i * (2 * DH) + p * DH, DH)]).then_inc(
                        sem("v_staged"), 1)
            pool.wait_ge(sem("newk_staged"), NA_H)
            pool.dma_start(new_na_k[0, 0].rearrange("h t d -> t h d"),
                           NEWK.rearrange("p (h d) -> p h d", h=NA_H)).then_inc(sem("newk_out"), 16)
            pool.wait_ge(head_done, 2 + NA_H)
            pool.wait_ge(sem("newv_out"), 16)
            nc.gpsimd.memset(SCR[:, 2 * S4:3 * S4], 0.0).then_inc(y_zero, 1)

        QG = SCR[:, 0:S4 // 2].rearrange("p (s n) -> p s n", s=2)
        KG = SCR[:, S4 // 2:S4].rearrange("p (s n) -> p s n", s=2)
        QKG = SCR[:, 0:S4].rearrange("p (x s n) -> p x s n", x=2, s=2)
        VG = SCR[:, S4:2 * S4].rearrange("p (s n) -> p s n", s=2)
        GG = SCR[:, 2 * S4:3 * S4].rearrange("p (s n) -> p s n", s=2)
        A1 = SCR[:, 2 * S4:2 * S4 + KC * 64].rearrange("p (c n) -> p c n", c=KC)
        ROT = SCR[:, 2 * S4:3 * S4].rearrange("p (x r h n) -> p x r h n", x=2, r=4, h=2 * GLA_H)
        CUM_TAB = [CB[:, 0:P], CB[:, P:2 * P]]
        AFTER_TAB = [CB[:, 2 * P:3 * P], CB[:, 3 * P:4 * P]]
        COS = CB[:, 4 * P:5 * P].rearrange("p (h n) -> p h n", h=2)
        SIN = CB[:, 5 * P:6 * P].rearrange("p (h n) -> p h n", h=2)
        W2A = CB[0:64, 768:768 + KEY]
        LOWR = CB[0:64, 1792:2048]
        FREE_A = GLA_A[:, 2:4, :].rearrange("p a n -> p (a n)")
        FREE_B = GLA_B[:, 2:4, :].rearrange("p a n -> p (a n)")
        ST0 = FREE_A[:, 0:2048].rearrange("p (d j v) -> p d j v", d=2, j=2)
        FINAL = FREE_A[:, 2048:4096].rearrange("p (d j v) -> p d j v", d=2, j=2)
        ST1 = FREE_B[:, 0:2048].rearrange("p (d j v) -> p d j v", d=2, j=2)
        GHEAD = FREE_B[:, 2048:2560]
        W2H = FREE_B[0:64, 2560:2560 + 2 * DK]
        OSQ = FREE_B[:, 3072:3080]
        ORS = FREE_B[:, 3080:3088]
        DECAY = [FREE_B[:, 3088 + 8 * t:3096 + 8 * t].rearrange("p (d n j) -> p d n j", d=2, n=2) for t in range(2)]
        WAITED = FREE_B[:, 3104:3105]
        QKST = TMP[:, 0:512].rearrange("p (x n) -> p x n", x=2)
        QKTT = TMP[:, 512:1024].rearrange("p (x n) -> p x n", x=2)
        LOGA = TMP[:, 1024:1536]
        EZ, EG = TMP[:, 1536:2048], TMP[:, 2048:2560]
        EZG = TMP[:, 1536:2560]

        def by_stream(at):
            return [TMP[:, at + 512 * t:at + 512 * t + 512] for t in range(2)]

        QDEC, KDEC, KEND, VHEAD = by_stream(2560), by_stream(3584), by_stream(4608), by_stream(5632)
        ATT = TMP[:, 6656:6912].rearrange("p (d n) -> p d n", d=2)
        ATTSUM = TMP[:, 6912:7040]
        OJUNK = TMP[:, 7040:7552]
        ATT_B, O_B, CUM_B, AFTER_B = psum[0], psum[1], psum[2], psum[3]
        Z_B, QK_B = CUM_B, AFTER_B
        KV_B = psum[4:8]
        gla_saved = sem("gla_saved")
        final_free = sem("final_free")

        def gla_low_rank_tensor(pe):
            pe.wait_ge(sem("a1_in"), 32)
            for g in range(4):
                pe.wait_ge(mod_x, 4 * 2 + g + 1)
                for k in range(4 * g, 4 * g + 4):
                    end = nc.tensor.matmul(psum[7][0:64, 0:T2], A1[:, k, :], SQ[:, k, :], start=(k == 0),
                                           stop=(k == KC - 1))
            end.then_inc(sem("low_rank_done"), 1)

        def gla_low_rank_vector(dve):
            dve.wait_ge(sem("low_rank_done"), 1)
            dve.wait_ge(sem("low_rank_ones"), 1)
            for d in range(2):
                rows = slice(32 * d, 32 * d + RANK)
                end = nc.vector.tensor_copy(LOWR[rows, :], psum[7][rows, 0:T2])
            end.then_inc(sem("low_rank_ready"), 1)

        def gla_tensor(pe):
            mm, turn = nc.tensor.matmul, nc.tensor.transpose
            pe.wait_ge(bank_free, 4 + 2 * M_WO1)
            pe.wait_ge(sem("low_rank_ready"), 1)
            pe.wait_ge(sem("gla_in"), 5 * 16)

            def gates_and_turns(i, t, first=False):
                if not first:
                    pe.wait_ge(sem("gla_exps"), i * 2 + t)
                if t == 0:
                    pe.wait_ge(sem("gla_w2_staged"), i + 1)
                mm(Z_B[:, :], LOWR[:, TOK * t:TOK * t + TOK], W2H, start=True, stop=True).then_inc(sem("gla_z"), 1)
                pe.wait_ge(sem("gla_staged"), i * 2 + (t + 1))
                for x in range(2):
                    for j in range(2):
                        b = 2 * x + j
                        end = turn(QK_B[:, P * b:P * b + P], QKST[:, x, P * j:P * j + P], IDENT)
                end.then_inc(sem("gla_qk_turned"), 1)

            def gate_sums(i, t):
                pe.wait_ge(sem("gla_loga"), i * 2 + (t + 1))
                for d in range(2):
                    for j in range(2):
                        b = 2 * d + j
                        mm(CUM_B[:, P * b:P * b + P], LOGA[:, P * b:P * b + P], CUM_TAB[d], start=True, stop=True)
                pe.wait_ge(sem("gla_qkt"), i * 2 + (t + 1))
                for d in range(2):
                    end = mm(AFTER_B[:, DK * d:DK * d + DK], AFTER_TAB[d], LOGA[:, DK * d:DK * d + DK],
                             start=True, stop=True)
                end.then_inc(sem("gla_cum"), 1)

            def states(t, second, name):
                for j in range(2):
                    for d in range(2):
                        c = d if not second else 1 - d
                        rows = slice(CHUNK * c, CHUNK * c + CHUNK)
                        at = DK * d + P * j
                        e = mm(KV_B[2 * d + j][:, :], KEND[t][rows, at:at + P], VHEAD[t][rows, :], start=True,
                               stop=True)
                e.then_inc(sem(name), 1)

            def inner(i, t):
                pe.wait_ge(sem("gla_gated"), i * 2 + (t + 1))
                for d in range(2):
                    for j in range(2):
                        at = DK * d + P * j
                        end = mm(ATT_B[:, P * d:P * d + P], KDEC[t][:, at:at + P], QDEC[t][:, at:at + P],
                                 start=(j == 0), stop=(j == 1))
                end.then_inc(sem("gla_att"), 1)
                if t == 1:
                    pe.wait_ge(sem("gla_final"), i + 1)
                states(t, False, "gla_kv")

            def outer(i, t):
                n = i * 2 + (t + 1)
                pe.wait_ge(sem("gla_state"), n)
                if t == 0:
                    states(t, True, "gla_kv2")
                pe.wait_ge(sem("gla_att_ready"), n)
                pe.wait_ge(gla_saved, n)
                mm(O_B[:, :], ATTSUM, VHEAD[t], start=True, stop=False)
                terms = []
                for j in range(2):
                    if t == 1:
                        terms += [(d, d, j, ST0) for d in range(2)]
                    terms += [(1 - d, d, j, ST1) for d in range(2)]
                for x, (c, d, j, st) in enumerate(terms):
                    rows = slice(CHUNK * c, CHUNK * c + CHUNK)
                    at = DK * d + P * j + CHUNK * c
                    end = mm(O_B[rows, :], QDEC[t][:, at:at + CHUNK], st[:, d, j, :], start=False,
                             stop=(x >= len(terms) - 2))
                end.then_inc(sem("gla_o"), 1)

            gates_and_turns(0, 0, True)
            gate_sums(0, 0)

            def head(i, last=False):
                gates_and_turns(i, 1)
                inner(i, 0)
                gate_sums(i, 1)
                outer(i, 0)
                if not last:
                    gates_and_turns(i + 1, 0)
                inner(i, 1)
                if not last:
                    gate_sums(i + 1, 0)
                outer(i, 1)

            with pe.Fori(0, GLA_H - 1) as i:
                head(i)
            head(GLA_H - 1, True)

            for g in range(4):
                pe.wait_ge(sem("gla_out_ready"), g + 1)
                if g >= 2:
                    pe.wait_ge(h_ready, 4 * 4 + g - 1)
                for k in range(4 * g, 4 * g + 4):
                    bank = MAIN[2 * (g % 2) + (k % 4) // 2]
                    for s in range(2):
                        at = T2 * (k % 2) + TOK * s
                        end = turn(bank[:, at:at + TOK], VG[:, s, P * k:P * k + P], IDENT)
                end.then_inc(sem("gla_out_turned"), 1)
            pe.wait_ge(h_ready, 4 * 5)

        def gla_scalar(act):
            actv = nc.scalar.activation

            def gates(i, t, first=False):
                n = i * 2 + (t + 1)
                act.wait_ge(sem("gla_z"), n)
                if not first:
                    act.wait_ge(sem("gla_sig_used"), i * 2 + t)
                actv(EZ, Z_B[:, :], ACT.Abs).then_inc(sem("gla_abs"), 1)
                actv(EG, GG[:, t, ds(i * DV, DV)], ACT.Exp, scale=-1.0)
                act.wait_ge(sem("gla_abs"), n)
                actv(EZ, EZ, ACT.Exp, scale=-1.0).then_inc(sem("gla_absexp"), 1)
                act.wait_ge(sem("gla_absexp"), n)
                actv(EZG, EZG, ACT.Ln, bias=ONEC[:, :]).then_inc(sem("gla_ln"), 1)
                act.wait_ge(sem("gla_qk_turned"), n)
                actv(QKTT[:, 0, :], QK_B[:, 0:DK], ACT.Copy, scale=GLA_SCALE)
                actv(QKTT[:, 1, :], QK_B[:, DK:2 * DK], ACT.Copy).then_inc(sem("gla_qkt"), 1)
                act.wait_ge(sem("gla_ln"), n)
                actv(EG, EG, ACT.Exp, scale=-1.0).then_inc(sem("gla_sig"), 1)

            def decays(i, t):
                act.wait_ge(sem("gla_cum"), i * 2 + (t + 1))
                actv(QDEC[t], CUM_B[:, :], ACT.Exp)
                actv(KDEC[t], CUM_B[:, :], ACT.Exp, scale=-1.0)
                actv(KEND[t], AFTER_B[:, :], ACT.Exp).then_inc(sem("gla_exps"), 1)

            def square_o(i, t):
                act.wait_ge(sem("gla_o"), i * 2 + (t + 1))
                actv(OJUNK, O_B[:, :], ACT.Square, accum_out=OSQ[:, ds(i * 2 + t, 1)]).then_inc(sem("gla_osq"), 1)

            gates(0, 0, True)
            decays(0, 0)

            def head(i, last=False):
                gates(i, 1)
                decays(i, 1)
                square_o(i, 0)
                if not last:
                    gates(i + 1, 0)
                    decays(i + 1, 0)
                square_o(i, 1)

            with act.Fori(0, GLA_H - 1) as i:
                head(i)
            head(GLA_H - 1, True)
            act.wait_ge(sem("gla_osq"), 2 * GLA_H)
            actv(ORS, OSQ, ACT.Sqrt, bias=EPSC[:, :], scale=1.0 / DV).then_inc(sem("gla_ostd"), 1)
            for g in range(4):
                act.wait_ge(sem("gla_out_turned"), g + 1)
                for b in range(2):
                    k = 4 * g + 2 * b
                    end = actv(HM[:, k:k + 2, 0:T2],
                               MAIN[2 * (g % 2) + b][:, :].rearrange("p (c t) -> p c t", c=2), ACT.Copy)
                end.then_inc(sem("gla_hi"), 1)
            act.wait_ge(sem("gla_final_out"), 32 * GLA_H)

        def gla_vector(dve, link):
            ts, tt, stt = nc.vector.tensor_scalar, nc.vector.tensor_tensor, nc.vector.scalar_tensor_tensor
            dve.sem_inc(gla_saved, 1)
            dve.wait_ge(bank_free, 4 + 2 * M_WO1)
            dve.wait_ge(sem("gla_in"), 5 * 16)
            link(nc.vector.memset(W2H, 0.0))

            def stage(i, t, first=False):
                if not first:
                    dve.wait_ge(sem("gla_gated"), i * 2 + t)
                if t == 0:
                    if not first:
                        dve.wait_ge(sem("gla_z"), i * 2)
                    for d in range(2):
                        rows = slice(32 * d, 32 * d + RANK + 1)
                        end = ts(W2H[rows, DK * d:DK * d + DK], W2A[rows, ds(i * DK, DK)], 1.0, None, ALU.mult)
                    end.then_inc(sem("gla_w2_staged"), 1)
                ts(QKST, QKG[:, :, t, ds(i * DK, DK)], 1.0, None, ALU.mult).then_inc(sem("gla_staged"), 1)
                ts(VHEAD[t], VG[:, t, ds(i * DV, DV)], 1.0, None, ALU.mult)

            def log_gates(i, t):
                dve.wait_ge(sem("gla_ln"), i * 2 + (t + 1))
                stt(LOGA, Z_B[:, :], 0.0, EZ, ALU.min, ALU.subtract).then_inc(sem("gla_loga"), 1)

            def gate(i, t):
                n = i * 2 + (t + 1)
                dve.wait_ge(sem("gla_exps"), n)
                for d in range(2):
                    for k in range(2):
                        c = k if d == 0 else 1 - k
                        at = CHUNK * c + (CHUNK - 1 if d == 0 else 0)
                        end = nc.vector.tensor_copy(
                            DECAY[t][:, d, k, :],
                            QDEC[t][:, DK * d:DK * d + DK].rearrange("p (j t) -> p j t", j=2)[:, :, at])
                end.then_inc(sem("gla_decay"), 1)
                both = lambda ap: ap.rearrange("p (d n) -> p d n", d=2)
                tt(both(KDEC[t]), both(KDEC[t]), QKTT[:, 1:2, :].broadcast_to([P, 2, DK]), ALU.mult)
                tt(both(KEND[t]), both(KEND[t]), QKST[:, 1:2, :].broadcast_to([P, 2, DK]), ALU.mult)
                dve.wait_ge(sem("gla_decay"), n)
                tt(both(QDEC[t]), both(QDEC[t]), QKTT[:, 0:1, :].broadcast_to([P, 2, DK]), ALU.mult).then_inc(
                    sem("gla_gated"), 1)

            def mask(i, t):
                n = i * 2 + (t + 1)
                dve.wait_ge(sem("gla_att"), n)
                nc.vector.memset(ATT, 0.0).then_inc(sem("gla_att_zero"), 1)
                dve.wait_ge(sem("gla_att_zero"), n)
                nc.vector.memset(WAITED, 0.0)
                for d in range(2):
                    end = nc.vector.copy_predicated(ATT[:, d, :], CUM_TAB[d].bitcast(u32),
                                                    ATT_B[:, P * d:P * d + P])
                end.then_inc(sem("gla_masked"), 1)
                dve.wait_ge(sem("gla_masked"), n)
                tt(ATTSUM, ATT[:, 0, :], ATT[:, 1, :], ALU.add).then_inc(sem("gla_att_ready"), 1)

            def middle_state(i, t):
                dve.wait_ge(sem("gla_kv"), i * 2 + (t + 1))
                if t == 1:
                    dve.wait_ge(sem("gla_st0_in"), i * 32 + 32)
                for j in range(2):
                    for d in range(2):
                        if t == 0:
                            end = ts(ST1[:, d, j, :], KV_B[2 * d + j][:, :], 1.0, None, ALU.mult)
                        else:
                            end = stt(ST1[:, d, j, :], ST0[:, d, j, :], DECAY[t][:, d, 0, j:j + 1],
                                      KV_B[2 * d + j][:, :], ALU.mult, ALU.add)
                end.then_inc(sem("gla_state"), 1)

            def final_state(i):
                dve.wait_ge(sem("gla_state"), i * 2 + 1)
                dve.wait_ge(sem("gla_kv2"), i + 1)
                dve.wait_ge(final_free, i + 1)
                for d in range(2):
                    for j in range(2):
                        end = stt(FINAL[:, d, j, :], ST1[:, d, j, :], DECAY[0][:, d, 1, j:j + 1],
                                  KV_B[2 * d + j][:, :], ALU.mult, ALU.add)
                end.then_inc(sem("gla_final"), 1)

            def save(i, t):
                dve.wait_ge(sem("gla_osq"), i * 2 + (t + 1))
                nc.vector.memset(WAITED, 0.0)
                ts(VG[:, t, ds(i * DV, DV)], O_B[:, :], 1.0, None, ALU.mult).then_inc(gla_saved, 1)

            stage(0, 0, True)
            log_gates(0, 0)
            gate(0, 0)

            def head(i, last=False):
                stage(i, 1)
                log_gates(i, 1)
                mask(i, 0)
                middle_state(i, 0)
                gate(i, 1)
                final_state(i)
                save(i, 0)
                if not last:
                    stage(i + 1, 0)
                    log_gates(i + 1, 0)
                mask(i, 1)
                middle_state(i, 1)
                if not last:
                    gate(i + 1, 0)
                save(i, 1)

            with dve.Fori(0, GLA_H - 1) as i:
                head(i)
            head(GLA_H - 1, True)
            dve.wait_ge(sem("gla_ostd"), 1)
            link(nc.vector.reciprocal(ORS, ORS))
            dve.wait_ge(sem("gla_gg"), 2 * GLA_H)
            for h in range(GLA_H):
                for t in range(2):
                    cols = slice(DV * h, DV * h + DV)
                    end = stt(VG[:, t, cols], VG[:, t, cols], ORS[:, 2 * h + t:2 * h + t + 1], GG[:, t, cols],
                              ALU.mult, ALU.mult)
                end.then_inc(sem("gla_out_ready"), 1)
            for g in range(4):
                dve.wait_ge(sem("gla_hi"), g + 1)
                for b in range(2):
                    k = 4 * g + 2 * b
                    end = tt(HM[:, k:k + 2, T2:2 * T2],
                             MAIN[2 * (g % 2) + b][:, :].rearrange("p (c t) -> p c t", c=2),
                             HM[:, k:k + 2, 0:T2].bitcast(f32), ALU.subtract)
                end.then_inc(h_ready, 1)

        def gla_pool(pool):
            tt = nc.gpsimd.tensor_tensor
            pool.sem_inc(final_free, 1)
            pool.wait_ge(hid_done, HID_GROUPS * KC + 2)
            pool.dma_start(CB[:, 0:768], t_gla).then_inc(sem("gla_in"), 16)
            nc.gpsimd.memset(CB[0:64, 768:2048], 1.0).then_inc(sem("low_rank_ones"), 1)
            pool.wait_ge(sem("low_rank_ones"), 1)
            for d in range(2):
                pool.dma_start(W2A[32 * d:32 * d + RANK, :], w_a2_gla[0, d]).then_inc(sem("gla_in"), 16)
                pool.dma_start(W2A[32 * d + RANK:32 * d + RANK + 1, :], b_a_gla[0, d:d + 1]).then_inc(
                    sem("gla_in"), 16)
            pool.wait_ge(x_ready, 8)
            nc.gpsimd.memset(A1, 0.0).then_inc(sem("a1_zero"), 1)
            pool.wait_ge(sem("a1_zero"), 1)
            for d in range(2):
                pool.dma_start(A1[:, :, 32 * d:32 * d + RANK],
                               w_a1_gla[0, d].rearrange("(c p) r -> p c r", p=P)).then_inc(sem("a1_in"), 16)
            pool.wait_ge(sem("gla_in"), 5 * 16)
            pool.wait_ge(sem("low_rank_done"), 1)
            pool.wait_ge(bank_free, 4 + 2 * (M_QKV1 + 2 * KEY // UC))
            for x in range(2):
                pairs = QKG[:, x, 1, :].rearrange("p (h b x n) -> p h b x n", h=GLA_H, b=2, x=2)
                for r, (a, tab) in enumerate(((0, COS), (1, SIN), (0, SIN), (1, COS))):
                    for b in range(2):
                        rot = ROT[:, x, r].rearrange("p (h b) n -> p h b n", b=2)
                        end = tt(rot[:, :, b, :], pairs[:, :, b, a, :],
                                 tab[:, b:b + 1, :].broadcast_to([P, GLA_H, DK // 4]), ALU.mult)
            end.then_inc(sem("rot_parts"), 1)
            pool.wait_ge(sem("rot_parts"), 1)
            for x in range(2):
                pairs = QKG[:, x, 1, :].rearrange("p (h x n) -> p h x n", x=2, n=DK // 4)
                tt(pairs[:, :, 0, :], ROT[:, x, 0], ROT[:, x, 1], ALU.subtract)
                end = tt(pairs[:, :, 1, :], ROT[:, x, 2], ROT[:, x, 3], ALU.add)
            end.then_inc(sem("rotated"), 1)

            def load_states(i):
                for d in range(2):
                    pool.dma_start(ST0[:, d, :, :], state_gla[0, 0, d, i].rearrange("(j p) v -> p j v", p=P))                         .then_inc(sem("gla_st0_in"), 16)

            pool.wait_ge(bank_free, 4 + 2 * M_WO1)
            pool.dma_start(GHEAD, g_head_gla[0:1, :].partition_broadcast(P)).then_inc(sem("ghead_in"), 16)
            load_states(0)
            pool.wait_ge(sem("ghead_in"), 16)
            for i in range(GLA_H):
                for t in range(2):
                    n = 2 * i + t + 1
                    g = GG[:, t, DV * i:DV * i + DV]
                    pool.wait_ge(sem("gla_sig"), n)
                    tt(g, g, EG, ALU.mult).then_inc(sem("gla_sig_used"), 1)
                    pool.wait_ge(sem("gla_sig_used"), n)
                    tt(g, g, GHEAD, ALU.mult).then_inc(sem("gla_gg"), 1)
                    if t == 1:
                        pool.wait_ge(sem("gla_final"), i + 1)
                        for d in range(2):
                            pool.dma_start(new_gla[0, 0, d, i].rearrange("(j p) v -> p j v", p=P),
                                           FINAL[:, d, :, :]).then_inc(sem("gla_final_out"), 16)
                        pool.wait_ge(sem("gla_final_out"), i * 32 + 32)
                        pool.sem_inc(final_free, 1)
                    if t == 1 and i + 1 < GLA_H:
                        pool.wait_ge(gla_saved, 2 * i + 3)
                        load_states(i + 1)
            pool.wait_ge(sem("gla_out_turned"), 4)
            nc.gpsimd.memset(SCR[:, 2 * S4:3 * S4], 0.0).then_inc(y_zero, 1)

        block = ctx.enter_context(nc.Block())

        @block.sync
        def _(sp):
            def load_slab(m, w, row, col):
                for u in range(2):
                    sp.wait_ge(lo_done, m * 2 + u + 1)
                    src = w[ds(row + u * UNIT_ROWS, UNIT_ROWS), ds(col, UC)].rearrange("(c p) n -> p c n", p=P)
                    sp.dma_start(RAW[:, u, :].rearrange("p (c n) -> p c n", c=UKC), src).then_inc(raw_in[u], 16)

            def load_ada(a, layer, col):
                for u in range(2):
                    sp.wait_ge(ada0_used if u == 0 else ada_done, a + 1)
                    src = w_ada[layer, u * UNIT_ROWS:(u + 1) * UNIT_ROWS, ds(col, UC)] \
                        .rearrange("(c p) n -> p c n", p=P)
                    sp.dma_start(ADW[:, u, :].rearrange("p (c n) -> p c n", c=UKC), src).then_inc(ada_in[u], 16)

            def stream(m, bodies, w, row, ada, a=0, layer=0, a_first=0):
                with sp.Fori(0, bodies) as i:
                    for s in range(2):
                        load_slab(i * 2 + (m + s), w, row, i * (2 * UC) + s * UC)
                        if s < ada:
                            load_ada(i * ada + (a + s), layer, i * (ada * UC) + (a + s - a_first) * UC)

            wq0 = w_qkv_na[0]
            load_slab(0, wq0, 0, 0)
            with sp.Fori(0, A_QKV0) as i:
                load_ada(i, 0, i * UC)
            load_slab(1, wq0, 0, UC)
            load_ada(A_QKV0, 0, A_QKV0 * UC)
            load_ada(A_QKV0 + 1, 0, (A_QKV0 + 1) * UC)
            with sp.Fori(1, 3 * NB) as i:
                for s in range(2):
                    load_slab(i * 2 + s, wq0, 0, i * (2 * UC) + s * UC)
                    load_ada(i * 2 + (A_QKV0 + s), 0, i * (2 * UC) + (A_QKV0 + s) * UC)
            stream(M_WO0, NB, w_o_na[0], 0, 2, A_WO0, 0, 0)

            def mlp(layer, m, a):
                with sp.Fori(0, HID_GROUPS) as g:
                    for half, w in ((0, w1_mlp[layer]), (1, w2_mlp[layer])):
                        with sp.Fori(0, NB) as i:
                            for s in range(2):
                                mm = g * (4 * NB) + i * 2 + (m + 2 * NB * half + s)
                                if half == 0:
                                    load_slab(mm, w, 0, g * D + i * (2 * UC) + s * UC)
                                else:
                                    load_slab(mm, w, g * D, i * (2 * UC) + s * UC)
                                if s == 0 and a is not None:
                                    aa = g * (2 * NB) + i + NB * half
                                    load_ada(aa + a, 1, aa * UC)

            mlp(0, M_MLP0, A_MLP0)
            stream(M_QKV1, 3 * NB, w_qkvg_gla[0], 0, 1, A_QKV1, 1, A_MLP0)
            stream(M_WO1, NB, w_o_gla[0], 0, 1, A_WO1, 1, A_MLP0)
            mlp(1, M_MLP1, None)
            for q in range(8):
                s, cols = q // 4, slice(512 * (q % 4), 512 * (q % 4) + 512)
                sp.wait_ge(sem("out_staged"), q + 1)
                sp.dma_start((y_prompt, y_sample)[s][0, :, cols], OUTS[:, s, cols]).then_inc(sem("y_out"), 16)
            sp.wait_ge(sem("y_out"), 8 * 16)

        @block.tensor
        def _(pe):
            mm = nc.tensor.matmul
            pe.sem_inc(unit0_used, 2)
            pe.sem_inc(block_done, 4)
            pe.sem_inc(ada0_used, 1)
            pe.sem_inc(ada_done, 1)

            def unit(m, s, u, body):
                pe.wait_ge(lo_done, m * 2 + u + 3)
                slot = 2 * s + u
                hi = WHI[:, slot, :].rearrange("p (c n) -> p c n", c=UKC)
                lo = WLO[:, slot, :].rearrange("p (c n) -> p c n", c=UKC)
                for b in range(2):
                    if u == 0:
                        pe.wait_ge(bank_free, m * 2 + b + 1)
                    bank = MAIN[2 * s + b]
                    for k in range(UKC):
                        first, last = u == 0 and k == 0, u == 1 and k == UKC - 1
                        end = body(bank, hi, lo, b, UKC * u + k, k, first, last)
                    if u == 1:
                        end.then_inc(block_done, 1)
                if u == 0:
                    end.then_inc(unit0_used, 1)

            def features_out(act):
                def body(bank, hi, lo, b, kc, k, first, last):
                    cols = slice(P * b, P * b + P)
                    mm(bank[:, 0:T2], hi[:, k, cols], act[:, kc, 0:T2], start=first, stop=False)
                    mm(bank[:, 0:T2], hi[:, k, cols], act[:, kc, T2:2 * T2], start=False, stop=False)
                    return mm(bank[:, 0:T2], lo[:, k, cols], act[:, kc, 0:T2], start=False, stop=last)
                return body

            def tokens_out(act):
                def body(bank, hi, lo, b, kc, k, first, last):
                    xh = act[:, kc, TOK * b:TOK * b + TOK]
                    xl = act[:, kc, T2 + TOK * b:T2 + TOK * b + TOK]
                    mm(bank[:, 0:UC], xh, hi[:, k, :], start=first, stop=False)
                    mm(bank[:, 0:UC], xh, lo[:, k, :], start=False, stop=False)
                    return mm(bank[:, 0:UC], xl, hi[:, k, :], start=False, stop=last)
                return body

            def ada_rows(a):
                for u in range(2):
                    pe.wait_ge(ada_in[u], a * 16 + 16)
                    w = ADW[:, u, :].rearrange("p (c n) -> p c n", c=UKC)
                    for r in range(2):
                        for j in range(4):
                            k = 4 * r + j
                            end = mm(ROWB[32 * j:32 * j + 32, 0:UC], CS[:, UKC * u + k, :], w[:, k, :],
                                     start=(u == 0 and r == 0), stop=(u == 1 and r == 1))
                    end.then_inc(ada0_used if u == 0 else ada_done, 1)

            def ada_select(a):
                pe.wait_ge(row_ready, a + 1)
                pe.wait_ge(mod_done, a + 1)
                for b in range(2):
                    end = mm(SELB[:, 2 * b:2 * b + 2], MROW[:, P * b:P * b + P], SEL, start=True, stop=True)
                end.then_inc(sel_done, 1)

            def step(m, s, body, ada=None, act_waits=None):
                for u in range(2):
                    if act_waits:
                        act_waits(u)
                    unit(m, s, u, body)
                    if ada is not None:
                        (ada_rows if u == 0 else ada_select)(ada)

            def stream(m, bodies, body, ada, a=0, act_waits=None, start=0):
                with pe.Fori(start, bodies) as i:
                    for s in range(2):
                        step(i * 2 + (m + s), s, body, i * ada + (a + s) if s < ada else None, act_waits)

            def filled(f):
                return lambda u: pe.wait_ge(h_ready, 4 * f + 2 + 2 * u)

            def norm_sum(r):
                for g in range(4):
                    pe.wait_ge(parts, 4 * r + g + 1)
                    end = mm(NORMB[:, 0:T2], ONES[:, :], PART[:, g, :], start=(g == 0), stop=(g == 3))
                end.then_inc(sumsq, 1)

            pe.wait_ge(sem("small_in"), 6 * 16)
            rows = (P, ADA_BLOCKS, ADA_BLOCKS, 2 * KC)
            off = 0
            for a, n in enumerate(rows):
                end = nc.tensor.transpose(psum[7][:, off:off + n], SMALL[0:n, a, :], IDENT[0:n, 0:n])
                off += n
            end.then_inc(sem("small_turned"), 1)
            pe.wait_ge(sem("x_in"), 2 * 16)
            for q in range(8):
                s, c0 = q // 4, 4 * (q % 4)
                if q >= 4:
                    pe.wait_ge(sem("x_copied"), q - 3)
                for j in range(4):
                    end = nc.tensor.transpose(MAIN[q % 4][:, P * j:P * j + P],
                                              XLD[:, s, P * (c0 + j):P * (c0 + j + 1)], IDENT)
                end.then_inc(sem("x_turned"), 1)
            pe.wait_ge(sem("ones_set"), 3)
            pe.wait_ge(sem("cond_ready"), 1)
            with pe.Fori(0, A_QKV0) as i:
                ada_rows(i)
                ada_select(i)

            norm_sum(0)
            with pe.Fori(0, 2 * NB) as i:
                for s in range(2):
                    step(i * 2 + s, s, features_out(HM), i * 2 + (A_QKV0 + s), filled(0))
            stream(M_QKV0 + 4 * NB, NB, tokens_out(HM), 2, A_QKV0 + 4 * NB)
            attention_tensor(pe)
            stream(M_WO0, NB, features_out(HM), 2, A_WO0, filled(1))
            norm_sum(1)
            norm_sum(2)

            def mlp(layer, m, a, f):
                with pe.Fori(0, HID_GROUPS) as g:
                    for half in range(2):
                        with pe.Fori(0, NB) as i:
                            for s in range(2):
                                slab = g * (4 * NB) + i * 2 + (m + 2 * NB * half + s)
                                ada = None
                                if s == 0 and a is not None:
                                    ada = g * (2 * NB) + i + (NB * half + a)
                                if half == 0:
                                    step(slab, s, features_out(HM), ada, filled(f))
                                else:
                                    step(slab, s, features_out(HID), ada,
                                         lambda u, g=g: pe.wait_ge(
                                             hid_done, g * KC + (layer * HID_GROUPS * KC + UKC * (u + 1) + 2)))

            mlp(0, M_MLP0, A_MLP0, 2)
            norm_sum(3)
            norm_sum(4)
            gla_low_rank_tensor(pe)
            stream(M_QKV1, 3 * NB, tokens_out(HM), 1, A_QKV1, filled(3))
            gla_tensor(pe)
            stream(M_WO1, NB, features_out(HM), 1, A_WO1, filled(4))
            norm_sum(5)
            norm_sum(6)
            mlp(1, M_MLP1, None, 5)
            norm_sum(7)
            for q in range(8):
                s, c0 = q // 4, 4 * (q % 4)
                pe.wait_ge(x_ready, 4 * 3 + (q % 4) + 1)
                if q >= 4:
                    pe.wait_ge(sem("out_staged"), q - 3)
                for j in range(4):
                    end = nc.tensor.transpose(MAIN[q % 4][:, P * j:P * j + P],
                                              X[:, c0 + j, TOK * s:TOK * s + TOK], IDENT)
                end.then_inc(sem("out_turned"), 1)

        @block.scalar
        def _(act):
            actv = nc.scalar.activation

            def split_hi(m, s):
                for u in range(2):
                    act.wait_ge(raw_in[u], m * 16 + 16)
                    if u == 0:
                        act.wait_ge(unit0_used, m + 1)
                    else:
                        act.wait_ge(block_done, m * 2 + 2)
                    actv(WHI[:, 2 * s + u, :], RAW[:, u, :], ACT.Copy).then_inc(hi_done, 1)

            def ada_row(a):
                act.wait_ge(ada_done, a + 2)
                actv(MROW[:, :], ROWB[:, 0:UC], ACT.Copy).then_inc(row_ready, 1)

            def square_hidden(k):
                for b in range(2):
                    act.wait_ge(relu_done, k + b + 1)
                    actv(RELU[:, b, :], RELU[:, b, :], ACT.Square).then_inc(square_done, 1)

            def step(m, s, ada=None, hidden=None, prefetch=True):
                if prefetch:
                    split_hi(m + 1, 1 - s)
                if ada is not None:
                    ada_row(ada)
                if hidden is not None:
                    square_hidden(hidden)

            def stream(m, bodies, ada, a=0):
                with act.Fori(0, bodies) as i:
                    for s in range(2):
                        step(i * 2 + (m + s), s, i * ada + (a + s) if s < ada else None)

            def norm_squares(r, src):
                for g in range(4):
                    if r in (2, 4, 6):
                        act.wait_ge(x_ready, 4 * (r // 2 - 1) + g + 1)
                    actv(SQ[:, 4 * g:4 * g + 4, :], src[:, 4 * g:4 * g + 4, :], ACT.Square).then_inc(squares, 1)
                act.wait_ge(sumsq, r + 1)
                actv(STD, NORMB[:, 0:T2], ACT.Sqrt, bias=EPSC[:, :], scale=1.0 / D).then_inc(std_ready, 1)

            def modulate(f, layer, j):
                shift = ADA_BLOCKS * layer + KC * j
                for g in range(4):
                    act.wait_ge(xn_ready, 4 * f + g + 1)
                    for k in range(4 * g, 4 * g + 4):
                        for s in range(2):
                            t = slice(TOK * s, TOK * s + TOK)
                            end = actv(SQ[:, k, t], SQ[:, k, t], ACT.Identity,
                                       bias=MODT[:, shift + k, s:s + 1], scale=GAIN[:, k, s:s + 1])
                    end.then_inc(mod_x, 1)
                    act.wait_ge(mod_x, 4 * f + g + 1)
                    actv(HM[:, 4 * g:4 * g + 4, 0:T2], SQ[:, 4 * g:4 * g + 4, :], ACT.Copy).then_inc(hm_hi, 1)

            act.dma_start(BASE[:, :], t_base).then_inc(sem("small_in"), 16)
            act.dma_start(SMALL[:, 0, :], norm_g.rearrange("l j (c p) -> (l j c) p", p=P)).then_inc(
                sem("small_in"), 16)
            for layer in range(2):
                act.dma_start(SMALL[0:ADA_BLOCKS, 1 + layer, :],
                              b_ada[layer].rearrange("(c p) -> c p", p=P)).then_inc(sem("small_in"), 16)
            act.dma_start(SMALL[0:KC, 3, :], c_ctx.rearrange("(c p) -> c p", p=P)).then_inc(sem("small_in"), 16)
            act.dma_start(SMALL[KC:2 * KC, 3, :], c[0].rearrange("(c p) -> c p", p=P)).then_inc(
                sem("small_in"), 16)
            act.wait_ge(sem("ones_set"), 3)
            split_hi(0, 0)
            act.wait_ge(sem("small_turned"), 1)
            actv(NGT[:, :], psum[7][:, 0:P], ACT.Copy).then_inc(sem("gains_ready"), 1)
            actv(BT[:, :], psum[7][:, P:P + 2 * ADA_BLOCKS], ACT.Copy).then_inc(sem("biases_ready"), 1)
            actv(CC, psum[7][:, P + 2 * ADA_BLOCKS:P + 2 * ADA_BLOCKS + 2 * KC], ACT.Copy).then_inc(
                sem("cond_copied"), 1)
            act.wait_ge(sem("cond_copied"), 1)
            actv(CE, CC, ACT.Exp, scale=-1.0).then_inc(sem("cond_exp"), 1)
            for q in range(8):
                s, c0 = q // 4, 4 * (q % 4)
                act.wait_ge(sem("x_turned"), q + 1)
                actv(X[:, c0:c0 + 4, TOK * s:TOK * s + TOK],
                     MAIN[q % 4][:, :].rearrange("p (c t) -> p c t", c=4), ACT.Copy).then_inc(sem("x_copied"), 1)
            act.wait_ge(sem("x_copied"), 8)
            with act.Fori(0, A_QKV0) as i:
                ada_row(i)

            norm_squares(0, X)
            modulate(0, 0, 0)
            stream(M_QKV0, 3 * NB, 2, A_QKV0)
            attention_scalar(act)
            stream(M_WO0, NB, 2, A_WO0)
            act.wait_ge(bank_free, 4 + 2 * M_MLP0)
            norm_squares(1, Y)
            norm_squares(2, X)
            modulate(1, 0, 3)

            def mlp(layer, m, a, last):
                with act.Fori(0, HID_GROUPS - (1 if last else 0)) as g:
                    mlp_group(g, layer, m, a)
                if last:
                    mlp_group(HID_GROUPS - 1, layer, m, a, last)

            def mlp_group(g, layer, m, a, last=False):
                for half in range(2):
                    peel = last and half == 1
                    with act.Fori(0, NB - (1 if peel else 0)) as i:
                        mlp_body(g, i, half, layer, m, a)
                    if peel:
                        mlp_body(g, NB - 1, half, layer, m, a, True)

            def mlp_body(g, i, half, layer, m, a, end=False):
                for s in range(2):
                    slab = g * (4 * NB) + i * 2 + (m + 2 * NB * half + s)
                    ada = None
                    if s == 0 and a is not None:
                        ada = g * (2 * NB) + i + (NB * half + a)
                    hidden = None
                    if half == 0:
                        hidden = g * KC + i * 4 + (layer * HID_GROUPS * KC + 2 * s)
                    step(slab, s, ada, hidden, prefetch=not (end and s == 1))

            mlp(0, M_MLP0, A_MLP0, False)
            act.wait_ge(bank_free, 4 + 2 * M_QKV1)
            norm_squares(3, Y)
            norm_squares(4, X)
            modulate(2, 1, 0)
            stream(M_QKV1, 3 * NB, 1, A_QKV1)
            gla_scalar(act)
            stream(M_WO1, NB, 1, A_WO1)
            act.wait_ge(bank_free, 4 + 2 * M_MLP1)
            norm_squares(5, Y)
            norm_squares(6, X)
            modulate(3, 1, 3)
            mlp(1, M_MLP1, None, True)
            act.wait_ge(bank_free, 4 + 2 * M_END)
            norm_squares(7, Y)
            for q in range(8):
                act.wait_ge(sem("out_turned"), q + 1)
                actv(OUTS[:, q // 4, 512 * (q % 4):512 * (q % 4) + 512], MAIN[q % 4][:, :], ACT.Copy).then_inc(
                    sem("out_staged"), 1)

        @block.vector
        def _(dve):
            tt = nc.vector.tensor_tensor
            ts = nc.vector.tensor_scalar
            own = sem("dve_own")
            count = [0]

            def link(ins):
                count[0] += 1
                ins.then_inc(own, 1)
                dve.wait_ge(own, count[0])

            dve.sem_inc(lo_done, 2)
            dve.sem_inc(bank_free, 4)
            dve.sem_inc(mod_done, 1)
            dve.sem_inc(hid_done, 2)

            def split_lo(m, s):
                for u in range(2):
                    dve.wait_ge(hi_done, m * 2 + u + 1)
                    tt(WLO[:, 2 * s + u, :], RAW[:, u, :], WHI[:, 2 * s + u, :].bitcast(f32),
                       ALU.subtract).then_inc(lo_done, 1)

            def ada_mod(a):
                dve.wait_ge(sel_done, a + 1)
                tt(MODT[:, ds(a * 2, 2), :], SELB[:, 0:4].rearrange("p (b s) -> p b s", b=2),
                   BT[:, ds(a * 2, 2)].unsqueeze(2).broadcast_to([P, 2, 2]),
                   ALU.add).then_inc(mod_done, 1)

            def evacuate(m, s, how):
                for b in range(2):
                    dve.wait_ge(block_done, m * 2 + b + 5)
                    how(MAIN[2 * s + b][:, 0:T2], b).then_inc(bank_free, 1)

            def step(m, s, how, ada=None, after=None, prefetch=True):
                if prefetch:
                    split_lo(m + 1, 1 - s)
                evacuate(m, s, how)
                if ada is not None:
                    ada_mod(ada)
                if after:
                    after()

            def stream(m, bodies, how, ada, a=0):
                with dve.Fori(0, bodies) as i:
                    for s in range(2):
                        step(i * 2 + (m + s), s, how(i, s), i * ada + (a + s) if s < ada else None)

            def to_blocks(dst, first):
                return lambda i, s: lambda src, b: ts(
                    dst[:, ds(i * 4 + (first + 2 * s + b), 1), :].rearrange("p o t -> p (o t)"), src, 1.0, None,
                    ALU.mult)

            def to_tokens(dst, col):
                return lambda i, s: lambda src, b: ts(
                    dst[:, b, ds(i * (2 * UC) + (col + s * UC), UC)], src, 1.0, None, ALU.mult)

            def add_to_y(i, s):
                def how(src, b):
                    y = Y[:, ds(i * 4 + (2 * s + b), 1), :].rearrange("p o t -> p (o t)")
                    return tt(y, src, y, ALU.add)
                return how

            def norm_rstd(r):
                for g in range(4):
                    dve.wait_ge(squares, 4 * r + g + 1)
                    nc.vector.tensor_reduce(PART[:, g, :], SQ[:, 4 * g:4 * g + 4, :].rearrange("p c t -> p t c"),
                                            AX.X, ALU.add).then_inc(parts, 1)
                dve.wait_ge(std_ready, r + 1)
                link(nc.vector.reciprocal(RSTD, STD))

            def gain(layer, norm, mod, plus):
                first = ADA_BLOCKS * layer + KC * mod
                ng = NGT[:, (4 * layer + norm) * KC:(4 * layer + norm + 1) * KC]
                link(ts(GAIN[:, :, :], MODT[:, first:first + KC, :], plus, None, ALU.add))
                link(tt(GAIN[:, :, :], GAIN[:, :, :],
                        ng.unsqueeze(2).broadcast_to([P, KC, 2]), ALU.mult))

            def residual(r, layer, norm, mod):
                gain(layer, norm, mod, 0.0)
                norm_rstd(r)
                for g in range(4):
                    q = slice(4 * g, 4 * g + 4)
                    link(tt(SQ[:, q, :], Y[:, q, :], RSTD.unsqueeze(1).broadcast_to([P, 4, T2]), ALU.mult))
                    for k in range(4 * g, 4 * g + 4):
                        for s in range(2):
                            t = slice(TOK * s, TOK * s + TOK)
                            end = nc.vector.scalar_tensor_tensor(X[:, k, t], SQ[:, k, t], GAIN[:, k, s:s + 1],
                                                                 X[:, k, t], ALU.mult, ALU.add)
                    end.then_inc(x_ready, 1)

            def pre_norm(r, f, layer, norm, mod, residual_no=None):
                if residual_no is not None:
                    dve.wait_ge(x_ready, 4 * residual_no + 4)
                gain(layer, norm, mod, 1.0)
                norm_rstd(r)
                for g in range(4):
                    q = slice(4 * g, 4 * g + 4)
                    tt(SQ[:, q, :], X[:, q, :], RSTD.unsqueeze(1).broadcast_to([P, 4, T2]), ALU.mult).then_inc(xn_ready, 1)
                for g in range(4):
                    q = slice(4 * g, 4 * g + 4)
                    dve.wait_ge(hm_hi, 4 * f + g + 1)
                    tt(HM[:, q, T2:2 * T2], SQ[:, q, :], HM[:, q, 0:T2].bitcast(f32), ALU.subtract).then_inc(
                        h_ready, 1)

            split_lo(0, 0)
            dve.wait_ge(sem("cond_exp"), 1)
            link(nc.vector.memset(CS[:, :, :], 0.0))
            link(ts(CE, CE, 1.0, None, ALU.add))
            link(nc.vector.reciprocal(CE, CE))
            tt(CS[:, :, 0:2], CC.rearrange("p (s c) -> p c s", s=2), CE.rearrange("p (s c) -> p c s", s=2),
               ALU.mult).then_inc(sem("cond_ready"), 1)
            dve.wait_ge(sem("biases_ready"), 1)
            with dve.Fori(0, A_QKV0) as i:
                ada_mod(i)
            dve.wait_ge(mod_done, A_QKV0 + 1)

            pre_norm(0, 0, 0, 0, 1)
            dve.wait_ge(sem("bias_ready"), 1)
            stream(M_QKV0, 2 * NB, to_blocks(QK, 0), 2, A_QKV0)
            stream(M_QKV0 + 4 * NB, NB, to_tokens(VN, 0), 2, A_QKV0 + 4 * NB)
            attention_vector(dve, link)
            dve.wait_ge(y_zero, 1)
            stream(M_WO0, NB, add_to_y, 2, A_WO0)
            dve.wait_ge(bank_free, 4 + 2 * M_MLP0)
            dve.wait_ge(mod_done, A_MLP0 + 1)
            residual(1, 0, 1, 2)
            pre_norm(2, 1 + 0, 0, 2, 4, 0)

            def mlp(layer, m, a, last):
                with dve.Fori(0, HID_GROUPS - (1 if last else 0)) as g:
                    mlp_group(g, layer, m, a)
                if last:
                    mlp_group(HID_GROUPS - 1, layer, m, a, last)

            def mlp_group(g, layer, m, a, last=False):
                for half in range(2):
                    peel = last and half == 1
                    with dve.Fori(0, NB - (1 if peel else 0)) as i:
                        mlp_body(g, i, half, layer, m, a)
                    if peel:
                        mlp_body(g, NB - 1, half, layer, m, a, True)

            def mlp_body(g, i, half, layer, m, a, end=False):
                for s in range(2):
                    slab = g * (4 * NB) + i * 2 + (m + 2 * NB * half + s)
                    ada = None
                    if s == 0 and a is not None:
                        ada = g * (2 * NB) + i + (NB * half + a)
                    if half == 1:
                        step(slab, s, add_to_y(i, s), ada, prefetch=not (end and s == 1))
                        continue
                    k = g * KC + i * 4 + (layer * HID_GROUPS * KC + 2 * s)
                    hid = [HID[:, ds(i * 4 + (2 * s + b), 1), :].rearrange("p o t -> p (o t)") for b in range(2)]
                    split_lo(slab + 1, 1 - s)
                    for b in range(2):
                        dve.wait_ge(hid_done, k + b + 1)
                        dve.wait_ge(block_done, slab * 2 + b + 5)
                        ts(RELU[:, b, :], MAIN[2 * s + b][:, 0:T2], 0.0, None, ALU.max).then_inc(relu_done, 1)
                    if ada is not None:
                        ada_mod(ada)
                    for b in range(2):
                        dve.wait_ge(square_done, k + b + 1)
                        ts(hid[b][:, 0:T2], RELU[:, b, :], 1.0, None, ALU.mult).then_inc(bank_free, 1)
                    for b in range(2):
                        dve.wait_ge(bank_free, slab * 2 + b + 5)
                        tt(hid[b][:, T2:2 * T2], RELU[:, b, :], hid[b][:, 0:T2].bitcast(f32),
                           ALU.subtract).then_inc(hid_done, 1)

            dve.wait_ge(y_zero, 2)
            mlp(0, M_MLP0, A_MLP0, False)
            dve.wait_ge(bank_free, 4 + 2 * M_QKV1)
            dve.wait_ge(mod_done, A_QKV1 + 1)
            residual(3, 0, 3, 5)
            pre_norm(4, 2, 1, 0, 1, 1)
            gla_low_rank_vector(dve)
            m, a = M_QKV1, A_QKV1
            for dst, n in ((QG, KEY), (KG, KEY), (VG, D), (GG, D)):
                bodies = n // (2 * UC)
                if dst is GG:
                    dve.wait_ge(sem("rotated"), 1)
                stream(m, bodies, to_tokens(dst, 0), 1, a)
                m, a = m + 2 * bodies, a + bodies
            gla_vector(dve, link)
            dve.wait_ge(y_zero, 3)
            stream(M_WO1, NB, add_to_y, 1, A_WO1)
            dve.wait_ge(bank_free, 4 + 2 * M_MLP1)
            dve.wait_ge(mod_done, A_END + 1)
            residual(5, 1, 1, 2)
            pre_norm(6, 3, 1, 2, 4, 2)
            dve.wait_ge(y_zero, 4)
            mlp(1, M_MLP1, None, True)
            dve.wait_ge(bank_free, 4 + 2 * M_END)
            residual(7, 1, 3, 5)

        @block.gpsimd
        def _(pool):
            for s, x in enumerate((x_prompt, x_sample)):
                pool.dma_start(XLD[:, s, :], x[0]).then_inc(sem("x_in"), 16)
            nc.gpsimd.memset(ONES[:, :], 1.0).then_inc(sem("ones_set"), 1)
            nc.gpsimd.memset(EPSC[:, :], EPS).then_inc(sem("ones_set"), 1)
            nc.gpsimd.memset(ONEC[:, :], 1.0).then_inc(sem("ones_set"), 1)
            nc.gpsimd.memset(RPT[0:N_DR * NA_H, :], 0.0).then_inc(sem("pad_zero"), 1)
            pool.wait_ge(sem("pad_zero"), 1)
            pool.dma_start(WINM, t_window).then_inc(sem("window_in"), 16)
            mid = GRID_W - 1
            for r in range(N_DR):
                pool.dma_start(RPT[NA_H * r:NA_H * r + NA_H, mid - WIN_COLS + 1:mid + WIN_COLS],
                               rpb_na[0, :, 6 + r, :]).then_inc(sem("rpb_in"), 16)
            pool.wait_ge(sem("rpb_in"), 16 * N_DR)
            pool.dma_start(rpb_pad.rearrange("r h q w -> (r h) q w"),
                           RPT[0:N_DR * NA_H, 0:LINE].unsqueeze(1).broadcast_to([N_DR * NA_H, GRID_W, LINE])).then_inc(
                sem("rpb_padded"), 16)
            pool.wait_ge(sem("rpb_padded"), 16)
            for qr in range(2):
                for kr in range(2):
                    src = bass.AP(rpb_pad.tensor, (1 - qr + kr) * NA_H * GRID_W * LINE + mid,
                                  [[LINE - 1, GRID_W], [GRID_W * LINE, NA_H], [1, GRID_W]])
                    pool.dma_start(BIAS[GRID_W * qr:GRID_W * qr + GRID_W, :, GRID_W * kr:GRID_W * kr + GRID_W],
                                   src).then_inc(sem("bias_in"), 16)
            pool.wait_ge(sem("bias_in"), 64)
            pool.wait_ge(sem("window_in"), 16)
            nc.gpsimd.tensor_tensor(BIAS, BIAS, WINM.unsqueeze(1).broadcast_to([P, NA_H, P]), ALU.add).then_inc(
                sem("bias_ready"), 1)
            attention_pool(pool)
            pool.wait_ge(x_ready, 4)
            nc.gpsimd.memset(SCR[:, 2 * S4:3 * S4], 0.0).then_inc(y_zero, 1)
            gla_pool(pool)
            pool.wait_ge(x_ready, 12)
            nc.gpsimd.memset(SCR[:, 2 * S4:3 * S4], 0.0).then_inc(y_zero, 1)
            pool.wait_ge(sem("newk_out"), 16)
            pool.wait_ge(sem("newv_out"), 16)
            pool.wait_ge(sem("gla_final_out"), 32 * GLA_H)


_INS = ['x_prompt', 'x_sample', 'cache_na_k', 'cache_na_v', 'state_gla', 'c', 'c_ctx', 'w_ada', 'b_ada', 'norm_g',
        'w_qkv_na', 'w_o_na', 'rpb_na', 'w_qkvg_gla', 'w_a1_gla', 'w_a2_gla', 'b_a_gla', 'g_head_gla', 'w_o_gla',
        'w1_mlp', 'w2_mlp']
_OUTS = [(1, TOK, D), (1, TOK, D), (1, 1, NA_H, TOK, DH), (1, 1, NA_H, TOK, DH), (1, 1, 2, GLA_H, DK, DV)]


def kernel(**inputs):
    import numpy as _np
    import concourse.bacc as _bacc
    from concourse import mybir as _mybir
    from concourse.bass_utils import run_bass_kernel_spmd as _run

    nc = _bacc.Bacc("TRN2", target_bir_lowering=False, num_devices=1)
    arrays, args = {}, []
    named = [(n, _np.ascontiguousarray(inputs[n])) for n in _INS]
    named += list(zip(("t_base", "t_window", "t_gla"), shape_tables()))
    for name, a in named:
        arrays[f"in_{name}"] = a
        args.append(nc.dram_tensor(f"in_{name}", a.shape, _mybir.dt.from_np(a.dtype), kind="ExternalInput").ap())
    for i, shape in enumerate(_OUTS):
        args.append(nc.dram_tensor(f"out_{i}", shape, _mybir.dt.float32, kind="ExternalOutput").ap())
    build_program(nc, *args)
    r = _run(nc, [arrays], core_ids=[0])
    return tuple(r.results[0][f"out_{i}"] for i in range(len(_OUTS)))
```

```python
import concourse.bass as bass
from concourse import mybir
from contextlib import ExitStack
import numpy as np

P = 128
D = 2048
KC = D // P
TOK = 128
T2 = 2 * TOK
FF = 4 * D
HID_GROUPS = FF // D
ADA = 6 * D
UNIT_ROWS = 1024
UKC = UNIT_ROWS // P
UC = 256
UNIT = UKC * UC
NA_H = 16
DH = 128
GRID_W = 64
WIN_COLS = 16
LINE = 2 * GRID_W - 1
N_DR = 3
GLA_H = 4
DK = 256
DV = 512
KEY = GLA_H * DK
CHUNK = 64
RANK = 16
EPS = 1e-6
NA_SCALE = DH ** -0.5
GLA_SCALE = DK ** -0.5
GATE_NORM = 16.0
NEG = -1e30
ADA_BLOCKS = ADA // P


def shape_tables():
    ident = np.eye(P, dtype=np.float32)
    sel = np.zeros((P, 2), np.float32)
    for j in range(4):
        sel[32 * j, 0] = 1.0
        sel[32 * j + 1, 1] = 1.0
    c = np.arange(P) % GRID_W
    start = np.clip(c - WIN_COLS // 2, 0, GRID_W - WIN_COLS)
    inside = (c[None, :] >= start[:, None]) & (c[None, :] < start[:, None] + WIN_COLS)
    window = np.where(inside, 0.0, NEG).astype(np.float32)
    s, t = np.arange(P)[:, None], np.arange(P)[None, :]
    same = (s // CHUNK) == (t // CHUNK)
    upto = [same & (s <= t), same & (s >= t)]
    after = [same & (s > t), same & (s < t)]
    gates = [m.astype(np.float32) / np.float32(GATE_NORM) for m in upto + after]
    n = DK // 4
    freqs = np.float32(10000.0) ** (-np.arange(n, dtype=np.float32) / np.float32(n))
    pos = np.arange(TOK)
    ang = np.concatenate([(pos // GRID_W).astype(np.float32)[:, None] * freqs[None],
                          (pos % GRID_W).astype(np.float32)[:, None] * freqs[None]], axis=1)
    base = np.concatenate([ident, sel], axis=1)
    gla = np.concatenate(gates + [np.cos(ang).astype(np.float32), np.sin(ang).astype(np.float32)], axis=1)
    return base, window, gla


def build_program(nc, x_prompt, x_sample, cache_na_k, cache_na_v, state_gla, c, c_ctx, w_ada, b_ada, norm_g,
                  w_qkv_na, w_o_na, rpb_na, w_qkvg_gla, w_a1_gla, w_a2_gla, b_a_gla, g_head_gla, w_o_gla,
                  w1_mlp, w2_mlp, t_base, t_window, t_gla,
                  y_prompt, y_sample, new_na_k, new_na_v, new_gla):
    f32 = mybir.dt.float32
    f32r = mybir.dt.float32r
    u32 = mybir.dt.uint32
    ALU = mybir.AluOpType
    ACT = mybir.ActivationFunctionType
    AX = mybir.AxisListType
    ds = bass.ds

    ctx = ExitStack()
    with ctx:
        def sb(name, shape, dt=f32):
            return ctx.enter_context(nc.sbuf_tensor(name, shape, dt))

        sems = {}

        def sem(name):
            if name not in sems:
                sems[name] = ctx.enter_context(nc.semaphore(name))
            return sems[name]

        with nc.sbuf_tensor("HID", [P, KC, 2 * T2], f32r) as HID:
            pass
        SCR = sb("SCR", [P, 3 * KC * T2])
        with nc.sbuf_tensor("HM", [P, KC, 2 * T2], f32r) as HM:
            pass
        TMP = sb("TMP", [P, 2 * KC * T2])
        X = sb("X", [P, KC, T2])
        RAW = sb("RAW", [P, 2, UNIT])
        with nc.sbuf_tensor("GLA_A", [P, 4, UNIT], f32) as GLA_A:
            pass
        WHI = sb("WHI", [P, 4, UNIT], f32r)
        with nc.sbuf_tensor("GLA_B", [P, 4, UNIT], f32) as GLA_B:
            pass
        WLO = sb("WLO", [P, 4, UNIT], f32r)
        ADW = sb("ADW", [P, 2, UNIT])
        CB = sb("CB", [P, 2048])
        BASE = sb("BASE", [P, P + 2])
        ONES = sb("ONES", [P, P])
        MODT = sb("MODT", [P, 2 * ADA_BLOCKS, 2])
        BT = sb("BT", [P, 2 * ADA_BLOCKS])
        NGT = sb("NGT", [P, P])
        CS = sb("CS", [P, KC, 32])
        MROW = sb("MROW", [P, UC])
        GAIN = sb("GAIN", [P, KC, 2])
        WINM = sb("WINM", [P, P])
        EPSC = sb("EPSC", [P, 1])
        ONEC = sb("ONEC", [P, 1])

        IDENT = BASE[:, 0:P]
        SEL = BASE[:, P:P + 2]
        S4 = KC * T2
        SQ = SCR[:, 0:S4].rearrange("p (c t) -> p c t", c=KC)
        STD = SCR[:, S4 + 4 * T2:S4 + 5 * T2]
        RSTD = SCR[:, S4 + 5 * T2:S4 + 6 * T2]
        Y = SCR[:, 2 * S4:3 * S4].rearrange("p (c t) -> p c t", c=KC)
        XLD = SCR[:, 0:S4].rearrange("p (s n) -> p s n", s=2)
        OUTS = XLD
        SMALL = SCR[:, S4 + 8 * T2:S4 + 8 * T2 + 4 * P].rearrange("p (a n) -> p a n", a=4)
        CE = SCR[:, S4 + 10 * T2:S4 + 10 * T2 + 32]
        CC = SCR[:, S4 + 11 * T2:S4 + 11 * T2 + 32]
        RPT = CB[:, 0:P]
        BIAS = CB[:, :].rearrange("p (h k) -> p h k", h=NA_H)
        RELU = CB[:, 0:2 * T2].rearrange("p (b t) -> p b t", b=2)
        QK = SCR[:, 0:2 * S4].rearrange("p (h t) -> p h t", h=2 * NA_H)
        VN = SCR[:, 2 * S4:3 * S4].rearrange("p (s n) -> p s n", s=2)

        psum = [ctx.enter_context(nc.psum_tensor(f"PS{i}", [P, 512], f32)) for i in range(8)]
        rpb_pad = nc.dram_tensor("rpb_pad", [N_DR, NA_H, GRID_W, LINE], f32, kind="Internal").ap()

        FIRST = [ADW[:, :, :], GLA_A[:, 2:4, :], GLA_B[:, 2:4, :],
                 SCR[:, 2 * S4:3 * S4].rearrange("p (u n) -> p u n", u=2)]

        M_QKV0 = 0
        M_WO0 = M_QKV0 + 3 * D // UC
        M_MLP0 = M_WO0 + D // UC
        MLP_SLABS = 2 * HID_GROUPS * D // UC
        M_QKV1 = M_MLP0 + MLP_SLABS
        M_WO1 = M_QKV1 + 3 * D // UC
        M_MLP1 = M_WO1 + D // UC
        M_END = M_MLP1 + MLP_SLABS
        NB = D // UC // 2
        A_QKV0 = 2 * D // UC
        A_ATT = A_QKV0 + 3 * NB
        A_WO0 = A_ATT + NA_H
        A_MLP0 = A_WO0 + NB
        A_QKV1 = A_MLP0 + 2 * HID_GROUPS * NB
        A_WO1 = A_QKV1 + 3 * NB
        A_END = A_WO1 + NB
        assert A_END == 2 * ADA // UC

        raw_in = [sem("raw_in0"), sem("raw_in1")]
        hi_done = sem("hi_done")
        lo_done = sem("lo_done")
        unit0_used = sem("unit0_used")
        block_done = sem("block_done")
        bank_free = sem("bank_free")
        ada_in = [sem("ada_in0"), sem("ada_in1")]
        first_in = [sem(f"first_in{p}") for p in range(4)]
        att_ada_in = [sem("att_ada_in0"), sem("att_ada_in1")]
        ada0_used = sem("ada0_used")
        ada_done = sem("ada_done")
        row_ready = sem("row_ready")
        sel_done = sem("sel_done")
        mod_done = sem("mod_done")
        relu_done = sem("relu_done")
        square_done = sem("square_done")
        hid_hi = sem("hid_hi")
        hid_done = sem("hid_done")
        h_ready = sem("h_ready")
        squares = sem("squares")
        sumsq = sem("sumsq")
        std_ready = sem("std_ready")
        x_ready = sem("x_ready")
        xn_ready = sem("xn_ready")
        mod_x = sem("mod_x")
        mod_xs = sem("mod_xs")
        hm_hi = sem("hm_hi")
        y_zero = sem("y_zero")

        MAIN = psum[0:4]
        ROWB = psum[4]
        SELB = psum[5]
        NORMB = psum[6]

        Y_SUM = [SCR[:, S4:S4 + 2 * T2], TMP[:, 0:2 * T2]]
        Y_SQ = [SCR[:, S4 + 2 * T2:S4 + 4 * T2], TMP[:, 2 * T2:4 * T2]]
        Y_SLABS = D // UC
        y_squared, y_gained = sem("y_squared"), sem("y_gained")
        y_summed = sem("y_summed")

        PAIRS = NA_H // 2
        W = 2 * DH
        QS = TMP[:, 0:2 * T2].rearrange("p (h t) -> p h t", h=2)
        KS = TMP[:, 512:512 + 2 * T2].rearrange("p (h t) -> p h t", h=2)
        VS = TMP[:, 1024:1024 + 2 * W].rearrange("p (s n) -> p s n", s=2)
        KCACHE = TMP[:, 1536:1536 + W]
        VCACHE = TMP[:, 1792:1792 + W]
        KCT = TMP[:, 2048:2048 + W]
        PROB = [TMP[:, 2304 + 384 * p:2304 + 384 * p + 3 * P] for p in range(2)]
        PROBT = [TMP[:, 3072 + 384 * p:3072 + 384 * p + 3 * P] for p in range(2)]
        MAXES, NEGMAX, ROWSUM, RECIP = (TMP[:, 3840 + 4 * x:3844 + 4 * x] for x in range(4))
        NEWK = TMP[:, 4096:4096 + D]
        SCORE_B, TURN_B, OUT_B, PROBT_B = psum[0:2], psum[2], psum[3], psum[6:8]
        KCACHES = GLA_B[:, 2, :]
        VCACHES = GLA_B[:, 3, :]
        k_turned = sem("k_turned")
        pair_done = sem("pair_done")
        o_copied = sem("o_copied")

        def attention_tensor(pe, ada_rows, ada_select):
            mm, turn = nc.tensor.matmul, nc.tensor.transpose
            pe.sem_inc(k_turned, 1)
            pe.sem_inc(pair_done, 1)
            pe.wait_ge(bank_free, 4 + 2 * M_WO0)

            def scores(i, first=False):
                pe.wait_ge(sem("qk_staged"), i + 1)
                pe.wait_ge(sem("kcache_staged"), i + 1)
                if not first:
                    pe.wait_ge(sem("newk_staged"), i)
                for p in range(2):
                    turn(TURN_B[:, P * p:P * p + P], KCACHE[:, DH * p:DH * p + DH], IDENT)
                for p in range(2):
                    end = turn(TURN_B[:, W + P * p:W + P * p + P], KS[:, p, 0:TOK], IDENT)
                end.then_inc(k_turned, 1)
                for p in range(2):
                    for st in range(2):
                        t = slice(TOK * st, TOK * st + TOK)
                        mm(SCORE_B[p][:, t], QS[:, p, t], KS[:, p, t], start=True, stop=True)
                pe.wait_ge(sem("kct_ready"), i + 1)
                for p in range(2):
                    mm(SCORE_B[p][:, 2 * P:3 * P], QS[:, p, TOK:T2], KCT[:, P * p:P * p + P], start=True,
                       stop=True).then_inc(sem("scores_done"), 1)

            def turn_probs(i):
                for p in range(2):
                    pe.wait_ge(sem("probs_ready"), i * 2 + (p + 1))
                    for b in range(3):
                        end = turn(PROBT_B[p][:, P * b:P * b + P], PROB[p][:, P * b:P * b + P], IDENT)
                    end.then_inc(sem("probs_turned"), 1)

            def outputs(i):
                pe.wait_ge(sem("v_staged"), i + 1)
                pe.wait_ge(o_copied, i + 1)
                for p in range(2):
                    pe.wait_ge(sem("probt_ready"), i * 2 + (p + 1))
                    o = OUT_B[:, T2 * p:T2 * p + T2]
                    d = slice(DH * p, DH * p + DH)
                    mm(o[:, 0:TOK], VS[:, 0, d], PROBT[p][:, 0:P], start=True, stop=True)
                    mm(o[:, TOK:T2], VS[:, 1, d], PROBT[p][:, P:2 * P], start=True, stop=False)
                    end = mm(o[:, TOK:T2], VCACHE[:, d], PROBT[p][:, 2 * P:3 * P], start=False, stop=True)
                end.then_inc(pair_done, 1)

            def pair(i, last=False):
                ada = i * 2 + A_ATT
                ada_rows(ada, (att_ada_in[0], i, 0))
                turn_probs(i)
                ada_select(ada)
                if not last:
                    scores(i + 1)
                ada_rows(ada + 1, (att_ada_in[1], i, 1))
                outputs(i)
                ada_select(ada + 1)

            scores(0, True)
            with pe.Fori(0, PAIRS - 1) as i:
                pair(i)
            pair(PAIRS - 1, True)

        def attention_scalar(act, ada_row):
            actv = nc.scalar.activation

            def turned_k(i):
                act.wait_ge(k_turned, i + 2)
                actv(KCT, TURN_B[:, 0:W], ACT.Copy).then_inc(sem("kct_ready"), 1)
                actv(NEWK[:, ds(i * W, W)], TURN_B[:, W:2 * W], ACT.Copy).then_inc(sem("newk_staged"), 1)

            def pair(i, last=False):
                act.wait_ge(sem("negmax_ready"), i + 1)
                for p in range(2):
                    actv(PROB[p][:, 0:P], SCORE_B[p][:, 0:P], ACT.Exp, bias=NEGMAX[:, 2 * p:2 * p + 1],
                         accum_out=ROWSUM[:, 2 * p:2 * p + 1])
                    end = actv(PROB[p][:, P:3 * P], SCORE_B[p][:, P:3 * P], ACT.Exp,
                               bias=NEGMAX[:, 2 * p + 1:2 * p + 2], accum_out=ROWSUM[:, 2 * p + 1:2 * p + 2])
                end.then_inc(sem("exp_done"), 1)
                ada_row(i * 2 + A_ATT)
                for p in range(2):
                    act.wait_ge(sem("probs_turned"), i * 2 + (p + 1))
                    actv(PROBT[p], PROBT_B[p][:, 0:3 * P], ACT.Copy).then_inc(sem("probt_ready"), 1)
                if not last:
                    turned_k(i + 1)
                ada_row(i * 2 + (A_ATT + 1))

            turned_k(0)
            with act.Fori(0, PAIRS - 1) as i:
                pair(i)
            pair(PAIRS - 1, True)
            act.wait_ge(o_copied, 1 + PAIRS)
            act.wait_ge(sem("newk_out"), 16)
            for g in range(4):
                actv(HM[:, 4 * g:4 * g + 4, 0:T2], QK[:, 4 * g:4 * g + 4, :], ACT.Copy).then_inc(sem("o_hi"), 1)

        def attention_vector(dve, link, ada_mod):
            ts, tt = nc.vector.tensor_scalar, nc.vector.tensor_tensor
            dve.sem_inc(o_copied, 1)
            dve.wait_ge(bank_free, 4 + 2 * M_WO0)

            def stage(i, first=False):
                if not first:
                    dve.wait_ge(sem("scores_done"), i * 2)
                ts(QS, QK[:, ds(i * 2, 2), :], NA_SCALE, None, ALU.mult)
                ts(KS, QK[:, ds(i * 2 + NA_H, 2), :], 1.0, None, ALU.mult).then_inc(sem("qk_staged"), 1)

            def pair(i, last=False):
                for p in range(2):
                    dve.wait_ge(sem("scores_done"), i * 2 + (p + 1))
                    lat = SCORE_B[p][:, P:2 * P]
                    tt(lat, lat, BIAS[:, ds(i * 2 + p, 1), :].rearrange("p o t -> p (o t)"), ALU.add).then_inc(
                        sem("biased"), 1)
                    nc.vector.reduce_max(MAXES[:, 2 * p:2 * p + 1], SCORE_B[p][:, 0:P], AX.X)
                for p in range(2):
                    dve.wait_ge(sem("biased"), i * 2 + (p + 1))
                    end = nc.vector.reduce_max(MAXES[:, 2 * p + 1:2 * p + 2], SCORE_B[p][:, P:3 * P], AX.X)
                end.then_inc(sem("maxed"), 1)
                dve.wait_ge(sem("maxed"), i + 1)
                ts(NEGMAX, MAXES, -1.0, None, ALU.mult).then_inc(sem("negmax_ready"), 1)
                if not last:
                    stage(i + 1)
                dve.wait_ge(sem("exp_done"), i + 1)
                nc.vector.reciprocal(RECIP, ROWSUM).then_inc(sem("recip_done"), 1)
                dve.wait_ge(sem("recip_done"), i + 1)
                for p in range(2):
                    ts(PROB[p][:, 0:P], PROB[p][:, 0:P], RECIP[:, 2 * p:2 * p + 1], None, ALU.mult)
                    ts(PROB[p][:, P:3 * P], PROB[p][:, P:3 * P], RECIP[:, 2 * p + 1:2 * p + 2], None,
                       ALU.mult).then_inc(sem("probs_ready"), 1)
                ada_mod(i * 2 + A_ATT)
                dve.wait_ge(pair_done, i + 2)
                ts(QK[:, ds(i * 2, 2), :], OUT_B[:, :].rearrange("p (h t) -> p h t", h=2), 1.0, None,
                   ALU.mult).then_inc(o_copied, 1)
                ada_mod(i * 2 + (A_ATT + 1))

            stage(0, True)
            with dve.Fori(0, PAIRS - 1) as i:
                pair(i)
            pair(PAIRS - 1, True)
            for g in range(4):
                q = slice(4 * g, 4 * g + 4)
                dve.wait_ge(sem("o_hi"), g + 1)
                tt(HM[:, q, T2:2 * T2], QK[:, q, :], HM[:, q, 0:T2].bitcast(f32), ALU.subtract).then_inc(h_ready, 1)

        def attention_pool(pool):
            pool.wait_ge(bank_free, 4 + 2 * M_WO0)
            pool.dma_start(new_na_v[0, 0].rearrange("h t d -> t h d"),
                           VN[:, 0, :].rearrange("p (h d) -> p h d", h=NA_H)).then_inc(sem("newv_out"), 16)
            with pool.Fori(0, PAIRS) as i:
                pool.wait_ge(sem("kcache_in"), 16)
                pool.wait_ge(k_turned, i + 1)
                nc.gpsimd.tensor_copy(KCACHE, KCACHES[:, ds(i * W, W)]).then_inc(sem("kcache_staged"), 1)
                pool.wait_ge(sem("vcache_in"), 16)
                pool.wait_ge(pair_done, i + 1)
                nc.gpsimd.tensor_copy(VCACHE, VCACHES[:, ds(i * W, W)])
                nc.gpsimd.tensor_copy(VS, VN[:, :, ds(i * W, W)]).then_inc(sem("v_staged"), 1)
            pool.wait_ge(sem("newk_staged"), PAIRS)
            pool.dma_start(new_na_k[0, 0].rearrange("h t d -> t h d"),
                           NEWK.rearrange("p (h d) -> p h d", h=NA_H)).then_inc(sem("newk_out"), 16)
            pool.wait_ge(pair_done, 1 + PAIRS)
            pool.wait_ge(sem("newv_out"), 16)
            nc.gpsimd.memset(SCR[:, 2 * S4:3 * S4], 0.0).then_inc(y_zero, 1)

        QG = SCR[:, 0:S4 // 2].rearrange("p (s n) -> p s n", s=2)
        KG = SCR[:, S4 // 2:S4].rearrange("p (s n) -> p s n", s=2)
        QKG = SCR[:, 0:S4].rearrange("p (x s n) -> p x s n", x=2, s=2)
        VG = SCR[:, S4:2 * S4].rearrange("p (s n) -> p s n", s=2)
        GG = SCR[:, 2 * S4:3 * S4].rearrange("p (s n) -> p s n", s=2)
        A1 = SCR[:, 2 * S4:2 * S4 + KC * 64].rearrange("p (c n) -> p c n", c=KC)
        ROT = SCR[:, 2 * S4:3 * S4].rearrange("p (x r h n) -> p x r h n", x=2, r=4, h=2 * GLA_H)
        CUM_TAB = [CB[:, 0:P], CB[:, P:2 * P]]
        AFTER_TAB = [CB[:, 2 * P:3 * P], CB[:, 3 * P:4 * P]]
        COS = CB[:, 4 * P:5 * P].rearrange("p (h n) -> p h n", h=2)
        SIN = CB[:, 5 * P:6 * P].rearrange("p (h n) -> p h n", h=2)
        W2A = CB[0:64, 768:768 + KEY]
        LOWR = CB[0:64, 1792:2048]
        FREE_A = GLA_A[:, 2:4, :].rearrange("p a n -> p (a n)")
        FREE_B = GLA_B[:, 2:4, :].rearrange("p a n -> p (a n)")
        ST0 = FREE_A[:, 0:2048].rearrange("p (d j v) -> p d j v", d=2, j=2)
        FINAL = FREE_A[:, 2048:4096].rearrange("p (d j v) -> p d j v", d=2, j=2)
        ST1 = FREE_B[:, 0:2048].rearrange("p (d j v) -> p d j v", d=2, j=2)
        GHEAD = FREE_B[:, 2048:2560]
        W2H = FREE_B[0:64, 2560:2560 + 2 * DK]
        OSQ = FREE_B[:, 3072:3080]
        ORS = FREE_B[:, 3080:3088]
        DECAY = [FREE_B[:, 3088 + 8 * t:3096 + 8 * t].rearrange("p (d n j) -> p d n j", d=2, n=2) for t in range(2)]
        WAITED = FREE_B[:, 3104:3105]
        QKST = TMP[:, 0:512].rearrange("p (x n) -> p x n", x=2)
        QKTT = TMP[:, 512:1024].rearrange("p (x n) -> p x n", x=2)
        LOGA = TMP[:, 1024:1536]
        EZ, EG = TMP[:, 1536:2048], TMP[:, 2048:2560]
        EZG = TMP[:, 1536:2560]

        def by_stream(at):
            return [TMP[:, at + 512 * t:at + 512 * t + 512] for t in range(2)]

        QDEC, KDEC, KEND, VHEAD = by_stream(2560), by_stream(3584), by_stream(4608), by_stream(5632)
        ATT = TMP[:, 6656:6912].rearrange("p (d n) -> p d n", d=2)
        ATTSUM = TMP[:, 6912:7040]
        OJUNK = TMP[:, 7040:7552]
        ATT_B, O_B, CUM_B, AFTER_B = psum[0], psum[1], psum[2], psum[3]
        Z_B, QK_B = CUM_B, AFTER_B
        KV_B = psum[4:8]
        gla_saved = sem("gla_saved")
        final_free = sem("final_free")

        def gla_low_rank_tensor(pe):
            pe.wait_ge(sem("a1_in"), 32)
            for g in range(4):
                pe.wait_ge(mod_x, 4 * 2 + g + 1)
                pe.wait_ge(mod_xs, 4 * 2 + g + 1)
                for k in range(4 * g, 4 * g + 4):
                    end = nc.tensor.matmul(psum[7][0:64, 0:T2], A1[:, k, :], SQ[:, k, :], start=(k == 0),
                                           stop=(k == KC - 1))
            end.then_inc(sem("low_rank_done"), 1)

        def gla_low_rank_vector(dve):
            dve.wait_ge(sem("low_rank_done"), 1)
            dve.wait_ge(sem("low_rank_ones"), 1)
            for d in range(2):
                rows = slice(32 * d, 32 * d + RANK)
                end = nc.vector.tensor_copy(LOWR[rows, :], psum[7][rows, 0:T2])
            end.then_inc(sem("low_rank_ready"), 1)

        def gla_tensor(pe):
            mm, turn = nc.tensor.matmul, nc.tensor.transpose
            pe.wait_ge(bank_free, 4 + 2 * M_WO1)
            pe.wait_ge(sem("low_rank_ready"), 1)
            pe.wait_ge(sem("gla_in"), 5 * 16)

            def gates(i, t, first=False):
                if not first:
                    pe.wait_ge(sem("gla_exps"), i * 2 + t)
                if t == 0:
                    pe.wait_ge(sem("gla_w2_staged"), i + 1)
                mm(Z_B[:, :], LOWR[:, TOK * t:TOK * t + TOK], W2H, start=True, stop=True).then_inc(sem("gla_z"), 1)

            def turns(i, t):
                pe.wait_ge(sem("gla_staged"), i * 2 + (t + 1))
                for x in range(2):
                    for j in range(2):
                        b = 2 * x + j
                        end = turn(QK_B[:, P * b:P * b + P], QKST[:, x, P * j:P * j + P], IDENT)
                end.then_inc(sem("gla_qk_turned"), 1)

            def gate_sums(i, t):
                pe.wait_ge(sem("gla_loga"), i * 2 + (t + 1))
                for d in range(2):
                    for j in range(2):
                        b = 2 * d + j
                        mm(CUM_B[:, P * b:P * b + P], LOGA[:, P * b:P * b + P], CUM_TAB[d], start=True, stop=True)
                pe.wait_ge(sem("gla_qkt"), i * 2 + (t + 1))
                for d in range(2):
                    end = mm(AFTER_B[:, DK * d:DK * d + DK], AFTER_TAB[d], LOGA[:, DK * d:DK * d + DK],
                             start=True, stop=True)
                end.then_inc(sem("gla_cum"), 1)

            def states(t, second, name):
                for j in range(2):
                    for d in range(2):
                        c = d if not second else 1 - d
                        rows = slice(CHUNK * c, CHUNK * c + CHUNK)
                        at = DK * d + P * j
                        e = mm(KV_B[2 * d + j][:, :], KEND[t][rows, at:at + P], VHEAD[t][rows, :], start=True,
                               stop=True)
                e.then_inc(sem(name), 1)

            def inner(i, t):
                pe.wait_ge(sem("gla_gated"), i * 2 + (t + 1))
                for d in range(2):
                    for j in range(2):
                        at = DK * d + P * j
                        end = mm(ATT_B[:, P * d:P * d + P], KDEC[t][:, at:at + P], QDEC[t][:, at:at + P],
                                 start=(j == 0), stop=(j == 1))
                end.then_inc(sem("gla_att"), 1)
                if t == 1:
                    pe.wait_ge(sem("gla_final"), i + 1)
                states(t, False, "gla_kv")

            def from_states(t, terms, last):
                for x, (c, d, j, st) in enumerate(terms):
                    rows = slice(CHUNK * c, CHUNK * c + CHUNK)
                    at = DK * d + P * j + CHUNK * c
                    end = mm(O_B[rows, :], QDEC[t][:, at:at + CHUNK], st[:, d, j, :], start=False,
                             stop=last and x >= len(terms) - 2)
                return end

            def outer_first(i, t):
                n = i * 2 + (t + 1)
                pe.wait_ge(sem("gla_att_ready"), n)
                pe.wait_ge(gla_saved, n)
                mm(O_B[:, :], ATTSUM, VHEAD[t], start=True, stop=False)
                if t == 1:
                    pe.wait_ge(sem("gla_st0_in"), i * 32 + 32)
                    from_states(t, [(d, d, j, ST0) for j in range(2) for d in range(2)], False)
                else:
                    pe.wait_ge(sem("gla_state"), n)
                    states(t, True, "gla_kv2")

            def outer_last(i, t):
                pe.wait_ge(sem("gla_state"), i * 2 + (t + 1))
                from_states(t, [(1 - d, d, j, ST1) for j in range(2) for d in range(2)], True).then_inc(
                    sem("gla_o"), 1)

            gates(0, 0, True)
            turns(0, 0)
            gate_sums(0, 0)
            gates(0, 1)

            def head(i, last=False):
                turns(i, 1)
                inner(i, 0)
                gate_sums(i, 1)
                outer_first(i, 0)
                if not last:
                    gates(i + 1, 0)
                outer_last(i, 0)
                if not last:
                    turns(i + 1, 0)
                inner(i, 1)
                if not last:
                    gate_sums(i + 1, 0)
                outer_first(i, 1)
                if not last:
                    gates(i + 1, 1)
                outer_last(i, 1)

            with pe.Fori(0, GLA_H - 1) as i:
                head(i)
            head(GLA_H - 1, True)

            for g in range(4):
                pe.wait_ge(sem("gla_out_ready"), g + 1)
                if g >= 2:
                    pe.wait_ge(h_ready, 4 * 4 + g - 1)
                for k in range(4 * g, 4 * g + 4):
                    bank = MAIN[2 * (g % 2) + (k % 4) // 2]
                    for s in range(2):
                        at = T2 * (k % 2) + TOK * s
                        end = turn(bank[:, at:at + TOK], VG[:, s, P * k:P * k + P], IDENT)
                end.then_inc(sem("gla_out_turned"), 1)
            pe.wait_ge(h_ready, 4 * 5)

        def gla_scalar(act):
            actv = nc.scalar.activation

            def gates(i, t, first=False):
                n = i * 2 + (t + 1)
                act.wait_ge(sem("gla_z"), n)
                if not first:
                    act.wait_ge(sem("gla_sig_used"), i * 2 + t)
                actv(EZ, Z_B[:, :], ACT.Abs).then_inc(sem("gla_abs"), 1)
                actv(EG, GG[:, t, ds(i * DV, DV)], ACT.Exp, scale=-1.0)
                act.wait_ge(sem("gla_abs"), n)
                actv(EZ, EZ, ACT.Exp, scale=-1.0).then_inc(sem("gla_absexp"), 1)
                act.wait_ge(sem("gla_absexp"), n)
                actv(EZG, EZG, ACT.Ln, bias=ONEC[:, :]).then_inc(sem("gla_ln"), 1)
                act.wait_ge(sem("gla_ln"), n)
                actv(EG, EG, ACT.Exp, scale=-1.0).then_inc(sem("gla_sig"), 1)

            def turned_qk(i, t):
                act.wait_ge(sem("gla_qk_turned"), i * 2 + (t + 1))
                actv(QKTT[:, 0, :], QK_B[:, 0:DK], ACT.Copy, scale=GLA_SCALE)
                actv(QKTT[:, 1, :], QK_B[:, DK:2 * DK], ACT.Copy).then_inc(sem("gla_qkt"), 1)

            def decays(i, t):
                act.wait_ge(sem("gla_cum"), i * 2 + (t + 1))
                actv(QDEC[t], CUM_B[:, :], ACT.Exp)
                actv(KDEC[t], CUM_B[:, :], ACT.Exp, scale=-1.0)
                actv(KEND[t], AFTER_B[:, :], ACT.Exp).then_inc(sem("gla_exps"), 1)

            def square_o(i, t):
                act.wait_ge(sem("gla_o"), i * 2 + (t + 1))
                actv(OJUNK, O_B[:, :], ACT.Square, accum_out=OSQ[:, ds(i * 2 + t, 1)]).then_inc(sem("gla_osq"), 1)

            gates(0, 0, True)
            turned_qk(0, 0)
            decays(0, 0)
            gates(0, 1)

            def head(i, last=False):
                turned_qk(i, 1)
                decays(i, 1)
                if not last:
                    gates(i + 1, 0)
                square_o(i, 0)
                if not last:
                    turned_qk(i + 1, 0)
                    decays(i + 1, 0)
                    gates(i + 1, 1)
                square_o(i, 1)

            with act.Fori(0, GLA_H - 1) as i:
                head(i)
            head(GLA_H - 1, True)
            act.wait_ge(sem("gla_osq"), 2 * GLA_H)
            actv(ORS, OSQ, ACT.Sqrt, bias=EPSC[:, :], scale=1.0 / DV).then_inc(sem("gla_ostd"), 1)
            for g in range(4):
                act.wait_ge(sem("gla_out_turned"), g + 1)
                for b in range(2):
                    k = 4 * g + 2 * b
                    end = actv(HM[:, k:k + 2, 0:T2],
                               MAIN[2 * (g % 2) + b][:, :].rearrange("p (c t) -> p c t", c=2), ACT.Copy)
                end.then_inc(sem("gla_hi"), 1)
            act.wait_ge(sem("gla_final_out"), 32 * GLA_H)

        def gla_vector(dve, link):
            ts, tt, stt = nc.vector.tensor_scalar, nc.vector.tensor_tensor, nc.vector.scalar_tensor_tensor
            dve.sem_inc(gla_saved, 1)
            dve.wait_ge(bank_free, 4 + 2 * M_WO1)
            dve.wait_ge(sem("gla_in"), 5 * 16)
            link(nc.vector.memset(W2H, 0.0))

            def stage(i, t, first=False):
                if t == 0:
                    if not first:
                        dve.wait_ge(sem("gla_z"), i * 2)
                    for d in range(2):
                        rows = slice(32 * d, 32 * d + RANK + 1)
                        end = ts(W2H[rows, DK * d:DK * d + DK], W2A[rows, ds(i * DK, DK)], 1.0, None, ALU.mult)
                    end.then_inc(sem("gla_w2_staged"), 1)
                if not first:
                    dve.wait_ge(sem("gla_gated"), i * 2 + t)
                ts(QKST, QKG[:, :, t, ds(i * DK, DK)], 1.0, None, ALU.mult).then_inc(sem("gla_staged"), 1)

            def stage_v(i, t):
                ts(VHEAD[t], VG[:, t, ds(i * DV, DV)], 1.0, None, ALU.mult)

            def log_gates(i, t):
                dve.wait_ge(sem("gla_ln"), i * 2 + (t + 1))
                stt(LOGA, Z_B[:, :], 0.0, EZ, ALU.min, ALU.subtract).then_inc(sem("gla_loga"), 1)

            def gate(i, t):
                n = i * 2 + (t + 1)
                dve.wait_ge(sem("gla_exps"), n)
                for d in range(2):
                    for k in range(2):
                        c = k if d == 0 else 1 - k
                        at = CHUNK * c + (CHUNK - 1 if d == 0 else 0)
                        end = nc.vector.tensor_copy(
                            DECAY[t][:, d, k, :],
                            QDEC[t][:, DK * d:DK * d + DK].rearrange("p (j t) -> p j t", j=2)[:, :, at])
                end.then_inc(sem("gla_decay"), 1)
                both = lambda ap: ap.rearrange("p (d n) -> p d n", d=2)
                tt(both(KDEC[t]), both(KDEC[t]), QKTT[:, 1:2, :].broadcast_to([P, 2, DK]), ALU.mult)
                tt(both(KEND[t]), both(KEND[t]), QKST[:, 1:2, :].broadcast_to([P, 2, DK]), ALU.mult)
                dve.wait_ge(sem("gla_decay"), n)
                tt(both(QDEC[t]), both(QDEC[t]), QKTT[:, 0:1, :].broadcast_to([P, 2, DK]), ALU.mult).then_inc(
                    sem("gla_gated"), 1)

            def mask(i, t):
                n = i * 2 + (t + 1)
                dve.wait_ge(sem("gla_att"), n)
                nc.vector.memset(ATT, 0.0).then_inc(sem("gla_att_zero"), 1)
                dve.wait_ge(sem("gla_att_zero"), n)
                nc.vector.memset(WAITED, 0.0)
                for d in range(2):
                    end = nc.vector.copy_predicated(ATT[:, d, :], CUM_TAB[d].bitcast(u32),
                                                    ATT_B[:, P * d:P * d + P])
                end.then_inc(sem("gla_masked"), 1)
                dve.wait_ge(sem("gla_masked"), n)
                tt(ATTSUM, ATT[:, 0, :], ATT[:, 1, :], ALU.add).then_inc(sem("gla_att_ready"), 1)

            def middle_state(i, t):
                dve.wait_ge(sem("gla_kv"), i * 2 + (t + 1))
                if t == 1:
                    dve.wait_ge(sem("gla_st0_in"), i * 32 + 32)
                for j in range(2):
                    for d in range(2):
                        if t == 0:
                            end = ts(ST1[:, d, j, :], KV_B[2 * d + j][:, :], 1.0, None, ALU.mult)
                        else:
                            end = stt(ST1[:, d, j, :], ST0[:, d, j, :], DECAY[t][:, d, 0, j:j + 1],
                                      KV_B[2 * d + j][:, :], ALU.mult, ALU.add)
                end.then_inc(sem("gla_state"), 1)

            def final_state(i):
                dve.wait_ge(sem("gla_state"), i * 2 + 1)
                dve.wait_ge(sem("gla_kv2"), i + 1)
                dve.wait_ge(final_free, i + 1)
                for d in range(2):
                    for j in range(2):
                        end = stt(FINAL[:, d, j, :], ST1[:, d, j, :], DECAY[0][:, d, 1, j:j + 1],
                                  KV_B[2 * d + j][:, :], ALU.mult, ALU.add)
                end.then_inc(sem("gla_final"), 1)

            def save(i, t):
                dve.wait_ge(sem("gla_osq"), i * 2 + (t + 1))
                nc.vector.memset(WAITED, 0.0)
                ts(VG[:, t, ds(i * DV, DV)], O_B[:, :], 1.0, None, ALU.mult).then_inc(gla_saved, 1)

            stage(0, 0, True)
            stage_v(0, 0)
            log_gates(0, 0)
            gate(0, 0)
            stage(0, 1)
            stage_v(0, 1)

            def head(i, last=False):
                mask(i, 0)
                log_gates(i, 1)
                middle_state(i, 0)
                gate(i, 1)
                if not last:
                    stage(i + 1, 0)
                final_state(i)
                save(i, 0)
                if not last:
                    stage_v(i + 1, 0)
                mask(i, 1)
                if not last:
                    log_gates(i + 1, 0)
                middle_state(i, 1)
                if not last:
                    gate(i + 1, 0)
                    stage(i + 1, 1)
                save(i, 1)
                if not last:
                    stage_v(i + 1, 1)

            with dve.Fori(0, GLA_H - 1) as i:
                head(i)
            head(GLA_H - 1, True)
            dve.wait_ge(sem("gla_ostd"), 1)
            link(nc.vector.reciprocal(ORS, ORS))
            dve.wait_ge(sem("gla_gg"), 2 * GLA_H)
            for h in range(GLA_H):
                for t in range(2):
                    cols = slice(DV * h, DV * h + DV)
                    end = stt(VG[:, t, cols], VG[:, t, cols], ORS[:, 2 * h + t:2 * h + t + 1], GG[:, t, cols],
                              ALU.mult, ALU.mult)
                end.then_inc(sem("gla_out_ready"), 1)
            for g in range(4):
                dve.wait_ge(sem("gla_hi"), g + 1)
                for b in range(2):
                    k = 4 * g + 2 * b
                    end = tt(HM[:, k:k + 2, T2:2 * T2],
                             MAIN[2 * (g % 2) + b][:, :].rearrange("p (c t) -> p c t", c=2),
                             HM[:, k:k + 2, 0:T2].bitcast(f32), ALU.subtract)
                end.then_inc(h_ready, 1)

        def gla_pool(pool):
            tt = nc.gpsimd.tensor_tensor
            pool.sem_inc(final_free, 1)
            pool.wait_ge(hid_done, HID_GROUPS * KC + 2)
            pool.dma_start(CB[:, 0:768], t_gla).then_inc(sem("gla_in"), 16)
            nc.gpsimd.memset(CB[0:64, 768:2048], 1.0).then_inc(sem("low_rank_ones"), 1)
            pool.wait_ge(sem("low_rank_ones"), 1)
            for d in range(2):
                pool.dma_start(W2A[32 * d:32 * d + RANK, :], w_a2_gla[0, d]).then_inc(sem("gla_in"), 16)
                pool.dma_start(W2A[32 * d + RANK:32 * d + RANK + 1, :], b_a_gla[0, d:d + 1]).then_inc(
                    sem("gla_in"), 16)
            pool.wait_ge(x_ready, 8)
            nc.gpsimd.memset(A1, 0.0).then_inc(sem("a1_zero"), 1)
            pool.wait_ge(sem("a1_zero"), 1)
            for d in range(2):
                pool.dma_start(A1[:, :, 32 * d:32 * d + RANK],
                               w_a1_gla[0, d].rearrange("(c p) r -> p c r", p=P)).then_inc(sem("a1_in"), 16)
            pool.wait_ge(sem("gla_in"), 5 * 16)
            pool.wait_ge(sem("low_rank_done"), 1)
            pool.wait_ge(bank_free, 4 + 2 * (M_QKV1 + 2 * KEY // UC))
            for x in range(2):
                pairs = QKG[:, x, 1, :].rearrange("p (h b x n) -> p h b x n", h=GLA_H, b=2, x=2)
                for r, (a, tab) in enumerate(((0, COS), (1, SIN), (0, SIN), (1, COS))):
                    for b in range(2):
                        rot = ROT[:, x, r].rearrange("p (h b) n -> p h b n", b=2)
                        end = tt(rot[:, :, b, :], pairs[:, :, b, a, :],
                                 tab[:, b:b + 1, :].broadcast_to([P, GLA_H, DK // 4]), ALU.mult)
            end.then_inc(sem("rot_parts"), 1)
            pool.wait_ge(sem("rot_parts"), 1)
            for x in range(2):
                pairs = QKG[:, x, 1, :].rearrange("p (h x n) -> p h x n", x=2, n=DK // 4)
                tt(pairs[:, :, 0, :], ROT[:, x, 0], ROT[:, x, 1], ALU.subtract)
                end = tt(pairs[:, :, 1, :], ROT[:, x, 2], ROT[:, x, 3], ALU.add)
            end.then_inc(sem("rotated"), 1)

            def load_states(i):
                for d in range(2):
                    pool.dma_start(ST0[:, d, :, :], state_gla[0, 0, d, i].rearrange("(j p) v -> p j v", p=P))                         .then_inc(sem("gla_st0_in"), 16)

            pool.wait_ge(bank_free, 4 + 2 * M_WO1)
            pool.dma_start(GHEAD, g_head_gla[0:1, :].partition_broadcast(P)).then_inc(sem("ghead_in"), 16)
            load_states(0)
            pool.wait_ge(sem("ghead_in"), 16)
            for i in range(GLA_H):
                for t in range(2):
                    n = 2 * i + t + 1
                    g = GG[:, t, DV * i:DV * i + DV]
                    pool.wait_ge(sem("gla_sig"), n)
                    tt(g, g, EG, ALU.mult).then_inc(sem("gla_sig_used"), 1)
                    pool.wait_ge(sem("gla_sig_used"), n)
                    tt(g, g, GHEAD, ALU.mult).then_inc(sem("gla_gg"), 1)
                    if t == 0 and i:
                        pool.wait_ge(gla_saved, 2 * i + 1)
                        load_states(i)
                    if t == 1:
                        pool.wait_ge(sem("gla_final"), i + 1)
                        for d in range(2):
                            pool.dma_start(new_gla[0, 0, d, i].rearrange("(j p) v -> p j v", p=P),
                                           FINAL[:, d, :, :]).then_inc(sem("gla_final_out"), 16)
                        pool.wait_ge(sem("gla_final_out"), i * 32 + 32)
                        pool.sem_inc(final_free, 1)
            pool.wait_ge(sem("gla_out_turned"), 4)
            nc.gpsimd.memset(SCR[:, 2 * S4:3 * S4], 0.0).then_inc(y_zero, 1)

        block = ctx.enter_context(nc.Block())

        @block.sync
        def _(sp):
            def load_slab(m, w, row, col):
                for u in range(2):
                    sp.wait_ge(lo_done, m * 2 + u + 1)
                    src = w[ds(row + u * UNIT_ROWS, UNIT_ROWS), ds(col, UC)].rearrange("(c p) n -> p c n", p=P)
                    sp.dma_start(RAW[:, u, :].rearrange("p (c n) -> p c n", c=UKC), src).then_inc(raw_in[u], 16)

            def load_ada(a, layer, col):
                for u in range(2):
                    sp.wait_ge(ada0_used if u == 0 else ada_done, a + 1)
                    src = w_ada[layer, u * UNIT_ROWS:(u + 1) * UNIT_ROWS, ds(col, UC)] \
                        .rearrange("(c p) n -> p c n", p=P)
                    sp.dma_start(ADW[:, u, :].rearrange("p (c n) -> p c n", c=UKC), src).then_inc(ada_in[u], 16)

            def stream(m, bodies, w, row, ada, a=0, layer=0, a_first=0):
                with sp.Fori(0, bodies) as i:
                    for s in range(2):
                        load_slab(i * 2 + (m + s), w, row, i * (2 * UC) + s * UC)
                        if s < ada:
                            load_ada(i * ada + (a + s), layer, i * (ada * UC) + (a + s - a_first) * UC)

            wq0 = w_qkv_na[0]

            def load_first(i, p):
                for u in range(2):
                    src = w_ada[0, u * UNIT_ROWS:(u + 1) * UNIT_ROWS, ds(i * (4 * UC) + p * UC, UC)] \
                        .rearrange("(c p) n -> p c n", p=P)
                    sp.dma_start(FIRST[p][:, u, :].rearrange("p (c n) -> p c n", c=UKC), src).then_inc(
                        first_in[p], 16)

            sp.dma_start(BASE[:, :], t_base).then_inc(sem("small_in"), 16)
            sp.dma_start(SMALL[:, 0, :], norm_g.rearrange("l j (c p) -> (l j c) p", p=P)).then_inc(
                sem("small_in"), 16)
            for layer in range(2):
                sp.dma_start(SMALL[0:ADA_BLOCKS, 1 + layer, :],
                              b_ada[layer].rearrange("(c p) -> c p", p=P)).then_inc(sem("small_in"), 16)
            sp.dma_start(SMALL[0:KC, 3, :], c_ctx.rearrange("(c p) -> c p", p=P)).then_inc(sem("small_in"), 16)
            sp.dma_start(SMALL[KC:2 * KC, 3, :], c[0].rearrange("(c p) -> c p", p=P)).then_inc(
                sem("small_in"), 16)
            for s, x in enumerate((x_prompt, x_sample)):
                sp.dma_start(XLD[:, s, :], x[0]).then_inc(sem("x_in"), 16)
            for p in range(4):
                load_first(0, p)
            load_slab(0, wq0, 0, 0)
            with sp.Fori(1, A_QKV0 // 4) as i:
                for p in range(4):
                    sp.wait_ge(ada_done, i * 4 + (p - 2))
                    load_first(i, p)
            load_slab(1, wq0, 0, UC)
            load_ada(A_QKV0, 0, A_QKV0 * UC)
            with sp.Fori(1, 3 * NB) as i:
                for s in range(2):
                    load_slab(i * 2 + s, wq0, 0, i * (2 * UC) + s * UC)
                    if s == 0:
                        load_ada(i + A_QKV0, 0, i * UC + A_QKV0 * UC)
            load_slab(M_WO0, w_o_na[0], 0, 0)
            def load_att_ada(i, x):
                for u in range(2):
                    src = w_ada[0, u * UNIT_ROWS:(u + 1) * UNIT_ROWS, ds(i * (2 * UC) + (A_ATT + x) * UC, UC)] \
                        .rearrange("(c p) n -> p c n", p=P)
                    sp.dma_start(FIRST[x][:, u, :].rearrange("p (c n) -> p c n", c=UKC), src).then_inc(
                        att_ada_in[x], 16)

            sp.wait_ge(ada_done, A_ATT + 1)
            load_att_ada(0, 0)
            sp.wait_ge(bank_free, 4 + 2 * M_WO0)
            for all_heads, src, name in ((KCACHES, cache_na_k, "kcache_in"), (VCACHES, cache_na_v, "vcache_in")):
                sp.dma_start(all_heads.rearrange("p (h d) -> p h d", h=NA_H),
                             src[0, 0].rearrange("h t d -> t h d")).then_inc(sem(name), 16)
            load_att_ada(0, 1)
            with sp.Fori(1, PAIRS) as i:
                for x in range(2):
                    sp.wait_ge(ada_done, i * 2 + (A_ATT + x))
                    load_att_ada(i, x)
            load_ada(A_WO0, 0, A_WO0 * UC)
            load_slab(M_WO0 + 1, w_o_na[0], 0, UC)
            with sp.Fori(1, NB) as i:
                for s in range(2):
                    load_slab(i * 2 + (M_WO0 + s), w_o_na[0], 0, i * (2 * UC) + s * UC)
                    if s == 0:
                        load_ada(i + A_WO0, 0, i * UC + A_WO0 * UC)

            def mlp(layer, m, a):
                with sp.Fori(0, HID_GROUPS) as g:
                    for half, w in ((0, w1_mlp[layer]), (1, w2_mlp[layer])):
                        with sp.Fori(0, NB) as i:
                            for s in range(2):
                                mm = g * (4 * NB) + i * 2 + (m + 2 * NB * half + s)
                                if half == 0:
                                    load_slab(mm, w, 0, g * D + i * (2 * UC) + s * UC)
                                else:
                                    load_slab(mm, w, g * D, i * (2 * UC) + s * UC)
                                if s == 0 and a is not None:
                                    aa = g * (2 * NB) + i + NB * half
                                    load_ada(aa + a, 1, aa * UC)

            mlp(0, M_MLP0, A_MLP0)
            stream(M_QKV1, 3 * NB, w_qkvg_gla[0], 0, 1, A_QKV1, 1, A_MLP0)
            stream(M_WO1, NB, w_o_gla[0], 0, 1, A_WO1, 1, A_MLP0)
            mlp(1, M_MLP1, None)
            for q in range(8):
                s, cols = q // 4, slice(512 * (q % 4), 512 * (q % 4) + 512)
                sp.wait_ge(sem("out_staged"), q + 1)
                sp.dma_start((y_prompt, y_sample)[s][0, :, cols], OUTS[:, s, cols]).then_inc(sem("y_out"), 16)
            sp.wait_ge(sem("y_out"), 8 * 16)

        @block.tensor
        def _(pe):
            mm = nc.tensor.matmul
            pe.sem_inc(unit0_used, 2)
            pe.sem_inc(block_done, 4)
            pe.sem_inc(ada0_used, 1)
            pe.sem_inc(ada_done, 1)

            def unit(m, s, u, body, quarter=None):
                pe.wait_ge(lo_done, m * 2 + u + 3)
                slot = 2 * s + u
                hi = WHI[:, slot, :].rearrange("p (c n) -> p c n", c=UKC)
                lo = WLO[:, slot, :].rearrange("p (c n) -> p c n", c=UKC)
                for b in range(2):
                    if u == 0:
                        pe.wait_ge(bank_free, m * 2 + b + 1)
                    bank = MAIN[2 * s + b]
                    for k in range(UKC):
                        if quarter and b == 0 and k % 4 == 0:
                            quarter(2 * u + k // 4)
                        first, last = u == 0 and k == 0, u == 1 and k == UKC - 1
                        end = body(bank, hi, lo, b, UKC * u + k, k, first, last)
                    if u == 1:
                        end.then_inc(block_done, 1)
                if u == 0:
                    end.then_inc(unit0_used, 1)

            def features_out(act):
                def body(bank, hi, lo, b, kc, k, first, last):
                    cols = slice(P * b, P * b + P)
                    mm(bank[:, 0:T2], hi[:, k, cols], act[:, kc, 0:T2], start=first, stop=False)
                    mm(bank[:, 0:T2], hi[:, k, cols], act[:, kc, T2:2 * T2], start=False, stop=False)
                    return mm(bank[:, 0:T2], lo[:, k, cols], act[:, kc, 0:T2], start=False, stop=last)
                return body

            def tokens_out(act):
                def body(bank, hi, lo, b, kc, k, first, last):
                    xh = act[:, kc, TOK * b:TOK * b + TOK]
                    xl = act[:, kc, T2 + TOK * b:T2 + TOK * b + TOK]
                    mm(bank[:, 0:UC], xh, hi[:, k, :], start=first, stop=False)
                    mm(bank[:, 0:UC], xh, lo[:, k, :], start=False, stop=False)
                    return mm(bank[:, 0:UC], xl, hi[:, k, :], start=False, stop=last)
                return body

            before = [A_QKV0]

            def ada_loads(a):
                return a * 16 + (16 - before[0] * 16)

            def ada_rows(a, first=None):
                for u in range(2):
                    if first is None:
                        pe.wait_ge(ada_in[u], ada_loads(a))
                        w = ADW[:, u, :].rearrange("p (c n) -> p c n", c=UKC)
                    else:
                        arrived, i, p = first
                        pe.wait_ge(arrived, i * 32 + 32)
                        w = FIRST[p][:, u, :].rearrange("p (c n) -> p c n", c=UKC)
                    for r in range(2):
                        for j in range(4):
                            k = 4 * r + j
                            end = mm(ROWB[32 * j:32 * j + 32, 0:UC], CS[:, UKC * u + k, :], w[:, k, :],
                                     start=(u == 0 and r == 0), stop=(u == 1 and r == 1))
                    end.then_inc(ada0_used if u == 0 else ada_done, 1)

            def ada_select(a):
                pe.wait_ge(row_ready, a + 1)
                pe.wait_ge(mod_done, a + 1)
                for b in range(2):
                    end = mm(SELB[:, 2 * b:2 * b + 2], MROW[:, P * b:P * b + P], SEL, start=True, stop=True)
                end.then_inc(sel_done, 1)

            def step(m, s, body, ada=None, act_waits=None, hidden=False):
                for u in range(2):
                    if act_waits and not hidden:
                        unit(m, s, u, body, act_waits)
                    else:
                        if hidden:
                            act_waits(u)
                        unit(m, s, u, body)
                    if ada is not None:
                        (ada_rows if u == 0 else ada_select)(ada)

            def stream(m, bodies, body, ada, a=0, act_waits=None, start=0):
                with pe.Fori(start, bodies) as i:
                    for s in range(2):
                        step(i * 2 + (m + s), s, body, i * ada + (a + s) if s < ada else None, act_waits)

            def filled(f):
                return lambda q: pe.wait_ge(h_ready, 4 * f + 1 + q)

            def norm_sum(r):
                if r % 2:
                    pe.wait_ge(y_summed, (r // 2 + 1) * (Y_SLABS + 1))
                    for b in range(2):
                        end = mm(NORMB[:, 0:T2], ONES[:, :], Y_SUM[r // 2 % 2][:, T2 * b:T2 * b + T2],
                                 start=(b == 0), stop=(b == 1))
                else:
                    for g in range(4):
                        pe.wait_ge(squares, 4 * (r // 2) + g + 1)
                        for k in range(4 * g, 4 * g + 4):
                            end = mm(NORMB[:, 0:T2], ONES[:, :], SQ[:, k, :], start=(k == 0), stop=(k == KC - 1))
                end.then_inc(sumsq, 1)

            pe.wait_ge(sem("small_in"), 6 * 16)
            rows = (P, ADA_BLOCKS, ADA_BLOCKS, 2 * KC)
            off = 0
            for a, n in enumerate(rows):
                end = nc.tensor.transpose(psum[7][:, off:off + n], SMALL[0:n, a, :], IDENT[0:n, 0:n])
                off += n
            end.then_inc(sem("small_turned"), 1)
            pe.wait_ge(sem("x_in"), 2 * 16)
            for q in range(8):
                s, c0 = q // 4, 4 * (q % 4)
                if q >= 4:
                    pe.wait_ge(sem("x_copied"), q - 3)
                for j in range(4):
                    end = nc.tensor.transpose(MAIN[q % 4][:, P * j:P * j + P],
                                              XLD[:, s, P * (c0 + j):P * (c0 + j + 1)], IDENT)
                end.then_inc(sem("x_turned"), 1)
            pe.wait_ge(sem("ones_set"), 3)
            pe.wait_ge(sem("cond_ready"), 1)
            norm_sum(0)
            with pe.Fori(0, A_QKV0 // 4) as i:
                for p in range(4):
                    ada_rows(i * 4 + p, (first_in[p], i, p))
                    ada_select(i * 4 + p)

            stream(M_QKV0, 2 * NB, features_out(HM), 1, A_QKV0, filled(0))
            stream(M_QKV0 + 4 * NB, NB, tokens_out(HM), 1, A_QKV0 + 2 * NB)
            attention_tensor(pe, ada_rows, ada_select)
            before[0] += NA_H
            stream(M_WO0, NB, features_out(HM), 1, A_WO0, filled(1))
            norm_sum(1)
            norm_sum(2)

            def mlp(layer, m, a, f):
                with pe.Fori(0, HID_GROUPS) as g:
                    for half in range(2):
                        with pe.Fori(0, NB) as i:
                            for s in range(2):
                                slab = g * (4 * NB) + i * 2 + (m + 2 * NB * half + s)
                                ada = None
                                if s == 0 and a is not None:
                                    ada = g * (2 * NB) + i + (NB * half + a)
                                if half == 0:
                                    step(slab, s, features_out(HM), ada, filled(f))
                                else:
                                    step(slab, s, features_out(HID), ada,
                                         lambda u, g=g: pe.wait_ge(
                                             hid_done, g * KC + (layer * HID_GROUPS * KC + UKC * (u + 1) + 2)), True)

            mlp(0, M_MLP0, A_MLP0, 2)
            norm_sum(3)
            norm_sum(4)
            gla_low_rank_tensor(pe)
            stream(M_QKV1, 3 * NB, tokens_out(HM), 1, A_QKV1, filled(3))
            gla_tensor(pe)
            stream(M_WO1, NB, features_out(HM), 1, A_WO1, filled(4))
            norm_sum(5)
            norm_sum(6)
            mlp(1, M_MLP1, None, 5)
            norm_sum(7)
            for q in range(8):
                s, c0 = q // 4, 4 * (q % 4)
                pe.wait_ge(x_ready, 4 * 3 + (q % 4) + 1)
                if q >= 4:
                    pe.wait_ge(sem("out_staged"), q - 3)
                for j in range(4):
                    end = nc.tensor.transpose(MAIN[q % 4][:, P * j:P * j + P],
                                              X[:, c0 + j, TOK * s:TOK * s + TOK], IDENT)
                end.then_inc(sem("out_turned"), 1)

        @block.scalar
        def _(act):
            actv = nc.scalar.activation

            def split_hi(m, s):
                for u in range(2):
                    act.wait_ge(raw_in[u], m * 16 + 16)
                    if u == 0:
                        act.wait_ge(unit0_used, m + 1)
                    else:
                        act.wait_ge(block_done, m * 2 + 2)
                    actv(WHI[:, 2 * s + u, :], RAW[:, u, :], ACT.Copy).then_inc(hi_done, 1)

            def ada_row(a):
                act.wait_ge(ada_done, a + 2)
                actv(MROW[:, :], ROWB[:, 0:UC], ACT.Copy).then_inc(row_ready, 1)

            def square_hidden(k):
                for b in range(2):
                    act.wait_ge(relu_done, k + b + 1)
                    actv(RELU[:, b, :], RELU[:, b, :], ACT.Square).then_inc(square_done, 1)

            def step(m, s, ada=None, hidden=None, prefetch=True):
                if prefetch:
                    split_hi(m + 1, 1 - s)
                if ada is not None:
                    ada_row(ada)
                if hidden is not None:
                    square_hidden(hidden)

            def stream(m, bodies, ada, a=0):
                with act.Fori(0, bodies) as i:
                    for s in range(2):
                        step(i * 2 + (m + s), s, i * ada + (a + s) if s < ada else None)

            def norm_squares(r):
                for g in range(4):
                    if r:
                        act.wait_ge(x_ready, 4 * (r // 2 - 1) + g + 1)
                    actv(SQ[:, 4 * g:4 * g + 4, :], X[:, 4 * g:4 * g + 4, :], ACT.Square).then_inc(squares, 1)
                norm_std(r)

            def norm_std(r):
                act.wait_ge(sumsq, r + 1)
                actv(STD, NORMB[:, 0:T2], ACT.Sqrt, bias=EPSC[:, :], scale=1.0 / D).then_inc(std_ready, 1)

            def modulate(f, layer, j):
                shift = ADA_BLOCKS * layer + KC * j
                for g in range(4):
                    act.wait_ge(xn_ready, 4 * f + g + 1)
                    for k in range(4 * g, 4 * g + 4):
                        end = actv(SQ[:, k, 0:TOK], SQ[:, k, 0:TOK], ACT.Identity,
                                   bias=MODT[:, shift + k, 0:1], scale=GAIN[:, k, 0:1])
                    end.then_inc(mod_x, 1)
                    act.wait_ge(mod_x, 4 * f + g + 1)
                    act.wait_ge(mod_xs, 4 * f + g + 1)
                    actv(HM[:, 4 * g:4 * g + 4, 0:T2], SQ[:, 4 * g:4 * g + 4, :], ACT.Copy).then_inc(hm_hi, 1)

            act.wait_ge(sem("ones_set"), 3)
            act.wait_ge(sem("small_turned"), 1)
            actv(NGT[:, :], psum[7][:, 0:P], ACT.Copy).then_inc(sem("gains_ready"), 1)
            actv(BT[:, :], psum[7][:, P:P + 2 * ADA_BLOCKS], ACT.Copy).then_inc(sem("biases_ready"), 1)
            actv(CC, psum[7][:, P + 2 * ADA_BLOCKS:P + 2 * ADA_BLOCKS + 2 * KC], ACT.Copy).then_inc(
                sem("cond_copied"), 1)
            act.wait_ge(sem("cond_copied"), 1)
            actv(CE, CC, ACT.Exp, scale=-1.0).then_inc(sem("cond_exp"), 1)
            for q in range(8):
                s, c0 = q // 4, 4 * (q % 4)
                act.wait_ge(sem("x_turned"), q + 1)
                actv(X[:, c0:c0 + 4, TOK * s:TOK * s + TOK],
                     MAIN[q % 4][:, :].rearrange("p (c t) -> p c t", c=4), ACT.Copy).then_inc(sem("x_copied"), 1)
            act.wait_ge(sem("x_copied"), 8)
            norm_squares(0)
            split_hi(0, 0)
            with act.Fori(0, A_QKV0) as i:
                ada_row(i)

            modulate(0, 0, 0)
            stream(M_QKV0, 3 * NB, 1, A_QKV0)
            attention_scalar(act, ada_row)
            stream(M_WO0, NB, 1, A_WO0)
            act.wait_ge(bank_free, 4 + 2 * M_MLP0)
            norm_std(1)
            norm_squares(2)
            modulate(1, 0, 3)

            def mlp(layer, m, a, last):
                with act.Fori(0, HID_GROUPS - (1 if last else 0)) as g:
                    mlp_group(g, layer, m, a)
                if last:
                    mlp_group(HID_GROUPS - 1, layer, m, a, last)

            def mlp_group(g, layer, m, a, last=False):
                for half in range(2):
                    peel = last and half == 1
                    with act.Fori(0, NB - (1 if peel else 0)) as i:
                        mlp_body(g, i, half, layer, m, a)
                    if peel:
                        mlp_body(g, NB - 1, half, layer, m, a, True)

            def mlp_body(g, i, half, layer, m, a, end=False):
                for s in range(2):
                    slab = g * (4 * NB) + i * 2 + (m + 2 * NB * half + s)
                    ada = None
                    if s == 0 and a is not None:
                        ada = g * (2 * NB) + i + (NB * half + a)
                    hidden = None
                    if half == 0:
                        hidden = g * KC + i * 4 + (layer * HID_GROUPS * KC + 2 * s)
                    step(slab, s, ada, hidden, prefetch=not (end and s == 1))

            mlp(0, M_MLP0, A_MLP0, False)
            act.wait_ge(bank_free, 4 + 2 * M_QKV1)
            norm_std(3)
            norm_squares(4)
            modulate(2, 1, 0)
            stream(M_QKV1, 3 * NB, 1, A_QKV1)
            gla_scalar(act)
            stream(M_WO1, NB, 1, A_WO1)
            act.wait_ge(bank_free, 4 + 2 * M_MLP1)
            norm_std(5)
            norm_squares(6)
            modulate(3, 1, 3)
            mlp(1, M_MLP1, None, True)
            act.wait_ge(bank_free, 4 + 2 * M_END)
            norm_std(7)
            for q in range(8):
                act.wait_ge(sem("out_turned"), q + 1)
                actv(OUTS[:, q // 4, 512 * (q % 4):512 * (q % 4) + 512], MAIN[q % 4][:, :], ACT.Copy).then_inc(
                    sem("out_staged"), 1)

        @block.vector
        def _(dve):
            tt = nc.vector.tensor_tensor
            ts = nc.vector.tensor_scalar
            own = sem("dve_own")
            count = [0]

            def link(ins):
                count[0] += 1
                ins.then_inc(own, 1)
                dve.wait_ge(own, count[0])

            dve.sem_inc(lo_done, 2)
            dve.sem_inc(bank_free, 4)
            dve.sem_inc(mod_done, 1)
            dve.sem_inc(hid_done, 2)

            def split_lo(m, s):
                for u in range(2):
                    dve.wait_ge(hi_done, m * 2 + u + 1)
                    tt(WLO[:, 2 * s + u, :], RAW[:, u, :], WHI[:, 2 * s + u, :].bitcast(f32),
                       ALU.subtract).then_inc(lo_done, 1)

            def ada_mod(a):
                dve.wait_ge(sel_done, a + 1)
                tt(MODT[:, ds(a * 2, 2), :], SELB[:, 0:4].rearrange("p (b s) -> p b s", b=2),
                   BT[:, ds(a * 2, 2)].unsqueeze(2).broadcast_to([P, 2, 2]),
                   ALU.add).then_inc(mod_done, 1)

            def evacuate(m, s, how):
                for b in range(2):
                    dve.wait_ge(block_done, m * 2 + b + 5)
                    how(MAIN[2 * s + b][:, 0:T2], b).then_inc(bank_free, 1)

            def step(m, s, how, ada=None, after=None, prefetch=True):
                if prefetch:
                    split_lo(m + 1, 1 - s)
                evacuate(m, s, how)
                if ada is not None:
                    ada_mod(ada)
                if after:
                    after()

            def stream(m, bodies, how, ada, a=0):
                with dve.Fori(0, bodies) as i:
                    for s in range(2):
                        step(i * 2 + (m + s), s, how(i, s), i * ada + (a + s) if s < ada else None)

            def to_blocks(dst, first):
                return lambda i, s: lambda src, b: ts(
                    dst[:, ds(i * 4 + (first + 2 * s + b), 1), :].rearrange("p o t -> p (o t)"), src, 1.0, None,
                    ALU.mult)

            def to_tokens(dst, col):
                return lambda i, s: lambda src, b: ts(
                    dst[:, b, ds(i * (2 * UC) + (col + s * UC), UC)], src, 1.0, None, ALU.mult)

            def add_to_y(i, s):
                def how(src, b):
                    y = Y[:, ds(i * 4 + (2 * s + b), 1), :].rearrange("p o t -> p (o t)")
                    return tt(y, src, y, ALU.add)
                return how

            def finish_y(slab, i, s, r):
                total, sq = Y_SUM[r // 2 % 2], Y_SQ[r // 2 % 2]
                y = Y[:, ds(i * 4 + 2 * s, 2), :]
                before = r // 2 * (Y_SLABS + 1) + s + 1
                dve.wait_ge(bank_free, slab * 2 + 6)
                dve.wait_ge(y_summed, i * 2 + before)
                tt(sq.rearrange("p (k t) -> p k t", k=2), y, y, ALU.mult).then_inc(y_squared, 1)
                dve.wait_ge(y_squared, i * 2 + (r // 2 * Y_SLABS + s + 1))
                tt(total, total, sq, ALU.add).then_inc(y_summed, 1)
                y = y.rearrange("p k (s t) -> p (k s) t", s=2)
                tt(y, y, GAIN[:, ds(i * 4 + 2 * s, 2), :].rearrange("p k s -> p (k s)").unsqueeze(2)
                   .broadcast_to([P, 4, TOK]), ALU.mult).then_inc(y_gained, 1)

            def begin_y(r, layer, norm, mod):
                gain(layer, norm, mod, 0.0)
                nc.vector.memset(Y_SUM[r // 2 % 2], 0.0).then_inc(y_summed, 1)

            def output_stream(m, ada, r):
                with dve.Fori(0, NB) as i:
                    for s in range(2):
                        step(i * 2 + (m + s), s, add_to_y(i, s), i + ada if s == 0 else None,
                             lambda: finish_y(i * 2 + (m + s), i, s, r))

            def norm_rstd(r):
                dve.wait_ge(std_ready, r + 1)
                link(nc.vector.reciprocal(RSTD, STD))

            def gain(layer, norm, mod, plus):
                first = ADA_BLOCKS * layer + KC * mod
                ng = NGT[:, (4 * layer + norm) * KC:(4 * layer + norm + 1) * KC]
                link(ts(GAIN[:, :, :], MODT[:, first:first + KC, :], plus, None, ALU.add))
                link(tt(GAIN[:, :, :], GAIN[:, :, :],
                        ng.unsqueeze(2).broadcast_to([P, KC, 2]), ALU.mult))

            def residual(r):
                norm_rstd(r)
                dve.wait_ge(y_gained, (r // 2 + 1) * Y_SLABS)
                for g in range(4):
                    q = slice(4 * g, 4 * g + 4)
                    link(tt(SQ[:, q, :], Y[:, q, :], RSTD.unsqueeze(1).broadcast_to([P, 4, T2]), ALU.mult))
                    tt(X[:, q, :], X[:, q, :], SQ[:, q, :], ALU.add).then_inc(x_ready, 1)

            def pre_norm(r, f, layer, norm, mod, residual_no=None):
                if residual_no is not None:
                    dve.wait_ge(x_ready, 4 * residual_no + 4)
                gain(layer, norm, mod, 1.0)
                norm_rstd(r)
                shift = ADA_BLOCKS * layer + KC * (mod - 1)
                for g in range(4):
                    q = slice(4 * g, 4 * g + 4)
                    tt(SQ[:, q, :], X[:, q, :], RSTD.unsqueeze(1).broadcast_to([P, 4, T2]), ALU.mult).then_inc(
                        xn_ready, 1)
                    dve.wait_ge(xn_ready, 4 * f + g + 1)
                    modulate_sample(g, shift)
                    if g:
                        modulated_lo(f, g - 1)
                modulated_lo(f, 3)

            def modulate_sample(g, shift):
                for k in range(4 * g, 4 * g + 4):
                    end = ts(SQ[:, k, TOK:T2], SQ[:, k, TOK:T2], GAIN[:, k, 1:2], MODT[:, shift + k, 1:2],
                             ALU.mult, ALU.add)
                end.then_inc(mod_xs, 1)

            def modulated_lo(f, g):
                q = slice(4 * g, 4 * g + 4)
                dve.wait_ge(hm_hi, 4 * f + g + 1)
                tt(HM[:, q, T2:2 * T2], SQ[:, q, :], HM[:, q, 0:T2].bitcast(f32), ALU.subtract).then_inc(h_ready, 1)

            dve.wait_ge(sem("cond_exp"), 1)
            link(nc.vector.memset(CS[:, :, :], 0.0))
            link(ts(CE, CE, 1.0, None, ALU.add))
            link(nc.vector.reciprocal(CE, CE))
            tt(CS[:, :, 0:2], CC.rearrange("p (s c) -> p c s", s=2), CE.rearrange("p (s c) -> p c s", s=2),
               ALU.mult).then_inc(sem("cond_ready"), 1)
            norm_rstd(0)
            link(tt(SQ, X[:, :, :], RSTD.unsqueeze(1).broadcast_to([P, KC, T2]), ALU.mult))
            dve.wait_ge(sem("biases_ready"), 1)
            split_lo(0, 0)
            with dve.Fori(0, A_QKV0) as i:
                ada_mod(i)
            dve.wait_ge(mod_done, A_QKV0 + 1)

            gain(0, 0, 1, 1.0)
            dve.sem_inc(xn_ready, 4)
            for g in range(4):
                modulate_sample(g, 0)
                if g:
                    modulated_lo(0, g - 1)
            modulated_lo(0, 3)
            stream(M_QKV0, 2 * NB, to_blocks(QK, 0), 1, A_QKV0)
            stream(M_QKV0 + 4 * NB, NB, to_tokens(VN, 0), 1, A_QKV0 + 2 * NB)
            attention_vector(dve, link, ada_mod)
            dve.wait_ge(y_zero, 1)
            dve.wait_ge(mod_done, A_WO0 + 1)
            begin_y(1, 0, 1, 2)
            output_stream(M_WO0, A_WO0, 1)
            dve.wait_ge(bank_free, 4 + 2 * M_MLP0)
            dve.wait_ge(mod_done, A_MLP0 + 1)
            residual(1)
            pre_norm(2, 1 + 0, 0, 2, 4, 0)

            def mlp(layer, m, a, last):
                with dve.Fori(0, HID_GROUPS - 1) as g:
                    mlp_group(g, layer, m, a)
                mlp_group(HID_GROUPS - 1, layer, m, a, True, last)

            def mlp_group(g, layer, m, a, complete=False, last=False):
                for half in range(2):
                    peel = last and half == 1
                    r = 4 * layer + 3 if complete and half == 1 else None
                    if r:
                        begin_y(r, layer, 3, 5)
                    with dve.Fori(0, NB - (1 if peel else 0)) as i:
                        mlp_body(g, i, half, layer, m, a, r)
                    if peel:
                        mlp_body(g, NB - 1, half, layer, m, a, r, True)

            def mlp_body(g, i, half, layer, m, a, r, end=False):
                for s in range(2):
                    slab = g * (4 * NB) + i * 2 + (m + 2 * NB * half + s)
                    ada = None
                    if s == 0 and a is not None:
                        ada = g * (2 * NB) + i + (NB * half + a)
                    if half == 1:
                        step(slab, s, add_to_y(i, s), ada, (lambda: finish_y(slab, i, s, r)) if r else None,
                             prefetch=not (end and s == 1))
                        continue
                    k = g * KC + i * 4 + (layer * HID_GROUPS * KC + 2 * s)
                    hid = [HID[:, ds(i * 4 + (2 * s + b), 1), :].rearrange("p o t -> p (o t)") for b in range(2)]
                    split_lo(slab + 1, 1 - s)
                    for b in range(2):
                        dve.wait_ge(hid_done, k + b + 1)
                        dve.wait_ge(block_done, slab * 2 + b + 5)
                        ts(RELU[:, b, :], MAIN[2 * s + b][:, 0:T2], 0.0, None, ALU.max).then_inc(relu_done, 1)
                    if ada is not None:
                        ada_mod(ada)
                    for b in range(2):
                        dve.wait_ge(square_done, k + b + 1)
                        ts(hid[b][:, 0:T2], RELU[:, b, :], 1.0, None, ALU.mult).then_inc(bank_free, 1)
                    for b in range(2):
                        dve.wait_ge(bank_free, slab * 2 + b + 5)
                        tt(hid[b][:, T2:2 * T2], RELU[:, b, :], hid[b][:, 0:T2].bitcast(f32),
                           ALU.subtract).then_inc(hid_done, 1)

            dve.wait_ge(y_zero, 2)
            mlp(0, M_MLP0, A_MLP0, False)
            dve.wait_ge(bank_free, 4 + 2 * M_QKV1)
            dve.wait_ge(mod_done, A_QKV1 + 1)
            residual(3)
            pre_norm(4, 2, 1, 0, 1, 1)
            gla_low_rank_vector(dve)
            m, a = M_QKV1, A_QKV1
            for dst, n in ((QG, KEY), (KG, KEY), (VG, D), (GG, D)):
                bodies = n // (2 * UC)
                if dst is GG:
                    dve.wait_ge(sem("rotated"), 1)
                stream(m, bodies, to_tokens(dst, 0), 1, a)
                m, a = m + 2 * bodies, a + bodies
            gla_vector(dve, link)
            dve.wait_ge(y_zero, 3)
            dve.wait_ge(mod_done, A_WO1 + 1)
            begin_y(5, 1, 1, 2)
            output_stream(M_WO1, A_WO1, 5)
            dve.wait_ge(bank_free, 4 + 2 * M_MLP1)
            dve.wait_ge(mod_done, A_END + 1)
            residual(5)
            pre_norm(6, 3, 1, 2, 4, 2)
            dve.wait_ge(y_zero, 4)
            mlp(1, M_MLP1, None, True)
            dve.wait_ge(bank_free, 4 + 2 * M_END)
            residual(7)

        @block.gpsimd
        def _(pool):
            nc.gpsimd.memset(ONES[:, :], 1.0).then_inc(sem("ones_set"), 1)
            nc.gpsimd.memset(EPSC[:, :], EPS).then_inc(sem("ones_set"), 1)
            nc.gpsimd.memset(ONEC[:, :], 1.0).then_inc(sem("ones_set"), 1)
            pool.wait_ge(block_done, 4 + 1)
            nc.gpsimd.memset(RPT[0:N_DR * NA_H, :], 0.0).then_inc(sem("pad_zero"), 1)
            pool.wait_ge(sem("pad_zero"), 1)
            pool.dma_start(WINM[:, :], t_window).then_inc(sem("window_in"), 16)
            mid = GRID_W - 1
            for r in range(N_DR):
                pool.dma_start(RPT[NA_H * r:NA_H * r + NA_H, mid - WIN_COLS + 1:mid + WIN_COLS],
                               rpb_na[0, :, 6 + r, :]).then_inc(sem("rpb_in"), 16)
            pool.wait_ge(sem("rpb_in"), 16 * N_DR)
            pool.dma_start(rpb_pad.rearrange("r h q w -> (r h) q w"),
                           RPT[0:N_DR * NA_H, 0:LINE].unsqueeze(1).broadcast_to([N_DR * NA_H, GRID_W, LINE])).then_inc(
                sem("rpb_padded"), 16)
            pool.wait_ge(sem("rpb_padded"), 16)
            for qr in range(2):
                for kr in range(2):
                    src = bass.AP(rpb_pad.tensor, (1 - qr + kr) * NA_H * GRID_W * LINE + mid,
                                  [[LINE - 1, GRID_W], [GRID_W * LINE, NA_H], [1, GRID_W]])
                    pool.dma_start(BIAS[GRID_W * qr:GRID_W * qr + GRID_W, :, GRID_W * kr:GRID_W * kr + GRID_W],
                                   src).then_inc(sem("bias_in"), 16)
            pool.wait_ge(sem("bias_in"), 64)
            pool.wait_ge(sem("window_in"), 16)
            nc.gpsimd.tensor_tensor(BIAS, BIAS, WINM[:, :].unsqueeze(1).broadcast_to([P, NA_H, P]), ALU.add).then_inc(
                sem("bias_ready"), 1)
            attention_pool(pool)
            pool.wait_ge(x_ready, 4)
            nc.gpsimd.memset(SCR[:, 2 * S4:3 * S4], 0.0).then_inc(y_zero, 1)
            gla_pool(pool)
            pool.wait_ge(x_ready, 12)
            nc.gpsimd.memset(SCR[:, 2 * S4:3 * S4], 0.0).then_inc(y_zero, 1)
            pool.wait_ge(sem("newk_out"), 16)
            pool.wait_ge(sem("newv_out"), 16)
            pool.wait_ge(sem("gla_final_out"), 32 * GLA_H)


_INS = ['x_prompt', 'x_sample', 'cache_na_k', 'cache_na_v', 'state_gla', 'c', 'c_ctx', 'w_ada', 'b_ada', 'norm_g',
        'w_qkv_na', 'w_o_na', 'rpb_na', 'w_qkvg_gla', 'w_a1_gla', 'w_a2_gla', 'b_a_gla', 'g_head_gla', 'w_o_gla',
        'w1_mlp', 'w2_mlp']
_OUTS = [(1, TOK, D), (1, TOK, D), (1, 1, NA_H, TOK, DH), (1, 1, NA_H, TOK, DH), (1, 1, 2, GLA_H, DK, DV)]


def kernel(**inputs):
    import numpy as _np
    import concourse.bacc as _bacc
    from concourse import mybir as _mybir
    from concourse.bass_utils import run_bass_kernel_spmd as _run

    nc = _bacc.Bacc("TRN2", target_bir_lowering=False, num_devices=1)
    arrays, args = {}, []
    named = [(n, _np.ascontiguousarray(inputs[n])) for n in _INS]
    named += list(zip(("t_base", "t_window", "t_gla"), shape_tables()))
    for name, a in named:
        arrays[f"in_{name}"] = a
        args.append(nc.dram_tensor(f"in_{name}", a.shape, _mybir.dt.from_np(a.dtype), kind="ExternalInput").ap())
    for i, shape in enumerate(_OUTS):
        args.append(nc.dram_tensor(f"out_{i}", shape, _mybir.dt.float32, kind="ExternalOutput").ap())
    build_program(nc, *args)
    r = _run(nc, [arrays], core_ids=[0])
    return tuple(r.results[0][f"out_{i}"] for i in range(len(_OUTS)))
```
